# Optimizing a Trainium2 kernel written in Bass

```python
import math
import jax
import jax.numpy as jnp
from jax import lax
import numpy as np
import jax, jax.numpy as jnp

D_MODEL = 1024
BATCH = 1
SEQ = 256
DEPTH = 2

N_MIXERS = 2
HEAD_DIM = 64
N_HEADS = D_MODEL // HEAD_DIM
ATTN_WIDTH = N_HEADS * HEAD_DIM
ROPE_THETA = 10000.0
NORM_EPS = 1e-6

NSA_KV_HEADS = 2
NSA_GROUP = N_HEADS // NSA_KV_HEADS
NSA_KV_WIDTH = NSA_KV_HEADS * HEAD_DIM
NSA_BRANCHES = 3
CMP_LEN = 32
CMP_STRIDE = 16
CMP_HIDDEN = 256
SLC_LEN = 64
SLC_TOP = 16
WIN_LEN = 512
NSA_IN = ATTN_WIDTH + 6 * NSA_KV_WIDTH + ATTN_WIDTH + NSA_BRANCHES * N_HEADS
SLC_Q_BLOCK = 32
WIN_Q_BLOCK = 128

DIL_PATTERNS = ((128, 1), (512, 4), (2048, 16))
DIL_GROUP_HEADS = (N_HEADS - 2 * (N_HEADS // 3), N_HEADS // 3, N_HEADS // 3)
DIL_IN = 4 * ATTN_WIDTH
DIL_Q_BLOCK = 32


def rms_norm(x, g):
    xf = x.astype(jnp.float32)
    y = xf * lax.rsqrt(jnp.mean(xf * xf, axis=-1, keepdims=True) + NORM_EPS)
    return (y * g.astype(jnp.float32)).astype(x.dtype)

def rope(x):
    T = x.shape[1]
    half = x.shape[-1] // 2
    inv = ROPE_THETA ** (-jnp.arange(half, dtype=jnp.float32) / half)
    ang = jnp.arange(T, dtype=jnp.float32)[:, None] * inv[None, :]
    cos = jnp.cos(ang)[None, :, None, :]
    sin = jnp.sin(ang)[None, :, None, :]
    xf = x.astype(jnp.float32)
    x1, x2 = xf[..., :half], xf[..., half:]
    return jnp.concatenate([x1 * cos - x2 * sin, x2 * cos + x1 * sin], axis=-1).astype(x.dtype)

def masked_softmax(s, mask):
    s = jnp.where(mask, s.astype(jnp.float32), -jnp.inf)
    m = jnp.max(s, axis=-1, keepdims=True)
    m = jnp.where(jnp.isfinite(m), m, 0.0)
    e = jnp.exp(s - m)
    den = jnp.sum(e, axis=-1, keepdims=True)
    return e / jnp.where(den > 0, den, 1.0)

def adaln_norm(x, c, g, w_ada, b_ada):
    mod = jax.nn.silu(c) @ w_ada + b_ada
    shift, scale, gate = jnp.split(mod, 3, axis=-1)
    h = rms_norm(x, g) * (1.0 + scale[:, None, :]) + shift[:, None, :]
    return h, gate[:, None, :]

def nsa_mixer(h, w_in, pe_k, pe_v, ck_w1, ck_w2, cv_w1, cv_w2, w_out):
    B, T, _ = h.shape
    G, HG, DH = NSA_KV_HEADS, NSA_GROUP, HEAD_DIM
    scale = DH ** -0.5
    u = h @ w_in
    cuts = np.cumsum([ATTN_WIDTH] + [NSA_KV_WIDTH] * 6 + [ATTN_WIDTH]).tolist()
    q, k_c, v_c, k_s, v_s, k_w, v_w, z, g_logit = jnp.split(u, cuts, axis=-1)
    k_c, v_c, k_s, v_s, k_w, v_w = [a.reshape(B, T, G, DH) for a in (k_c, v_c, k_s, v_s, k_w, v_w)]
    gates = jax.nn.sigmoid(g_logit.astype(jnp.float32)).reshape(B, T, G, HG, NSA_BRANCHES).astype(h.dtype)
    t = jnp.arange(T)

    q_plain = q.reshape(B, T, G, HG, DH)
    n_cmp = (T - CMP_LEN) // CMP_STRIDE + 1
    cmp_idx = CMP_STRIDE * np.arange(n_cmp)[:, None] + np.arange(CMP_LEN)[None, :]

    def compress(a, pe, w1, w2):
        blk = a[:, cmp_idx] + pe[:, None, :]
        blk = jnp.moveaxis(blk, 3, 2).reshape(B, n_cmp, G, CMP_LEN * DH)
        return jax.nn.silu(blk @ w1) @ w2

    k_cmp = compress(k_c, pe_k, ck_w1, ck_w2)
    v_cmp = compress(v_c, pe_v, cv_w1, cv_w2)
    cmp_end = CMP_STRIDE * jnp.arange(n_cmp) + CMP_LEN - 1
    cmask = cmp_end[None, :] <= t[:, None]
    s_cmp = jnp.einsum('btghd,bngd->btghn', q_plain, k_cmp) * scale
    p_cmp = masked_softmax(s_cmp, cmask[None, :, None, None, :])
    o_cmp = jnp.einsum('btghn,bngd->btghd', p_cmp.astype(v_cmp.dtype), v_cmp)

    n_slc = T // SLC_LEN
    c_start = CMP_STRIDE * np.arange(n_cmp)
    s_start = SLC_LEN * np.arange(n_slc)
    overlap = ((c_start[:, None] < s_start[None, :] + SLC_LEN)
               & (c_start[:, None] + CMP_LEN > s_start[None, :])).astype(np.float32)
    p_slc = jnp.einsum('btghn,nj->btgj', p_cmp, overlap)
    jblk = jnp.arange(n_slc)[None, :]
    cur = (t // SLC_LEN)[:, None]
    visible = jblk <= cur
    forced = (jblk == 0) | (jblk == cur) | (jblk == cur - 1)
    rank = jnp.where(forced[None, :, None, :], jnp.inf,
                     jnp.where(visible[None, :, None, :], p_slc, -jnp.inf))
    n_top = min(SLC_TOP, n_slc)
    top_val, top_idx = lax.top_k(rank, n_top)
    top_ok = top_val > -jnp.inf

    q_r = rope(q.reshape(B, T, N_HEADS, DH)).reshape(B, T, G, HG, DH)
    k_s = rope(k_s)
    k_w = rope(k_w)

    k_blk = k_s.reshape(B, n_slc, SLC_LEN, G, DH).transpose(0, 3, 1, 2, 4)
    v_blk = v_s.reshape(B, n_slc, SLC_LEN, G, DH).transpose(0, 3, 1, 2, 4)
    C = SLC_Q_BLOCK
    n_qb = T // C
    q_sb = jnp.moveaxis(q_r.reshape(B, n_qb, C, G, HG, DH), 1, 0)
    idx_sb = jnp.moveaxis(top_idx.reshape(B, n_qb, C, G, n_top), 1, 0)
    ok_sb = jnp.moveaxis(top_ok.reshape(B, n_qb, C, G, n_top), 1, 0)
    gather_blocks = jax.vmap(jax.vmap(lambda blk, ix: blk[ix]))

    def slc_block(args):
        s0, qq, ii, ok = args
        ii_g = jnp.swapaxes(ii, 1, 2)
        kg = gather_blocks(k_blk, ii_g)
        vg = gather_blocks(v_blk, ii_g)
        s = jnp.einsum('bcghd,bgcnld->bcghnl', qq, kg) * scale
        tq = s0 + jnp.arange(C)
        kpos = ii[..., None] * SLC_LEN + jnp.arange(SLC_LEN)
        mask = (kpos <= tq[None, :, None, None, None]) & ok[..., None]
        p = masked_softmax(s.reshape(B, C, G, HG, n_top * SLC_LEN),
                           mask.reshape(B, C, G, 1, n_top * SLC_LEN))
        return jnp.einsum('bcghnl,bgcnld->bcghd', p.reshape(s.shape).astype(vg.dtype), vg)

    o_slc = lax.map(slc_block, (jnp.arange(n_qb) * C, q_sb, idx_sb, ok_sb))
    o_slc = jnp.moveaxis(o_slc, 0, 1).reshape(B, T, G, HG, DH)

    span = WIN_LEN + WIN_Q_BLOCK
    n_wb = T // WIN_Q_BLOCK
    k_pad = jnp.pad(k_w, ((0, 0), (WIN_LEN, 0), (0, 0), (0, 0)))
    v_pad = jnp.pad(v_w, ((0, 0), (WIN_LEN, 0), (0, 0), (0, 0)))
    q_wb = jnp.moveaxis(q_r.reshape(B, n_wb, WIN_Q_BLOCK, G, HG, DH), 1, 0)

    def win_block(args):
        s0, qq = args
        kk = lax.dynamic_slice_in_dim(k_pad, s0, span, axis=1)
        vv = lax.dynamic_slice_in_dim(v_pad, s0, span, axis=1)
        s = jnp.einsum('bcghd,bkgd->bcghk', qq, kk) * scale
        tq = s0 + jnp.arange(WIN_Q_BLOCK)
        kpos = s0 - WIN_LEN + jnp.arange(span)
        mask = ((kpos[None, :] <= tq[:, None]) & (kpos[None, :] > tq[:, None] - WIN_LEN)
                & (kpos[None, :] >= 0))
        p = masked_softmax(s, mask[None, :, None, None, :])
        return jnp.einsum('bcghk,bkgd->bcghd', p.astype(vv.dtype), vv)

    o_win = lax.map(win_block, (jnp.arange(n_wb) * WIN_Q_BLOCK, q_wb))
    o_win = jnp.moveaxis(o_win, 0, 1).reshape(B, T, G, HG, DH)

    o = gates[..., 0:1] * o_cmp + gates[..., 1:2] * o_slc + gates[..., 2:3] * o_win
    o = o.reshape(B, T, ATTN_WIDTH)
    return (o * jax.nn.silu(z)) @ w_out

def dilated_mixer(h, w_in, w_out):
    B, T, _ = h.shape
    DH = HEAD_DIM
    scale = DH ** -0.5
    n_grp = len(DIL_PATTERNS)
    q, k, v, z = jnp.split(h @ w_in, 4, axis=-1)
    q = rope(q.reshape(B, T, N_HEADS, DH))
    k = rope(k.reshape(B, T, N_HEADS, DH))
    v = v.reshape(B, T, N_HEADS, DH)
    offs = np.cumsum((0,) + DIL_GROUP_HEADS).tolist()
    k_grp = [k[:, :, offs[i]:offs[i + 1]] for i in range(n_grp)]
    v_grp = [v[:, :, offs[i]:offs[i + 1]] for i in range(n_grp)]
    C = DIL_Q_BLOCK
    n_qb = T // C
    q_blocks = jnp.moveaxis(q.reshape(B, n_qb, C, N_HEADS, DH), 1, 0)

    def block(args):
        s0, qb = args
        tq = s0 + jnp.arange(C)
        outs, lses = [], []
        for gi, (win, dil) in enumerate(DIL_PATTERNS):
            n_k = win // dil + 1
            kpos = tq[:, None] - dil * jnp.arange(n_k)[None, :]
            ok = kpos >= 0
            kidx = jnp.maximum(kpos, 0)
            kg = k_grp[gi][:, kidx]
            vg = v_grp[gi][:, kidx]
            qg = qb[:, :, offs[gi]:offs[gi + 1]]
            s = jnp.einsum('bchd,bckhd->bchk', qg, kg).astype(jnp.float32) * scale
            s = jnp.where(ok[None, :, None, :], s, -jnp.inf)
            m = jnp.max(s, axis=-1, keepdims=True)
            e = jnp.exp(s - m)
            den = jnp.sum(e, axis=-1, keepdims=True)
            outs.append(jnp.einsum('bchk,bckhd->bchd', (e / den).astype(vg.dtype), vg))
            lse = (m + jnp.log(den))[..., 0]
            lses.append(jax.nn.logsumexp(lse, axis=-1) - math.log(DIL_GROUP_HEADS[gi]))
        alpha = jax.nn.softmax(jnp.stack(lses, axis=-1), axis=-1) * n_grp
        return jnp.concatenate(
            [outs[i] * alpha[:, :, i, None, None].astype(outs[i].dtype) for i in range(n_grp)], axis=2)

    o = lax.map(block, (jnp.arange(n_qb) * C, q_blocks))
    o = jnp.moveaxis(o, 0, 1).reshape(B, T, ATTN_WIDTH)
    return (o * jax.nn.silu(z)) @ w_out

def first_inputs(seed: int = 0) -> dict:
    key = jax.random.key(seed)
    ks = jax.random.split(key, 16)
    n_a = len(range(0, DEPTH, N_MIXERS))
    n_b = len(range(1, DEPTH, N_MIXERS))
    D = D_MODEL

    def nrm(k, shape, s):
        return jax.random.normal(k, shape, jnp.float32) * s

    return {
        "x": nrm(ks[0], (BATCH, SEQ, D), 1.0),
        "c": nrm(ks[1], (BATCH, D), 1.0),
        "norm_g": 1.0 + nrm(ks[2], (DEPTH, D), 0.05),
        "ada_w": nrm(ks[3], (DEPTH, D, 3 * D), 0.5 * D ** -0.5),
        "ada_b": nrm(ks[4], (DEPTH, 3 * D), 0.02),
        "nsa_w_in": nrm(ks[5], (n_a, D, NSA_IN), D ** -0.5),
        "nsa_pe_k": nrm(ks[6], (n_a, CMP_LEN, HEAD_DIM), 0.1),
        "nsa_pe_v": nrm(ks[7], (n_a, CMP_LEN, HEAD_DIM), 0.1),
        "nsa_ck_w1": nrm(ks[8], (n_a, CMP_LEN * HEAD_DIM, CMP_HIDDEN), (CMP_LEN * HEAD_DIM) ** -0.5),
        "nsa_ck_w2": nrm(ks[9], (n_a, CMP_HIDDEN, HEAD_DIM), CMP_HIDDEN ** -0.5),
        "nsa_cv_w1": nrm(ks[10], (n_a, CMP_LEN * HEAD_DIM, CMP_HIDDEN), (CMP_LEN * HEAD_DIM) ** -0.5),
        "nsa_cv_w2": nrm(ks[11], (n_a, CMP_HIDDEN, HEAD_DIM), CMP_HIDDEN ** -0.5),
        "nsa_w_out": nrm(ks[12], (n_a, ATTN_WIDTH, D), ATTN_WIDTH ** -0.5),
        "dil_w_in": nrm(ks[13], (n_b, D, DIL_IN), D ** -0.5),
        "dil_w_out": nrm(ks[14], (n_b, ATTN_WIDTH, D), ATTN_WIDTH ** -0.5),
        "final_g": 1.0 + nrm(ks[15], (D,), 0.05),
    }

def first_block(x, c, norm_g, ada_w, ada_b, nsa_w_in, nsa_pe_k, nsa_pe_v, nsa_ck_w1, nsa_ck_w2,
              nsa_cv_w1, nsa_cv_w2, nsa_w_out, dil_w_in, dil_w_out, final_g):
    for i in range(DEPTH):
        h, gate = adaln_norm(x, c, norm_g[i], ada_w[i], ada_b[i])
        j = i // N_MIXERS
        if i % N_MIXERS == 0:
            y = nsa_mixer(h, nsa_w_in[j], nsa_pe_k[j], nsa_pe_v[j], nsa_ck_w1[j], nsa_ck_w2[j],
                          nsa_cv_w1[j], nsa_cv_w2[j], nsa_w_out[j])
        else:
            y = dilated_mixer(h, dil_w_in[j], dil_w_out[j])
        x = x + gate * y
    return rms_norm(x, final_g)


DEPTH_2 = 1

CONV_A_WIDTH = 512
CONV_A_K = 3
DN_HEADS = 8
DN_DK = 128
DN_DV = 128
DN_CONV_K = 5
CHUNK = 64
DN_QK = DN_HEADS * DN_DK
DN_VW = DN_HEADS * DN_DV
N_BRANCH = 2
D_FF = 2816
N_MOD = 9
EPS = 1e-6

SPLIT_SIZES = (
    CONV_A_WIDTH,
    CONV_A_WIDTH,
    CONV_A_WIDTH,
    2 * DN_QK + DN_VW,
    DN_VW,
    4 * DN_HEADS,
    N_BRANCH * D_MODEL,
)
IN_COLS = sum(SPLIT_SIZES)
SPLIT_OFFSETS = tuple(int(v) for v in np.cumsum(SPLIT_SIZES)[:-1])


def _rmsnorm(x, w):
    xf = x.astype(jnp.float32)
    y = xf * lax.rsqrt(jnp.mean(xf * xf, axis=-1, keepdims=True) + EPS)
    return (y * w.astype(jnp.float32)).astype(x.dtype)

def _l2norm(x):
    return x * lax.rsqrt(jnp.sum(x * x, axis=-1, keepdims=True) + EPS)

def _modulate(x, shift, scale):
    return x * (1.0 + scale) + shift

def _swiglu(x, w_up, w_down):
    a, b = jnp.split(x @ w_up, 2, axis=-1)
    return (jax.nn.silu(a) * b) @ w_down

def _dwconv(x, w):
    k_taps = w.shape[0]
    pad = k_taps // 2
    s = x.shape[1]
    xp = jnp.pad(x, ((0, 0), (pad, pad), (0, 0)))
    y = xp[:, 0:s] * w[0]
    for i in range(1, k_taps):
        y = y + xp[:, i:i + s] * w[i]
    return y

def _chunk_gated_delta(q, k, v, beta, g):
    bn, s, h, dk = q.shape
    dv = v.shape[-1]
    n = s // CHUNK

    def to_chunks(t):
        t = t.reshape((bn, n, CHUNK, h) + t.shape[3:])
        return jnp.moveaxis(t, 3, 1)

    q, k, v, beta, g = (to_chunks(t) for t in (q, k, v, beta, g))
    g = jnp.cumsum(g, axis=-1)
    idx = jnp.arange(CHUNK)
    incl = idx[:, None] >= idx[None, :]
    strict = idx[:, None] > idx[None, :]
    decay = jnp.exp(jnp.where(incl, g[..., :, None] - g[..., None, :], -jnp.inf))
    k_beta = k * beta[..., None]
    a_mat = jnp.where(strict, jnp.einsum('bhnid,bhnjd->bhnij', k_beta, k) * decay, 0.0)
    a_mat = a_mat + jnp.eye(CHUNK, dtype=q.dtype)
    rhs = jnp.concatenate([v * beta[..., None], k_beta * jnp.exp(g)[..., None]], axis=-1)
    sol = lax.linalg.triangular_solve(a_mat, rhs, left_side=True, lower=True)
    u, w = sol[..., :dv], sol[..., dv:]
    attn = jnp.einsum('bhnid,bhnjd->bhnij', q, k) * decay

    xs = tuple(jnp.moveaxis(t, 2, 0) for t in (q, k, u, w, g, attn))

    def step(state, inp):
        q_c, k_c, u_c, w_c, g_c, attn_c = inp
        v_new = u_c - jnp.einsum('bhcd,bhde->bhce', w_c, state)
        o_c = (jnp.einsum('bhcd,bhde->bhce', q_c * jnp.exp(g_c)[..., None], state)
               + jnp.einsum('bhij,bhje->bhie', attn_c, v_new))
        g_last = g_c[..., -1:]
        state = (state * jnp.exp(g_last)[..., None]
                 + jnp.einsum('bhcd,bhce->bhde', k_c * jnp.exp(g_last - g_c)[..., None], v_new))
        return state, o_c

    state0 = jnp.zeros((bn, h, dk, dv), q.dtype)
    _, o = lax.scan(step, state0, xs)
    return o.transpose(1, 0, 3, 2, 4).reshape(bn, s, h, dv)

def _hybrid_mixer(u, w_in, conv_a, conv_dn, a_log_fwd, dt_bias_fwd, a_log_bwd, dt_bias_bwd,
                  dn_norm, w_a_out, w_b_out, w_out):
    bn, s, _ = u.shape
    f32 = jnp.float32
    proj = u @ w_in
    ca_b, ca_c, ca_v, dn_qkv, dn_z, dn_ba, gate_logits = jnp.split(proj, SPLIT_OFFSETS, axis=-1)

    y_a = ca_b * _dwconv(ca_c * ca_v, conv_a)

    qkv = jax.nn.silu(_dwconv(dn_qkv, conv_dn))
    q, k, v = jnp.split(qkv, [DN_QK, 2 * DN_QK], axis=-1)
    q = (_l2norm(q.reshape(bn, s, DN_HEADS, DN_DK).astype(f32)) * (DN_DK ** -0.5))
    k = _l2norm(k.reshape(bn, s, DN_HEADS, DN_DK).astype(f32))
    v = v.reshape(bn, s, DN_HEADS, DN_DV).astype(f32)
    b_f, b_b, al_f, al_b = jnp.split(dn_ba.astype(f32), 4, axis=-1)
    beta_f, beta_b = jax.nn.sigmoid(b_f), jax.nn.sigmoid(b_b)
    g_f = -jnp.exp(a_log_fwd.astype(f32)) * jax.nn.softplus(al_f + dt_bias_fwd.astype(f32))
    g_b = -jnp.exp(a_log_bwd.astype(f32)) * jax.nn.softplus(al_b + dt_bias_bwd.astype(f32))
    o_fwd = _chunk_gated_delta(q, k, v, beta_f, g_f)
    rev = lambda t: t[:, ::-1]
    o_bwd = rev(_chunk_gated_delta(rev(q), rev(k), rev(v), rev(beta_b), rev(g_b)))
    o = _rmsnorm(o_fwd + o_bwd, dn_norm) * jax.nn.silu(dn_z.reshape(bn, s, DN_HEADS, DN_DV).astype(f32))
    y_b = o.reshape(bn, s, DN_VW).astype(u.dtype)

    gate_a, gate_b = jnp.split(gate_logits, N_BRANCH, axis=-1)
    merged = jax.nn.sigmoid(gate_a) * (y_a @ w_a_out) + jax.nn.sigmoid(gate_b) * (y_b @ w_b_out)
    return merged @ w_out

def second_inputs(seed: int = 0) -> dict:
    key = jax.random.key(seed)
    ks = jax.random.split(key, 24)
    L = DEPTH_2
    f32 = jnp.float32

    def nrm(k, shape, fan_in):
        return jax.random.normal(k, shape, f32) * (fan_in ** -0.5)

    def gain(k, shape):
        return 1.0 + 0.02 * jax.random.normal(k, shape, f32)

    def a_log(k):
        return jnp.log(jax.random.uniform(k, (L, DN_HEADS), f32, minval=1.0, maxval=16.0))

    def dt_bias(k):
        dt = jnp.exp(jax.random.uniform(k, (L, DN_HEADS), f32,
                                        minval=math.log(1e-3), maxval=math.log(1e-1)))
        return dt + jnp.log(-jnp.expm1(-dt))

    return {
        "x": jax.random.normal(ks[0], (BATCH, SEQ, D_MODEL), f32),
        "c": jax.random.normal(ks[1], (BATCH, D_MODEL), f32),
        "w_ada": nrm(ks[2], (L, D_MODEL, N_MOD * D_MODEL), D_MODEL),
        "b_ada": 0.02 * jax.random.normal(ks[3], (L, N_MOD * D_MODEL), f32),
        "norm_ffn1": gain(ks[4], (L, D_MODEL)),
        "w_ffn1_up": nrm(ks[5], (L, D_MODEL, 2 * D_FF), D_MODEL),
        "w_ffn1_down": nrm(ks[6], (L, D_FF, D_MODEL), D_FF),
        "norm_mix": gain(ks[7], (L, D_MODEL)),
        "w_in": nrm(ks[8], (L, D_MODEL, IN_COLS), D_MODEL),
        "conv_a": nrm(ks[9], (L, CONV_A_K, CONV_A_WIDTH), CONV_A_K),
        "conv_dn": nrm(ks[10], (L, DN_CONV_K, 2 * DN_QK + DN_VW), DN_CONV_K),
        "a_log_fwd": a_log(ks[11]),
        "dt_bias_fwd": dt_bias(ks[12]),
        "a_log_bwd": a_log(ks[13]),
        "dt_bias_bwd": dt_bias(ks[14]),
        "dn_norm": gain(ks[15], (L, DN_DV)),
        "w_a_out": nrm(ks[16], (L, CONV_A_WIDTH, D_MODEL), CONV_A_WIDTH),
        "w_b_out": nrm(ks[17], (L, DN_VW, D_MODEL), DN_VW),
        "w_out": nrm(ks[18], (L, D_MODEL, D_MODEL), D_MODEL),
        "norm_ffn2": gain(ks[19], (L, D_MODEL)),
        "w_ffn2_up": nrm(ks[20], (L, D_MODEL, 2 * D_FF), D_MODEL),
        "w_ffn2_down": nrm(ks[21], (L, D_FF, D_MODEL), D_FF),
        "norm_final": gain(ks[22], (D_MODEL,)),
    }

def second_block(x, c, w_ada, b_ada, norm_ffn1, w_ffn1_up, w_ffn1_down, norm_mix, w_in, conv_a,
              conv_dn, a_log_fwd, dt_bias_fwd, a_log_bwd, dt_bias_bwd, dn_norm, w_a_out, w_b_out,
              w_out, norm_ffn2, w_ffn2_up, w_ffn2_down, norm_final):
    h = x
    c_act = jax.nn.silu(c)
    for l in range(DEPTH_2):
        mod = c_act @ w_ada[l] + b_ada[l]
        sh1, sc1, g1, sh2, sc2, g2, sh3, sc3, g3 = [m[:, None, :] for m in jnp.split(mod, N_MOD, axis=-1)]
        u = _modulate(_rmsnorm(h, norm_ffn1[l]), sh1, sc1)
        h = h + 0.5 * g1 * _swiglu(u, w_ffn1_up[l], w_ffn1_down[l])
        u = _modulate(_rmsnorm(h, norm_mix[l]), sh2, sc2)
        h = h + g2 * _hybrid_mixer(u, w_in[l], conv_a[l], conv_dn[l], a_log_fwd[l], dt_bias_fwd[l],
                                   a_log_bwd[l], dt_bias_bwd[l], dn_norm[l], w_a_out[l],
                                   w_b_out[l], w_out[l])
        u = _modulate(_rmsnorm(h, norm_ffn2[l]), sh3, sc3)
        h = h + 0.5 * g3 * _swiglu(u, w_ffn2_up[l], w_ffn2_down[l])
    return _rmsnorm(h, norm_final)


def setup_inputs(seed=0):
    out = dict(first_inputs(seed))
    for name, value in second_inputs(seed + 1).items():
        if name != "x":
            out[name + "_2"] = value
    return out


def reference(
    x, c, norm_g, ada_w, ada_b, nsa_w_in, nsa_pe_k, nsa_pe_v, nsa_ck_w1, nsa_ck_w2, nsa_cv_w1,
    nsa_cv_w2, nsa_w_out, dil_w_in, dil_w_out, final_g, c_2, w_ada_2, b_ada_2, norm_ffn1_2,
    w_ffn1_up_2, w_ffn1_down_2, norm_mix_2, w_in_2, conv_a_2, conv_dn_2, a_log_fwd_2,
    dt_bias_fwd_2, a_log_bwd_2, dt_bias_bwd_2, dn_norm_2, w_a_out_2, w_b_out_2, w_out_2,
    norm_ffn2_2, w_ffn2_up_2, w_ffn2_down_2, norm_final_2,
):
    x = first_block(
        x, c, norm_g, ada_w, ada_b, nsa_w_in, nsa_pe_k, nsa_pe_v, nsa_ck_w1, nsa_ck_w2,
        nsa_cv_w1, nsa_cv_w2, nsa_w_out, dil_w_in, dil_w_out, final_g,
    )
    return second_block(
        x, c_2, w_ada_2, b_ada_2, norm_ffn1_2, w_ffn1_up_2, w_ffn1_down_2, norm_mix_2, w_in_2,
        conv_a_2, conv_dn_2, a_log_fwd_2, dt_bias_fwd_2, a_log_bwd_2, dt_bias_bwd_2, dn_norm_2,
        w_a_out_2, w_b_out_2, w_out_2, norm_ffn2_2, w_ffn2_up_2, w_ffn2_down_2, norm_final_2,
    )


_drawn_inputs = setup_inputs


def setup_inputs(seed=0):
    import zlib

    import numpy as np

    out = dict(_drawn_inputs(seed))
    spreads = {}
    factors = {'norm_g': 3.882,
     'ada_b': 3.415,
     'nsa_pe_k': 8.0,
     'nsa_pe_v': 7.076,
     'nsa_ck_w1': 3.04,
     'nsa_ck_w2': 2.987,
     'norm_ffn1_2': 5.51,
     'norm_mix_2': 2.919,
     'a_log_fwd_2': 2.958,
     'dn_norm_2': 63.535,
     'norm_ffn2_2': 21.918,
     'norm_final_2': 8.697}
    for name, (base, spread) in spreads.items():
        noise = np.random.default_rng([zlib.crc32(name.encode()), seed]).standard_normal(out[name].shape)
        drawn = base * np.exp(spread * noise) if base else spread * noise
        out[name] = jnp.asarray(drawn.astype(out[name].dtype))
    for name, factor in factors.items():
        out[name] = (out[name] * factor).astype(out[name].dtype)
    return out
```

```python
from contextlib import ExitStack

import numpy as np
import concourse.bass as bass
from concourse import mybir

P = 128
T = 256
TT = T // P
D = 1024
KC = D // P
NH, DH = 16, 64
G, HG = 2, 8
SCALE = DH ** -0.5
CMP_LEN, CMP_STRIDE, CMP_HIDDEN = 32, 16, 256
NCMP = (T - CMP_LEN) // CMP_STRIDE + 1
D_FF = 2816
FFN_OUTS = D_FF // 256
FC = D_FF // P
DN_HEADS, DN_D = 8, 128
CONV_A = 512
EPS = 1e-6
NEG = -1e30
FLOOR = -1e25

F32 = mybir.dt.float32
ALU = mybir.AluOpType
ACT = mybir.ActivationFunctionType
AX = mybir.AxisListType.X

UNIT = 2048
RING = 7
DIL_MASK = ((0, 6, "window"), (6, 11, 4), (11, 16, 16))
N_LEVELS = 7


def constants():
    p = np.arange(P)
    parts, where, at = [], {}, 0

    def add(name, a):
        nonlocal at
        a = np.asarray(a, np.float32).reshape(P, -1)
        parts.append(a)
        where[name] = (at, at + a.shape[1])
        at += a.shape[1]

    add("ident", np.eye(P))
    add("ones", np.ones((P, P)))
    q = P + p[:, None]
    k = np.arange(T)[None, :]
    causal = k <= q
    add("mask_causal", np.where(causal, 0.0, NEG))
    add("mask_window", np.where(causal & (q - k <= 128), 0.0, NEG))
    add("mask_4", np.where(causal & ((q - k) % 4 == 0), 0.0, NEG))
    add("mask_16", np.where(causal & ((q - k) % 16 == 0), 0.0, NEG))
    t = p[:, None] + P * np.arange(TT)[None, :]
    cmp_end = CMP_STRIDE * np.arange(NCMP) + CMP_LEN - 1
    add("mask_cmp", np.where(cmp_end[None, None, :] <= t[:, :, None], 0.0, NEG))
    half = DH // 2
    inv = (np.float32(10000.0) ** (-np.arange(half, dtype=np.float32) / np.float32(half))).astype(np.float32)
    ang = (t.astype(np.float32)[:, :, None] * inv[None, None, :]).astype(np.float32)
    cos, sin = np.cos(ang), np.sin(ang)
    add("rope_cos", np.concatenate([cos, cos], -1))
    add("rope_sin", np.concatenate([-sin, sin], -1))
    add("head_block", np.where(p[:, None] // NCMP == np.arange(HG)[None, :], 1.0, 0.0))
    for lv in range(N_LEVELS):
        s = 1 << lv
        add(f"level_{lv}", (p[:, None] // (2 * s) == p[None, :] // (2 * s)) & (p[:, None] // s != p[None, :] // s))
    j, i = p[:, None], p[None, :]
    add("incl_fwd", np.where(j <= i, 0.0, NEG))
    add("incl_bwd", np.where(j >= i, 0.0, NEG))
    add("cum_fwd", j <= i)
    add("cum_bwd", j >= i)
    add("minus_half", np.full((P, 1), -0.5))
    add("after", j > i)
    add("before", j < i)
    add("half", np.full((P, 1), 0.5))
    return np.ascontiguousarray(np.concatenate(parts, 1)), where


CONST_TABLE, CONST_AT = constants()


class Plan:

    def __init__(self, stages):
        self.units = []
        self.count = {"pe": 0, "ada": 0}
        self.outputs = {}
        self.freers = []
        self.slot_total = [0] * RING
        self.arrive = []
        for kind, key, lots, freers in stages:
            first = len(self.units)
            for dmas in lots:
                slot = len(self.units) % RING
                self.slot_total[slot] += 16 * len(dmas)
                self.arrive.append(self.slot_total[slot])
                consumer = "ada" if kind == "ada" else "pe"
                self.units.append((dmas, consumer, self.count[consumer]))
                self.count[consumer] += 1
            if kind == "gemm":
                self.outputs[key] = (len(self.freers), list(range(first, len(self.units))))
                self.freers.append(freers)
            else:
                self.outputs[key] = (None, list(range(first, len(self.units))))

    def free_count(self, eng, tt, o):
        return sum(eng in f[tt] for f in self.freers[:o + 1])


def column_units(w, width_cols, kc_total, kc=4):
    lots = []
    for k0 in range(0, kc_total, kc):
        kn = min(kc, kc_total - k0)
        dmas, at = [], 0
        for ap, c0, cn in w:
            dmas.append((ap[k0 * P:(k0 + kn) * P, c0:c0 + cn].rearrange("(k p) n -> p k n", p=P), kn, width_cols, at, cn))
            at += cn
        lots.append(dmas)
    return lots

ARENA = 24470
LAST_BLOCK = 2


QKV = 3 * DN_HEADS * DN_D
Z_AT = 3 * CONV_A + QKV
BA_AT = Z_AT + DN_HEADS * DN_D
GATE_W = 416


def first_stages(A):
    both = {0: ("dve", "act"), 1: ("dve", "act")}
    dve, act = {0: ("dve",), 1: ("dve",)}, {0: ("act",), 1: ("act",)}
    gated = {0: ("gated",), 1: ("gated",)}
    ada0, ada1 = A["ada_w"][0], A["ada_w"][1]
    w, o, ck, cv = A["nsa_w_in"][0], A["nsa_w_out"][0], A["nsa_ck_w1"][0], A["nsa_cv_w1"][0]
    dw, do = A["dil_w_in"][0], A["dil_w_out"][0]
    a2 = A["w_ada_2"][0]

    def ada(n):
        src = (ada0, ada1, a2)[min(n // 6, 2)]
        c = 512 * (n - 6 * min(n // 6, 2))
        return ("ada", ("ada", n), column_units([(src, c, 512)], 512, KC), None)

    def gemm(stage, j, ap, c, n, freers, kc=KC):
        return ("gemm", (stage, j), column_units([(ap, c, n)], n, kc), freers)

    s = [ada(n) for n in range(4)]
    s += [gemm("nsa", 2, w, 1024, 512, both), ada(4), gemm("nsa", 3, w, 1536, 512, both), ada(5)]
    s += [gemm("nsa", 0, w, 0, 512, both), ada(6), gemm("nsa", 1, w, 512, 512, both), ada(7)]
    s += [("pe", ("cmp", 0), column_units([(ck, 0, 256)], 256, 16, 8), None),
          ("pe", ("cmp", 1), column_units([(cv, 0, 256)], 256, 16, 8), None)]
    s += [gemm("nsa", 4, w, 2048, 512, act), ada(8), gemm("nsa", 5, w, 2560, 304, act), ada(9)]
    s += [gemm("nsa_out", j, o, 512 * j, 512, gated) for j in range(2)]
    s += [ada(10), ada(11)]
    for j in range(8):
        s.append(gemm("dil", j, dw, 512 * j, 512, dve if j < 4 else act))
        if j < 6:
            s.append(ada(12 + j))
    s += [gemm("dil_out", j, do, 512 * j, 512, gated) for j in range(2)]
    return s, ada, gemm


def second_stages(A, ada, gemm):
    dve, act = {0: ("dve",), 1: ("dve",)}, {0: ("act",), 1: ("act",)}
    gated = {0: ("gated",), 1: ("gated",)}
    s = []

    def ffn(name, up, down, adas):
        for j in range(FFN_OUTS):
            s.append(("gemm", (name + "_up", j),
                      column_units([(up, 256 * j, 256), (up, D_FF + 256 * j, 256)], 512, KC), dve))
            if j < len(adas):
                s.append(ada(adas[j]))
        for j in range(2):
            s.append(gemm(name + "_down", j, down, 512 * j, 512, gated, FC))

    ffn("ffn1", A["w_ffn1_up_2"][0], A["w_ffn1_down_2"][0], range(18, 24))
    w = A["w_in_2"][0]
    for j in range(6):
        s.append(gemm("qkv", j, w, 3 * CONV_A + 512 * j, 512, act))
    both = {0: ("dve", "act"), 1: ("dve", "act")}
    s.append(gemm("ba", 0, w, BA_AT, GATE_W, both))
    for j in range(3):
        s.append(gemm("ca", j, w, CONV_A * j, CONV_A, (act, act, dve)[j]))
    for j in range(2):
        s += [gemm("z", j, w, Z_AT + 512 * j, 512, act), ada(24 + j)]
    for j in range(4):
        s += [gemm("gate", j, w, BA_AT + GATE_W * (j + 1), GATE_W, act), ada(26 + j)]
    for j in range(2):
        s.append(gemm("a_out", j, A["w_a_out_2"][0], 512 * j, 512, dve, CONV_A // P))
    for j in range(2):
        s.append(gemm("b_out", j, A["w_b_out_2"][0], 512 * j, 512, dve))
    for j in range(2):
        s.append(gemm("mix_out", j, A["w_out_2"][0], 512 * j, 512, gated))
    ffn("ffn2", A["w_ffn2_up_2"][0], A["w_ffn2_down_2"][0], [])
    return s


def second_turns():
    t = [("norm2", b) for b in range(4)] + [("ffn1_h", j) for j in range(FFN_OUTS)]
    t += [("norm3", b) for b in range(4)]
    t += [("qkv", b) for b in range(12)] + [("prod", b) for b in range(2)] + [("cab", b) for b in range(2)]
    t += [("v", b) for b in range(4)] + [("grow", 0)] + [("y_b", b) for b in range(4)] + [("merged", b) for b in range(4)]
    t += [("norm4", b) for b in range(4)] + [("ffn2_h", j) for j in range(FFN_OUTS)]
    return t


class Chain:

    def __init__(self, eng, sem):
        self.eng, self.sem, self.n = eng, sem, 0

    def __call__(self, ins):
        self.mark(ins)
        self.wait()

    def mark(self, ins):
        self.n += 1
        ins.then_inc(self.sem, 1)

    def wait(self):
        self.eng.wait_ge(self.sem, self.n)


def build(nc, A, const_ap, out, last_block=2):
    ctx = ExitStack()
    with ctx:
        def sb(name, shape):
            return ctx.enter_context(nc.sbuf_tensor(name, shape, F32))

        def sem(name):
            return ctx.enter_context(nc.semaphore(name))

        const = sb("const", [P, CONST_TABLE.shape[1]])

        def C(name):
            a, b = CONST_AT[name]
            return const[:, a:b]

        ident, ones = C("ident"), C("ones")
        ring = sb("ring", [P, RING, UNIT])
        x = sb("x", [P, TT, D])
        xn = sb("xn", [P, TT, D])
        lhs = sb("lhs", [P, KC, T])
        rows = sb("rows", [P, 3, P])
        cols = sb("cols", [P, 3, P])
        c_act = sb("c_act", [P, 2 * KC])
        ada_acc = sb("ada_acc", [P, 2, 512])
        mod_shift = sb("mod_shift", [P, 5, KC])
        mod_tmp = sb("mod_tmp", [P, 4])
        mod_scale = sb("mod_scale", [P, 5, KC])
        gate_row = sb("gate_row", [P, 2, D])
        y_gated = sb("y_gated", [P, 2, 512])
        stat = sb("stat", [P, 7, 3, TT])
        arena = sb("arena", [P, ARENA])
        bank = [ctx.enter_context(nc.psum_tensor(f"bank{i}", [P, 512], F32))[:, :] for i in range(8)]

        class Space:

            def __init__(self, at=0):
                self.at = at

            def take(self, *shape):
                n = 1
                for s in shape:
                    n *= s
                assert self.at + n <= ARENA, (self.at, n)
                view = arena[:, self.at:self.at + n]
                self.at += n
                names = "abcd"[:len(shape)]
                if len(shape) > 1:
                    view = view.rearrange(f"p ({' '.join(names)}) -> p {' '.join(names)}",
                                          **dict(zip(names, shape)))
                return view

        landed = [sem(f"landed{i}") for i in range(RING)]
        pe_units = sem("pe_units")
        ada_units = sem("ada_units")
        gemm_tile0 = sem("gemm_tile0")
        y_ready = [sem(f"y_ready{t}") for t in range(TT)]
        bank_free = {(e, t): sem(f"bank_free_{e}{t}") for e in ("dve", "act") for t in range(TT)}
        bank_free.update({("gated", t): y_ready[t] for t in range(TT)})
        turned = sem("turned")
        turn_read = {"dve": sem("turn_read_dve"), "act": sem("turn_read_act")}
        params_in = sem("params_in")
        x_in = sem("x_in")
        cols_done = sem("cols_done")
        cols_ready = sem("cols_ready")
        c_ready = sem("c_ready")
        ada_summed = sem("ada_summed")
        mod_ready = sem("mod_ready")
        dve_chain = sem("dve_chain")
        act_chain = sem("act_chain")
        x_ready = sem("x_ready")
        x_scaled = sem("x_scaled")
        gain_in = sem("gain_in")
        squares = sem("squares")
        mean_ready = sem("mean_ready")
        rstd_ready = sem("rstd_ready")
        xn_ready = {"dve": sem("xn_ready_dve"), "act": sem("xn_ready_act")}
        stored = sem("stored")

        stages, ada_stage, gemm_stage = first_stages(A)
        if last_block == 2:
            stages += second_stages(A, ada_stage, gemm_stage)
        plan = Plan(stages)

        TURNS = turn_order(last_block)
        TURN_AT = {t: i for i, t in enumerate(TURNS)}

        def turn_bank(name, b=0):
            return bank[4 + TURN_AT[name, b] % 2]

        def turn_reader(name, b=0):
            return ("dve", "act")[TURN_AT[name, b] % 2]

        def await_unit(eng, u):
            eng.wait_ge(landed[u % RING], plan.arrive[u])

        def gemm(pe, stage, j, left, n, kc_unit=4, kc_total=KC):
            o, units = plan.outputs[stage, j]
            k0 = 0
            for u in units:
                await_unit(pe, u)
                kn = min(kc_unit, kc_total - k0)
                for tt in range(TT):
                    if k0 == 0 and o >= 2:
                        for e in plan.freers[o - 2][tt]:
                            pe.wait_ge(bank_free[e, tt], plan.free_count(e, tt, o - 2))
                    for k in range(kn):
                        mm = pe.matmul(bank[2 * (o % 2) + tt][:, 0:n], left(k0 + k, tt),
                                       ring[:, u % RING, k * n:(k + 1) * n],
                                       start=(k0 + k == 0), stop=(k0 + k == kc_total - 1))
                    if tt == 0 and k0 + kn == kc_total:
                        mm.then_inc(gemm_tile0, 1)
                mm.then_inc(pe_units, 1)
                k0 += kn

        def gemm_bank(stage, j, tt):
            return bank[2 * (plan.outputs[stage, j][0] % 2) + tt]

        def await_output(eng, stage, j, tt):
            o, units = plan.outputs[stage, j]
            if tt == 0:
                eng.wait_ge(gemm_tile0, o + 1)
            else:
                eng.wait_ge(pe_units, plan.units[units[-1]][2] + 1)

        def turn(pe, name, b, blocks):
            i = TURN_AT[name, b]
            if i >= 2:
                e = ("dve", "act")[i % 2]
                pe.wait_ge(turn_read[e], i // 2)
            for src, kin, mout, col in blocks:
                mm = pe.transpose(bank[4 + i % 2][0:mout, col:col + kin], src, ident[0:kin, 0:kin])
            mm.then_inc(turned, 1)

        def await_turn(eng, name, b=0):
            eng.wait_ge(turned, TURN_AT[name, b] + 1)

        def turn_tokens(pe, name, src, banks):
            for b in banks:
                turn(pe, name, b, [(src(tt, 2 * b + h), P, P, h * T + tt * P)
                                   for h in range(2) for tt in range(TT)])

        def copy(eng, dst, src):
            return eng.tensor_copy(dst, src) if eng is nc.vector else eng.copy(dst, src)

        ENG = {"dve": nc.vector, "act": nc.scalar}

        def read_turns(who, name, dst, banks):
            for b in banks:
                if turn_reader(name, b) == who:
                    await_turn(ENG[who], name, b)
                    copy(ENG[who], dst(b), turn_bank(name, b)).then_inc(turn_read[who], 1)

        def await_turns_read(eng, name, banks):
            for e in ("dve", "act"):
                last = max([TURN_AT[name, b] for b in banks if turn_reader(name, b) == e], default=None)
                if last is not None:
                    eng.wait_ge(turn_read[e], last // 2 + 1)

        def ada_accumulate(dve, n, link):
            _, units = plan.outputs["ada", n]
            acc = ada_acc[:, n % 2, :]
            if n >= 2:
                dve.wait_ge(ada_summed, n - 1)
            c0 = 0 if n < 12 else KC
            for u in units:
                await_unit(dve, u)
                for k in range(4):
                    kk = 4 * units.index(u) + k
                    w = ring[:, u % RING, k * 512:(k + 1) * 512]
                    s = c_act[:, c0 + kk:c0 + kk + 1]
                    if kk == 0:
                        link(dve.tensor_scalar(acc, w, s, None, ALU.mult))
                    elif k < 3:
                        link(dve.scalar_tensor_tensor(acc, w, s, acc, ALU.mult, ALU.add))
                    else:
                        dve.scalar_tensor_tensor(acc, w, s, acc, ALU.mult, ALU.add).then_inc(ada_units, 1)
                        dve.wait_ge(ada_units, plan.units[u][2] + 1)

        def ada_sum(pe, n):
            _, units = plan.outputs["ada", n]
            pe.wait_ge(ada_units, plan.units[units[-1]][2] + 1)
            if n >= 1:
                pe.wait_ge(mod_ready, n)
            acc = ada_acc[:, n % 2, :]
            if n % 6 < 4:
                for c in range(4):
                    mm = pe.matmul(bank[7][:, c:c + 1], acc[:, c * P:(c + 1) * P], ones[:, 0:1],
                                   start=True, stop=True)
            else:
                for c in range(4):
                    r = 4 * n + c
                    mm = pe.matmul(bank[6][:, c * P:(c + 1) * P], ones, acc[:, c * P:(c + 1) * P],
                                   start=True, stop=False)
                    mm = pe.matmul(bank[6][:, c * P:(c + 1) * P], bias_pick(r), rows[0:120, 2, :],
                                   start=False, stop=True)
            mm.then_inc(ada_summed, 1)

        def bias_pick(r):
            return ident[0:120, r:r + 1].broadcast_to([120, P])

        def ada_collect(dve, n, link):
            layer, part = n // 6, n % 6
            dve.wait_ge(ada_summed, n + 1)
            half = slice(4 * (part % 2), 4 * (part % 2) + 4)
            bias = cols[:, 2, 4 * n:4 * n + 4]
            if part < 2:
                dve.tensor_tensor(mod_shift[:, layer, half], bank[7][:, 0:4], bias, ALU.add).then_inc(mod_ready, 1)
            elif part < 4:
                gain = cols[:, 0, 16 + 8 * layer + half.start:16 + 8 * layer + half.stop]
                link(dve.tensor_tensor(mod_tmp[:, :], bank[7][:, 0:4], bias, ALU.add))
                dve.scalar_tensor_tensor(mod_scale[:, layer, half], mod_tmp[:, :], 1.0, gain,
                                         ALU.add, ALU.mult).then_inc(mod_ready, 1)
            else:
                row = gate_row[:, layer % 2, 512 * (part % 2):512 * (part % 2) + 512]
                half_ffn = 0.5 if layer in (2, 4) else 1.0
                dve.tensor_scalar(row, bank[6][:, :], half_ffn, None, ALU.mult).then_inc(mod_ready, 1)

        def await_x(eng, n):
            if n == 0:
                eng.wait_ge(x_in, 16)
            elif n == 2:
                eng.wait_ge(x_scaled, TT)
            else:
                eng.wait_ge(x_ready, 4 * n)

        def statistic(n):
            return n if n < 2 else n + 1

        def mean_dve(dve, i, link):
            link(dve.tensor_tensor_reduce(xn[:, 1, :], x[:, 1, :], x[:, 1, :], 1.0, 0.0, ALU.mult, ALU.add,
                                          stat[:, i, 0, 1:2]))
            dve.wait_ge(squares, i + 1)
            dve.tensor_scalar(stat[:, i, 1, :], stat[:, i, 0, :], 1.0 / D, EPS, ALU.mult,
                              ALU.add).then_inc(mean_ready, 1)
            dve.wait_ge(rstd_ready, i + 1)

        def squares_act(act, i):
            act.activation(xn[:, 0, :], x[:, 0, :], ACT.Square, accum_out=stat[:, i, 0, 0:1]).then_inc(squares, 1)

        def rstd_pool(pool, i):
            pool.wait_ge(mean_ready, i + 1)
            pool.tensor_tensor(stat[:, i, 2, :], stat[:, i, 1, :], C("minus_half").broadcast_to([P, TT]),
                               ALU.pow).then_inc(rstd_ready, 1)

        def norm_dve(dve, n, link):
            i = statistic(n)
            await_x(dve, n)
            mean_dve(dve, i, link)
            dve.tensor_scalar(xn[:, 0, :], x[:, 0, :], stat[:, i, 2, 0:1], None, ALU.mult).then_inc(xn_ready["dve"], 1)

        def norm_act(act, n):
            i = statistic(n)
            await_x(act, n)
            squares_act(act, i)
            act.wait_ge(rstd_ready, i + 1)
            act.activation(xn[:, 1, :], x[:, 1, :], ACT.Copy, scale=stat[:, i, 2, 1:2]).then_inc(xn_ready["act"], 1)

        def norm_pe(pe, n):
            pe.wait_ge(xn_ready["dve"], n + 1)
            pe.wait_ge(xn_ready["act"], n + 1)
            turn_tokens(pe, f"norm{n}", lambda tt, c: xn[:, tt, c * P:(c + 1) * P], range(4))

        def norm_read(who, n):
            eng = ENG[who]
            eng.wait_ge(mod_ready, 6 * n + 4)
            for b in range(4):
                if turn_reader(f"norm{n}", b) != who:
                    continue
                await_turn(eng, f"norm{n}", b)
                for h in range(2):
                    c = 2 * b + h
                    src = turn_bank(f"norm{n}", b)[:, h * T:(h + 1) * T]
                    a, s = mod_scale[:, n, c:c + 1], mod_shift[:, n, c:c + 1]
                    if who == "dve":
                        ins = eng.tensor_scalar(lhs[:, c, :], src, a, s, ALU.mult, ALU.add)
                    else:
                        ins = eng.activation(lhs[:, c, :], src, ACT.Identity, bias=s, scale=a)
                ins.then_inc(turn_read[who], 1)

        def from_lhs(k, tt):
            return lhs[:, k, tt * P:(tt + 1) * P]

        def residual_dve(dve, layer, stage, link, between=None):
            for j in range(2):
                for tt in range(TT):
                    await_output(dve, stage, j, tt)
                    step = 2 * layer + j
                    if step >= 1:
                        dve.wait_ge(x_ready, 2 * step + tt - 1)
                    dve.wait_ge(mod_ready, 6 * layer + 5 + j)
                    dve.tensor_tensor(y_gated[:, tt, :], gemm_bank(stage, j, tt)[:, :],
                                      gate_row[:, layer % 2, 512 * j:512 * (j + 1)], ALU.mult).then_inc(y_ready[tt], 1)
                if between:
                    between(j)

        def residual_pool(pool, layer):
            for j in range(2):
                for tt in range(TT):
                    pool.wait_ge(y_ready[tt], 2 * layer + j + 1)
                    xs = x[:, tt, 512 * j:512 * (j + 1)]
                    pool.tensor_tensor(xs, xs, y_gated[:, tt, :], ALU.add).then_inc(x_ready, 1)

        nsa = Space()
        rope_a = nsa.take(2, TT, 512)
        rope_b = nsa.take(2, TT, 512)
        nsa_rope_end = nsa.at
        q_plain = nsa.take(TT, NH, DH)
        q_rope = nsa.take(TT, NH, DH)
        z_act = nsa.take(TT, D)
        gates = nsa.take(TT, 3 * NH)
        late = Space(nsa.at)
        kc2, vc2, ks2, kw2 = [nsa.take(TT, G, 2, DH) for _ in range(4)]
        v_slc, v_win = nsa.take(TT, G, DH), nsa.take(TT, G, DH)
        ksT, kwT = nsa.take(G, T), nsa.take(G, T)
        kc_next, vc_next = nsa.take(G, T), nsa.take(G, T)
        qpT, qrT = nsa.take(KC, T), nsa.take(KC, T)
        nsa_o = q_plain
        o_part = nsa.take(2, HG, DH)
        blocks = nsa.take(2, CMP_LEN // 2, G, NCMP)
        w2k = nsa.take(2, 2, DH)
        w2v = nsa.take(2, DH)
        hidden = nsa.take(2, CMP_HIDDEN)
        hidT = nsa.take(2, 2, G * NCMP)
        hid_rep = nsa.take(2, G, HG, NCMP)
        k_cmpT = nsa.take(G * NCMP)
        v_blocks = nsa.take(G, HG, DH)
        s_cmp = late.take(TT, NH, NCMP)
        p_cmp = late.take(TT, NH, NCMP)
        m_cmp, d_cmp, w_cmp = [late.take(TT, NH) for _ in range(3)]
        p_cmpT = late.take(TT, G, P)

        class Attention:

            def __init__(self, name, space, items):
                self.name, self.items, n = name, items, len(items)
                self.masked = space.take(2, 3 * P)
                self.probs = space.take(2, 3 * P)
                self.probsT = space.take(2, 3 * P)
                self.top = space.take(n, TT)
                self.bias = space.take(n, TT)
                self.den = space.take(n, TT)
                self.rden = space.take(n // 8, TT, 8)
                self.weight = space.take(n // 8, TT, 8)
                self.scored = sem(name + "_scored")
                self.masked_done = sem(name + "_masked")
                self.bias_ready = sem(name + "_bias_ready")
                self.exp_done = sem(name + "_exp_done")
                self.probs_turned = sem(name + "_probs_turned")
                self.probsT_ready = [sem(name + "_probsT_act"), sem(name + "_probsT_dve")]
                self.pv_done = sem(name + "_pv_done")
                self.pv_read = sem(name + "_pv_read")

            def pe(self, pe):
                n = len(self.items)
                for i in range(n + 2):
                    if i < n:
                        q, k, _, _ = self.items[i]
                        if i >= 2:
                            pe.wait_ge(self.masked_done, i - 1)
                        pe.matmul(bank[i % 2][:, 0:P], q(0), k()[:, 0:P], start=True, stop=True)
                        pe.matmul(bank[i % 2][:, P:3 * P], q(1), k(), start=True,
                                  stop=True).then_inc(self.scored, 1)
                    if 1 <= i <= n:
                        j = i - 1
                        pe.wait_ge(self.exp_done, j + 1)
                        if j >= 2:
                            pe.wait_ge(self.probsT_ready[j % 2], j // 2)
                        for b in range(3):
                            mm = pe.transpose(bank[2 + j % 2][:, b * P:(b + 1) * P],
                                              self.probs[:, j % 2, b * P:(b + 1) * P], ident)
                        mm.then_inc(self.probs_turned, 1)
                    if i >= 2:
                        j = i - 2
                        g, c = j // 8, (j % 8) * DH
                        pe.wait_ge(self.probsT_ready[j % 2], j // 2 + 1)
                        if j % 8 == 0 and g >= 2:
                            pe.wait_ge(self.pv_read, g - 1)
                        v = self.items[j][3]
                        pT = self.probsT[:, j % 2, :]
                        o0, o1 = bank[4 + 2 * (g % 2)], bank[5 + 2 * (g % 2)]
                        pe.matmul(o0[:, c:c + DH], pT[:, 0:P], v(0), start=True, stop=True)
                        pe.matmul(o1[:, c:c + DH], pT[:, P:2 * P], v(0), start=True, stop=False)
                        pe.matmul(o1[:, c:c + DH], pT[:, 2 * P:3 * P], v(1), start=False,
                                  stop=True).then_inc(self.pv_done, 1)

            def dve(self, dve, link, weigh):
                n = len(self.items)
                for i in range(n + 3):
                    if i < n:
                        mask = self.items[i][2]
                        dve.wait_ge(self.scored, i + 1)
                        if i >= 2:
                            dve.wait_ge(self.exp_done, i - 1)
                        m, s = self.masked[:, i % 2, :], bank[i % 2]
                        dve.tensor_tensor_reduce(m[:, 0:P], s[:, 0:P], mask[:, P:T], 1.0, NEG, ALU.add, ALU.max,
                                                 self.top[:, i, 0:1])
                        dve.tensor_tensor_reduce(m[:, P:3 * P], s[:, P:3 * P], mask, 1.0, NEG, ALU.add, ALU.max,
                                                 self.top[:, i, 1:2]).then_inc(self.masked_done, 1)
                        dve.wait_ge(self.masked_done, i + 1)
                        dve.tensor_scalar(self.bias[:, i, :], self.top[:, i, :], -SCALE, None,
                                          ALU.mult).then_inc(self.bias_ready, 1)
                    if 2 <= i < n + 2 and i % 2 == 1:
                        self.copy_turned(dve, i - 2)
                    if i >= 3 and (i - 3) % 8 == 7:
                        weigh((i - 3) // 8)
                    

            def copy_turned(self, eng, j):
                eng.wait_ge(self.probs_turned, j + 1)
                if j >= 2:
                    eng.wait_ge(self.pv_done, j - 1)
                copy(eng, self.probsT[:, j % 2, :], bank[2 + j % 2][:, 0:3 * P]).then_inc(self.probsT_ready[j % 2], 1)

            def act(self, act):
                n = len(self.items)
                for i in range(n + 1):
                    if i < n:
                        act.wait_ge(self.bias_ready, i + 1)
                        if i >= 2:
                            act.wait_ge(self.probs_turned, i - 1)
                        m, p = self.masked[:, i % 2, :], self.probs[:, i % 2, :]
                        act.activation(p[:, 0:P], m[:, 0:P], ACT.Exp, bias=self.bias[:, i, 0:1], scale=SCALE,
                                       accum_out=self.den[:, i, 0:1])
                        act.activation(p[:, P:3 * P], m[:, P:3 * P], ACT.Exp, bias=self.bias[:, i, 1:2],
                                       scale=SCALE, accum_out=self.den[:, i, 1:2]).then_inc(self.exp_done, 1)
                    if i >= 1 and (i - 1) % 2 == 0:
                        self.copy_turned(act, i - 1)

            def reciprocal(self, dve, g, link):
                dve.wait_ge(self.exp_done, 8 * g + 8)
                link(dve.reciprocal(self.rden[:, g, :, :],
                                    self.den[:, 8 * g:8 * g + 8, :].rearrange("p h t -> p t h")))

        def head_rows(h):
            return slice(DH * (h % 2), DH * (h % 2) + DH)

        def nsa_item(kT, v, g, h):
            hh = HG * g + h
            return (lambda tt: qrT[head_rows(hh), hh // 2, tt * P:(tt + 1) * P],
                    lambda: kT[head_rows(hh), g, :], C("mask_causal"),
                    lambda kt: v[:, kt, g, :])

        nsa_att = Attention("nsa_att", Space(0), [nsa_item(kT, v, g, h) for g in range(G)
                                             for kT, v in ((ksT, v_slc), (kwT, v_win)) for h in range(HG)])

        rope_done = sem("rope_done")
        blocks_ready = sem("blocks_ready")
        w2_in = sem("w2_in")
        hidden_act = sem("hidden_act")
        cmp_kv_done, cmp_kv_read = sem("cmp_kv_done"), sem("cmp_kv_read")
        cmp_scored, cmp_shifted, cmp_exp = sem("cmp_scored"), sem("cmp_shifted"), sem("cmp_exp")
        cmp_pv_done, cmp_pv_read = sem("cmp_pv_done"), sem("cmp_pv_read")
        o_added = sem("o_added")
        o_ready = sem("o_ready")

        ROPES = [("nsa", 2), ("nsa", 3), ("nsa", 0), ("nsa", 1), ("dil", 0), ("dil", 1), ("dil", 2), ("dil", 3)]

        def rope_parts(dve, key, src, heads):
            r = ROPES.index(key)
            cos = C("rope_cos").rearrange("p (t d) -> p t d", t=TT)
            sin = C("rope_sin").rearrange("p (t d) -> p t d", t=TT)
            for tt in range(TT):
                await_output(dve, *key, tt)
                if r >= 2:
                    dve.wait_ge(rope_done, 2 * (r - 2) + tt + 1)
                n = heads * DH
                s = src(tt).rearrange("p (h d) -> p h d", d=DH)
                a = rope_a[:, r % 2, tt, 0:n].rearrange("p (h d) -> p h d", d=DH)
                b = rope_b[:, r % 2, tt, 0:n].rearrange("p (h d) -> p h d", d=DH)
                half = DH // 2
                dve.tensor_tensor(a, s, cos[:, tt:tt + 1, :].broadcast_to([P, heads, DH]), ALU.mult)
                dve.tensor_tensor(b[:, :, 0:half], s[:, :, half:DH],
                                  sin[:, tt:tt + 1, 0:half].broadcast_to([P, heads, half]), ALU.mult)
                dve.tensor_tensor(b[:, :, half:DH], s[:, :, 0:half],
                                  sin[:, tt:tt + 1, half:DH].broadcast_to([P, heads, half]),
                                  ALU.mult).then_inc(bank_free["dve", tt], 1)

        def rope_add(pool, key, dst, heads):
            r = ROPES.index(key)
            o = plan.outputs[key][0]
            for tt in range(TT):
                pool.wait_ge(bank_free["dve", tt], plan.free_count("dve", tt, o))
                n = heads * DH
                a = rope_a[:, r % 2, tt, 0:n].rearrange("p (h d) -> p h d", d=DH)
                b = rope_b[:, r % 2, tt, 0:n].rearrange("p (h d) -> p h d", d=DH)
                for d in dst(tt)[:-1]:
                    pool.tensor_tensor(d, a, b, ALU.add)
                pool.tensor_tensor(dst(tt)[-1], a, b, ALU.add).then_inc(rope_done, 1)

        def nsa_dve(dve, link):
            for tt in range(TT):
                await_output(dve, "nsa", 2, tt)
                src = gemm_bank("nsa", 2, tt)
                for d, c in ((kc2, 0), (vc2, P)):
                    for twice in range(2):
                        ins = dve.tensor_copy(d[:, tt, :, twice, :],
                                              src[:, c:c + P].rearrange("p (g d) -> p g d", g=G))
            rope_parts(dve, ("nsa", 2), lambda tt: gemm_bank("nsa", 2, tt)[:, 2 * P:3 * P], G)
            ada_accumulate(dve, 4, link)
            rope_parts(dve, ("nsa", 3), lambda tt: gemm_bank("nsa", 3, tt)[:, 0:P], G)
            for kv, (name, d) in enumerate((("kc", kc_next), ("vc", vc_next))):
                if kv == 0:
                    assert turn_reader("kc") == "dve" and turn_reader("ks") == "dve"
                    await_turn(dve, "kc")
                    dve.tensor_copy(d[0:DH, :, :], turn_bank("kc")[0:DH, :].rearrange("p (g t) -> p g t", g=G))
                    dve.tensor_copy(d[DH:P, :, 0:T - 1],
                                    turn_bank("kc")[DH:P, :].rearrange("p (g t) -> p g t", g=G)[:, :, 1:T]).then_inc(
                                        turn_read["dve"], 1)
                    read_turns("dve", "ks", lambda b: ksT.rearrange("p g t -> p (g t)"), [0])
                else:
                    await_turns_read(dve, "vc", [0])
            await_turns_read(dve, "kc", [0])
            for kv, (d, pe0) in enumerate(((kc_next, 56), (vc_next, 72))):
                for g in range(G):
                    src = d[:, g, 0:CMP_STRIDE * (NCMP + 1)].rearrange("p (n s) -> p s n", s=CMP_STRIDE)
                    for h in range(2):
                        o = blocks[:, kv, 8 * h:8 * h + 8, g, :]
                        pos = cols[:, 0, pe0 + 8 * h:pe0 + 8 * h + 8].rearrange("p (j o) -> p j o", o=1)
                        ins = dve.tensor_tensor(o, src[:, 0:CMP_STRIDE:2, h:h + NCMP],
                                                pos.broadcast_to([P, 8, NCMP]), ALU.add)
                ins.then_inc(blocks_ready, 1)
            ada_collect(dve, 4, link)
            ada_accumulate(dve, 5, link)
            rope_parts(dve, ("nsa", 0), lambda tt: gemm_bank("nsa", 0, tt)[:, :], 8)
            ada_collect(dve, 5, link)
            ada_accumulate(dve, 6, link)
            rope_parts(dve, ("nsa", 1), lambda tt: gemm_bank("nsa", 1, tt)[:, :], 8)
            ada_collect(dve, 6, link)
            ada_accumulate(dve, 7, link)
            await_turn(dve, "hid")
            hb = turn_bank("hid")[:, 0:4 * G * NCMP].rearrange("p (v c m) -> p v c m", v=2, c=2)
            dve.tensor_copy(hidT, hb)
            for c in range(2):
                src = hb[:, 1, c, :].rearrange("p (g n) -> p g n", g=G)
                for g in range(G):
                    ins = dve.tensor_copy(hid_rep[:, c, g, :, :], src[:, g:g + 1, :].broadcast_to([P, HG, NCMP]))
            ins.then_inc(turn_read["dve"], 1)
            dve.wait_ge(cmp_kv_done, 1)
            dve.tensor_copy(k_cmpT, bank[6][:, 256:256 + G * NCMP])
            for g in range(G):
                n = HG * NCMP
                ins = dve.tensor_tensor(v_blocks[0:n, g, :, :],
                                        bank[7][0:n, 256 + g * DH:256 + (g + 1) * DH].rearrange(
                                            "p (o d) -> p o d", o=1).broadcast_to([n, HG, DH]),
                                        C("head_block")[0:n, :].rearrange("p (h o) -> p h o", o=1).broadcast_to([n, HG, DH]),
                                        ALU.mult)
            ins.then_inc(cmp_kv_read, 1)
            ada_collect(dve, 7, link)
            ada_accumulate(dve, 8, link)
            ada_collect(dve, 8, link)
            read_turns("dve", "qp", lambda b: qpT[:, 2 * b:2 * b + 2, :].rearrange("p c t -> p (c t)"), range(4))
            read_turns("dve", "qr", lambda b: qrT[:, 2 * b:2 * b + 2, :].rearrange("p c t -> p (c t)"), range(4))
            ada_accumulate(dve, 9, link)
            ada_collect(dve, 9, link)
            dve.wait_ge(cmp_scored, 1)
            for tt in range(TT):
                mask = C("mask_cmp").rearrange("p (t n) -> p t n", t=TT)[:, tt:tt + 1, :]
                for odd in range(2):
                    half = bank[6 + odd][:, tt * HG * NCMP:(tt + 1) * HG * NCMP]
                    ins = dve.tensor_tensor(s_cmp[:, tt, odd:NH:2, :], half.rearrange("p (h n) -> p h n", n=NCMP),
                                            mask.broadcast_to([P, HG, NCMP]), ALU.add)
            link(ins)
            link(dve.tensor_reduce(m_cmp, s_cmp, AX, ALU.max))
            link(dve.tensor_scalar(m_cmp, m_cmp, FLOOR, None, ALU.max))
            for tt in range(TT):
                ins = dve.tensor_tensor(s_cmp[:, tt, :, :], s_cmp[:, tt, :, :],
                                        m_cmp[:, tt, :].rearrange("p (h o) -> p h o", o=1).broadcast_to([P, NH, NCMP]),
                                        ALU.subtract)
            ins.then_inc(cmp_shifted, 1)
            dve.wait_ge(cmp_exp, 1)
            link(dve.tensor_reduce(d_cmp, p_cmp, AX, ALU.add))
            link(dve.tensor_scalar(d_cmp, d_cmp, 1e-30, None, ALU.max))
            link(dve.reciprocal(d_cmp, d_cmp))
            dve.wait_ge(bank_free["act", 1], plan.free_count("act", 1, plan.outputs["nsa", 5][0]))
            link(dve.tensor_tensor(w_cmp, d_cmp, gates.rearrange("p t (h b) -> p t h b", b=3)[:, :, :, 0], ALU.mult))
            if turn_reader("pc") == "dve":
                n = HG * NCMP
                await_turn(dve, "pc")
                dve.tensor_copy(p_cmpT.rearrange("p t g q -> p (t g q)")[0:n, :],
                                turn_bank("pc")[0:n, :]).then_inc(turn_read["dve"], 1)
            for i in range(4):
                tt, g = i // 2, i % 2
                dve.wait_ge(cmp_pv_done, i + 1)
                dve.tensor_tensor(nsa_o[:, tt, HG * g:HG * g + HG, :],
                                  bank[6 + i % 2].rearrange("p (h d) -> p h d", d=DH),
                                  w_cmp[:, tt, HG * g:HG * g + HG].rearrange("p (h o) -> p h o", o=1).broadcast_to([P, HG, DH]),
                                  ALU.mult).then_inc(cmp_pv_read, 1)

            def weigh(grp):
                g, branch = grp // 2, 1 + grp % 2
                nsa_att.reciprocal(dve, grp, link)
                gt = gates.rearrange("p t (h b) -> p t h b", b=3)[:, :, HG * g:HG * g + HG, branch]
                link(dve.tensor_tensor(nsa_att.weight[:, grp, :, :], nsa_att.rden[:, grp, :, :], gt, ALU.mult))
                dve.wait_ge(nsa_att.pv_done, 8 * grp + 8)
                for tt in range(TT):
                    if grp:
                        dve.wait_ge(o_added, 2 * (grp - 1) + tt + 1)
                    ins = dve.tensor_tensor(o_part[:, tt, :, :],
                                            bank[4 + 2 * (grp % 2) + tt].rearrange("p (h d) -> p h d", d=DH),
                                            nsa_att.weight[:, grp, tt, :].rearrange("p (h o) -> p h o", o=1).broadcast_to(
                                                [P, HG, DH]), ALU.mult)
                ins.then_inc(nsa_att.pv_read, 1)

            nsa_att.dve(dve, link, weigh)
            for tt in range(TT):
                dve.wait_ge(o_added, 2 * 3 + tt + 1)
                o = nsa_o[:, tt, :, :].rearrange("p h d -> p (h d)")
                dve.tensor_tensor(o, o, z_act[:, tt, :], ALU.mult).then_inc(o_ready, 1)
            read_turns("dve", "nsa_o", lambda b: lhs[:, 2 * b:2 * b + 2, :].rearrange("p c t -> p (c t)"), range(4))

        def await_rotation(act, j, tt):
            act.wait_ge(bank_free["dve", tt], plan.free_count("dve", tt, plan.outputs["nsa", j][0]))

        def nsa_act(act):
            for tt in range(TT):
                await_output(act, "nsa", 2, tt)
                await_rotation(act, 2, tt)
                act.copy(v_slc[:, tt, :, :], gemm_bank("nsa", 2, tt)[:, 3 * P:4 * P].rearrange(
                    "p (g d) -> p g d", g=G)).then_inc(bank_free["act", tt], 1)
            for tt in range(TT):
                await_output(act, "nsa", 3, tt)
                await_rotation(act, 3, tt)
                act.copy(v_win[:, tt, :, :], gemm_bank("nsa", 3, tt)[:, P:2 * P].rearrange("p (g d) -> p g d", g=G))
                act.activation(z_act[:, tt, 0:256], gemm_bank("nsa", 3, tt)[:, 256:512],
                               ACT.Silu).then_inc(bank_free["act", tt], 1)
            await_turn(act, "vc")
            b = turn_bank("vc")
            act.copy(vc_next[0:DH, :, :], b[0:DH, :].rearrange("p (g t) -> p g t", g=G))
            act.copy(vc_next[DH:P, :, 0:T - 1],
                     b[DH:P, :].rearrange("p (g t) -> p g t", g=G)[:, :, 1:T]).then_inc(turn_read["act"], 1)
            read_turns("act", "kw", lambda b: kwT.rearrange("p g t -> p (g t)"), [0])
            for j in range(2):
                for tt in range(TT):
                    await_output(act, "nsa", j, tt)
                    await_rotation(act, j, tt)
                    act.copy(q_plain[:, tt, 8 * j:8 * j + 8, :], gemm_bank("nsa", j, tt).rearrange(
                        "p (h d) -> p h d", d=DH)).then_inc(bank_free["act", tt], 1)
            act.wait_ge(pe_units, plan.units[plan.outputs["cmp", 0][1][-1]][2] + 1)
            act.activation(hidden[0:G * NCMP, 0, :], bank[6][0:G * NCMP, 0:CMP_HIDDEN], ACT.Silu)
            act.wait_ge(pe_units, plan.units[plan.outputs["cmp", 1][1][-1]][2] + 1)
            act.activation(hidden[0:G * NCMP, 1, :], bank[7][0:G * NCMP, 0:CMP_HIDDEN],
                           ACT.Silu).then_inc(hidden_act, 1)
            for tt in range(TT):
                await_output(act, "nsa", 4, tt)
                act.activation(z_act[:, tt, 256:768], gemm_bank("nsa", 4, tt)[:, :],
                               ACT.Silu).then_inc(bank_free["act", tt], 1)
            read_turns("act", "qp", lambda b: qpT[:, 2 * b:2 * b + 2, :].rearrange("p c t -> p (c t)"), range(4))
            read_turns("act", "qr", lambda b: qrT[:, 2 * b:2 * b + 2, :].rearrange("p c t -> p (c t)"), range(4))
            for tt in range(TT):
                await_output(act, "nsa", 5, tt)
                act.activation(z_act[:, tt, 768:1024], gemm_bank("nsa", 5, tt)[:, 0:256], ACT.Silu)
            for tt in range(TT):
                act.activation(gates[:, tt, :], gemm_bank("nsa", 5, tt)[:, 256:304],
                               ACT.Sigmoid).then_inc(bank_free["act", tt], 1)
            act.wait_ge(cmp_shifted, 1)
            act.activation(p_cmp, s_cmp, ACT.Exp, scale=SCALE).then_inc(cmp_exp, 1)
            if turn_reader("pc") == "act":
                n = HG * NCMP
                await_turn(act, "pc")
                act.copy(p_cmpT.rearrange("p t g q -> p (t g q)")[0:n, :],
                         turn_bank("pc")[0:n, :]).then_inc(turn_read["act"], 1)
            nsa_att.act(act)
            read_turns("act", "nsa_o", lambda b: lhs[:, 2 * b:2 * b + 2, :].rearrange("p c t -> p (c t)"), range(4))

        def nsa_pool(pool):
            rope_add(pool, ("nsa", 2), lambda tt: [ks2[:, tt, :, 0, :], ks2[:, tt, :, 1, :]], G)
            rope_add(pool, ("nsa", 3), lambda tt: [kw2[:, tt, :, 0, :], kw2[:, tt, :, 1, :]], G)
            rope_add(pool, ("nsa", 0), lambda tt: [q_rope[:, tt, 0:8, :]], 8)
            rope_add(pool, ("nsa", 1), lambda tt: [q_rope[:, tt, 8:16, :]], 8)
            pool.wait_ge(cmp_pv_read, 4)
            for grp in range(4):
                pool.wait_ge(nsa_att.pv_read, grp + 1)
                for tt in range(TT):
                    o = nsa_o[:, tt, HG * (grp // 2):HG * (grp // 2) + HG, :]
                    if grp % 2:
                        pool.wait_ge(o_added, 2 * (grp - 1) + tt + 1)
                    pool.tensor_tensor(o, o, o_part[:, tt, :, :], ALU.add).then_inc(o_added, 1)
            residual_pool(pool, 0)

        def nsa_pe(pe):
            gemm(pe, "nsa", 2, from_lhs, 512)
            gemm(pe, "nsa", 3, from_lhs, 512)
            ada_sum(pe, 4)
            o2 = plan.outputs["nsa", 2][0]
            for tt in range(TT):
                pe.wait_ge(bank_free["dve", tt], plan.free_count("dve", tt, o2))
            for name, src in (("kc", kc2), ("vc", vc2), ("ks", ks2), ("kw", kw2)):
                if name == "ks":
                    pe.wait_ge(rope_done, 2)
                if name == "kw":
                    pe.wait_ge(rope_done, 4)
                turn(pe, name, 0, [(src[:, tt, g, :, :].rearrange("p a d -> p (a d)"), P, P, g * T + tt * P)
                                   for g in range(G) for tt in range(TT)])
            gemm(pe, "nsa", 0, from_lhs, 512)
            ada_sum(pe, 5)
            gemm(pe, "nsa", 1, from_lhs, 512)
            ada_sum(pe, 6)
            for kv in range(2):
                pe.wait_ge(blocks_ready, kv + 1)
                if kv == 0:
                    pe.wait_ge(mod_ready, 7)
                for u, unit in enumerate(plan.outputs["cmp", kv][1]):
                    await_unit(pe, unit)
                    for k in range(8):
                        j = 8 * u + k
                        mm = pe.matmul(bank[6 + kv][0:G * NCMP, 0:CMP_HIDDEN],
                                       blocks[:, kv, j, :, :].rearrange("p g n -> p (g n)"),
                                       ring[:, unit % RING, k * 256:(k + 1) * 256], start=(j == 0), stop=(j == 15))
                    mm.then_inc(pe_units, 1)
            gemm(pe, "nsa", 4, from_lhs, 512)
            n = G * NCMP
            pe.wait_ge(hidden_act, 1)
            turn(pe, "hid", 0, [(hidden[0:n, kv, c * P:(c + 1) * P], n, P, (2 * kv + c) * n)
                                for kv in range(2) for c in range(2)])
            pe.wait_ge(w2_in, 48)
            await_turns_read(pe, "hid", [0])
            for c in range(2):
                pe.matmul(bank[6][:, 256:256 + n], w2k[:, c, :, :].rearrange("p a d -> p (a d)"), hidT[:, 0, c, :],
                          start=(c == 0), stop=(c == 1))
            for g in range(G):
                for c in range(2):
                    mm = pe.matmul(bank[7][0:HG * NCMP, 256 + g * DH:256 + (g + 1) * DH],
                                   hid_rep[:, c, g, :, :].rearrange("p h n -> p (h n)"), w2v[:, c, :],
                                   start=(c == 0), stop=(c == 1))
            mm.then_inc(cmp_kv_done, 1)
            pe.wait_ge(cmp_kv_read, 1)
            ada_sum(pe, 7)
            ada_sum(pe, 8)
            o1 = plan.outputs["nsa", 1][0]
            for tt in range(TT):
                pe.wait_ge(bank_free["act", tt], plan.free_count("act", tt, o1))
            turn_tokens(pe, "qp", lambda tt, c: q_plain[:, tt, 2 * c:2 * c + 2, :].rearrange("p h d -> p (h d)"), range(4))
            pe.wait_ge(rope_done, 8)
            turn_tokens(pe, "qr", lambda tt, c: q_rope[:, tt, 2 * c:2 * c + 2, :].rearrange("p h d -> p (h d)"), range(4))
            gemm(pe, "nsa", 5, from_lhs, 304)
            ada_sum(pe, 9)
            await_turns_read(pe, "qp", range(4))
            pe.wait_ge(mod_ready, 10)
            for tt in range(TT):
                for h in range(NH):
                    g = h // HG
                    at = (tt * HG + h // 2) * NCMP
                    mm = pe.matmul(bank[6 + h % 2][:, at:at + NCMP],
                                   qpT[head_rows(h), h // 2, tt * P:(tt + 1) * P],
                                   k_cmpT[head_rows(h), g * NCMP:(g + 1) * NCMP], start=True, stop=True)
            mm.then_inc(cmp_scored, 1)
            pe.wait_ge(cmp_exp, 1)
            turn(pe, "pc", 0, [(p_cmp[:, tt, HG * g:HG * g + HG, :].rearrange("p h n -> p (h n)"), P, HG * NCMP,
                                (2 * tt + g) * P) for tt in range(TT) for g in range(G)])
            await_turns_read(pe, "pc", [0])
            for i in range(4):
                tt, g = i // 2, i % 2
                if i >= 2:
                    pe.wait_ge(cmp_pv_read, i - 1)
                pe.matmul(bank[6 + i % 2][:, :], p_cmpT[0:HG * NCMP, tt, g, :],
                          v_blocks[0:HG * NCMP, g, :, :].rearrange("p h d -> p (h d)"),
                          start=True, stop=True).then_inc(cmp_pv_done, 1)
            await_turns_read(pe, "qr", range(4))
            o5 = plan.outputs["nsa", 5][0]
            for o in (o5 - 1, o5):
                for tt in range(TT):
                    pe.wait_ge(bank_free["act", tt], plan.free_count("act", tt, o))
            pe.wait_ge(cmp_pv_read, 4)
            nsa_att.pe(pe)
            pe.wait_ge(o_ready, 2)
            turn_tokens(pe, "nsa_o", lambda tt, c: nsa_o[:, tt, 2 * c:2 * c + 2, :].rearrange("p h d -> p (h d)"), range(4))
            await_turns_read(pe, "nsa_o", range(4))
            gemm(pe, "nsa_out", 0, from_lhs, 512)
            ada_sum(pe, 10)
            gemm(pe, "nsa_out", 1, from_lhs, 512)
            ada_sum(pe, 11)

        dil = Space(nsa_rope_end)
        dil_q, dil_k, dil_v = [dil.take(TT, NH, DH) for _ in range(3)]
        dil_z = dil.take(TT, D)
        dil_qT, dil_kT = dil.take(KC, T), dil.take(KC, T)
        dil_o = dil.take(TT, NH, DH)
        lse, lse_e = dil.take(TT, NH), dil.take(TT, NH)
        lse_top, lse_sum, alpha_den = [dil.take(TT) for _ in range(3)]
        alpha = dil.take(TT, 3)

        def dil_mask(h):
            kind = [m for a, b, m in DIL_MASK if a <= h < b][0]
            return C(f"mask_{kind}")

        def dil_item(h):
            return (lambda tt: dil_qT[head_rows(h), h // 2, tt * P:(tt + 1) * P],
                    lambda: dil_kT[head_rows(h), h // 2, :], dil_mask(h), lambda kt: dil_v[:, kt, h, :])

        dil_att = Attention("dil_att", Space(0), [dil_item(h) for h in range(NH)])
        lse_ln, lse_shifted, lse_exp = sem("lse_ln"), sem("lse_shifted"), sem("lse_exp")
        log_den = dil.take(NH, TT)

        def dil_dve(dve, link):
            for j in range(4):
                rope_parts(dve, ("dil", j), lambda tt: gemm_bank("dil", j, tt)[:, :], 8)
                if j:
                    ada_collect(dve, 11 + j, link)
                ada_accumulate(dve, 12 + j, link)
            ada_collect(dve, 15, link)
            ada_accumulate(dve, 16, link)
            read_turns("dve", "dil_q", lambda b: dil_qT[:, 2 * b:2 * b + 2, :].rearrange("p c t -> p (c t)"), range(4))
            ada_collect(dve, 16, link)
            ada_accumulate(dve, 17, link)
            read_turns("dve", "dil_k", lambda b: dil_kT[:, 2 * b:2 * b + 2, :].rearrange("p c t -> p (c t)"), range(4))
            ada_collect(dve, 17, link)

            def weigh(grp):
                dil_att.reciprocal(dve, grp, link)
                dve.wait_ge(dil_att.pv_done, 8 * grp + 8)
                for tt in range(TT):
                    ins = dve.tensor_tensor(dil_o[:, tt, 8 * grp:8 * grp + 8, :],
                                            bank[4 + 2 * (grp % 2) + tt].rearrange("p (h d) -> p h d", d=DH),
                                            dil_att.rden[:, grp, tt, :].rearrange("p (h o) -> p h o", o=1).broadcast_to(
                                                [P, HG, DH]), ALU.mult)
                ins.then_inc(dil_att.pv_read, 1)

            dil_att.dve(dve, link, weigh)
            dve.wait_ge(lse_ln, 1)
            link(dve.tensor_tensor(lse, log_den.rearrange("p h t -> p t h"),
                                   dil_att.bias.rearrange("p h t -> p t h"), ALU.subtract))
            link(dve.tensor_reduce(lse_top, lse, AX, ALU.max))
            dve.tensor_tensor(lse, lse, lse_top.rearrange("p (t o) -> p t o", o=1).broadcast_to([P, TT, NH]),
                              ALU.subtract).then_inc(lse_shifted, 1)
            dve.wait_ge(lse_exp, 1)
            for i, (a, b, _) in enumerate(DIL_MASK):
                ins = dve.tensor_reduce(alpha[:, :, i:i + 1], lse_e[:, :, a:b], AX, ALU.add)
            link(ins)
            for i, (a, b, _) in enumerate(DIL_MASK):
                ins = dve.tensor_scalar(alpha[:, :, i:i + 1], alpha[:, :, i:i + 1], 1.0 / (b - a), None, ALU.mult)
            link(ins)
            link(dve.tensor_reduce(lse_sum, alpha, AX, ALU.add))
            link(dve.reciprocal(alpha_den, lse_sum))
            link(dve.tensor_scalar(alpha_den, alpha_den, float(len(DIL_MASK)), None, ALU.mult))
            link(dve.tensor_tensor(alpha, alpha, alpha_den.rearrange("p (t o) -> p t o", o=1).broadcast_to([P, TT, 3]),
                                   ALU.mult))
            for tt in range(TT):
                dve.wait_ge(dil_att.pv_read, 2)
                for i, (a, b, _) in enumerate(DIL_MASK):
                    o = dil_o[:, tt, a:b, :].rearrange("p h d -> p (h d)")
                    ins = dve.scalar_tensor_tensor(o, o, alpha[:, tt, i:i + 1], dil_z[:, tt, a * DH:b * DH],
                                                   ALU.mult, ALU.mult)
                ins.then_inc(o_ready, 1)
            read_turns("dve", "dil_o", lambda b: lhs[:, 2 * b:2 * b + 2, :].rearrange("p c t -> p (c t)"), range(4))

        def dil_act(act):
            for j in (4, 5, 6, 7):
                for tt in range(TT):
                    await_output(act, "dil", j, tt)
                    if j < 6:
                        act.copy(dil_v[:, tt, 8 * (j - 4):8 * (j - 4) + 8, :], gemm_bank("dil", j, tt).rearrange(
                            "p (h d) -> p h d", d=DH)).then_inc(bank_free["act", tt], 1)
                    else:
                        act.activation(dil_z[:, tt, 512 * (j - 6):512 * (j - 6) + 512], gemm_bank("dil", j, tt)[:, :],
                                       ACT.Silu).then_inc(bank_free["act", tt], 1)
                if j == 4:
                    read_turns("act", "dil_q", lambda b: dil_qT[:, 2 * b:2 * b + 2, :].rearrange("p c t -> p (c t)"), range(4))
                if j == 5:
                    read_turns("act", "dil_k", lambda b: dil_kT[:, 2 * b:2 * b + 2, :].rearrange("p c t -> p (c t)"), range(4))
            dil_att.act(act)
            act.wait_ge(dil_att.exp_done, NH)
            act.activation(log_den, dil_att.den, ACT.Ln).then_inc(lse_ln, 1)
            act.wait_ge(lse_shifted, 1)
            act.activation(lse_e, lse, ACT.Exp).then_inc(lse_exp, 1)
            read_turns("act", "dil_o", lambda b: lhs[:, 2 * b:2 * b + 2, :].rearrange("p c t -> p (c t)"), range(4))

        def dil_pool(pool):
            for j, d in enumerate((dil_q, dil_q, dil_k, dil_k)):
                rope_add(pool, ("dil", j), lambda tt: [d[:, tt, 8 * (j % 2):8 * (j % 2) + 8, :]], 8)
            residual_pool(pool, 1)

        def dil_pe(pe):
            for j in range(8):
                gemm(pe, "dil", j, from_lhs, 512)
                if j < 6:
                    ada_sum(pe, 12 + j)
                if j == 4:
                    pe.wait_ge(rope_done, 12)
                    turn_tokens(pe, "dil_q", lambda tt, c: dil_q[:, tt, 2 * c:2 * c + 2, :].rearrange("p h d -> p (h d)"), range(4))
                if j == 5:
                    pe.wait_ge(rope_done, 16)
                    turn_tokens(pe, "dil_k", lambda tt, c: dil_k[:, tt, 2 * c:2 * c + 2, :].rearrange("p h d -> p (h d)"), range(4))
            await_turns_read(pe, "dil_k", range(4))
            pe.wait_ge(mod_ready, 18)
            o7 = plan.outputs["dil", 7][0]
            for tt in range(TT):
                pe.wait_ge(bank_free["act", tt], plan.free_count("act", tt, o7))
            dil_att.pe(pe)
            pe.wait_ge(o_ready, 4)
            turn_tokens(pe, "dil_o", lambda tt, c: dil_o[:, tt, 2 * c:2 * c + 2, :].rearrange("p h d -> p (h d)"), range(4))
            await_turns_read(pe, "dil_o", range(4))
            for j in range(2):
                gemm(pe, "dil_out", j, from_lhs, 512)


        silu_done, h_ready = sem("silu_done"), sem("h_ready")
        ffn = Space(0)
        up_a, up_h = ffn.take(2, TT, 256), ffn.take(2, TT, 256)
        upT = ffn.take(FC, T)
        FFN_AT = {"ffn1": 0, "ffn2": 1}

        def ffn_dve(dve, name, layer, link, adas=()):
            base = 2 * FFN_OUTS * FFN_AT[name]
            for j in range(FFN_OUTS + 1):
                if j < FFN_OUTS:
                    for tt in range(TT):
                        dve.wait_ge(silu_done, base + 2 * j + tt + 1)
                        if j >= 2:
                            await_turn(dve, name + "_h", j - 2)
                        dve.tensor_tensor(up_h[:, j % 2, tt, :], up_a[:, j % 2, tt, :],
                                          gemm_bank(name + "_up", j, tt)[:, 256:512],
                                          ALU.mult).then_inc(bank_free["dve", tt], 1)
                if j >= 1:
                    read_turns("dve", name + "_h", lambda b: upT[:, 2 * b:2 * b + 2, :].rearrange("p c t -> p (c t)"), [j - 1])
                if 0 <= j - 1 < len(adas):
                    ada_collect(dve, adas[j - 1], link)
                if j < len(adas):
                    ada_accumulate(dve, adas[j], link)
            residual_dve(dve, layer, name + "_down", link)

        def ffn_act(act, name):
            for j in range(FFN_OUTS + 1):
                if j < FFN_OUTS:
                    for tt in range(TT):
                        await_output(act, name + "_up", j, tt)
                        act.activation(up_a[:, j % 2, tt, :], gemm_bank(name + "_up", j, tt)[:, 0:256],
                                       ACT.Silu).then_inc(silu_done, 1)
                if j >= 1:
                    read_turns("act", name + "_h", lambda b: upT[:, 2 * b:2 * b + 2, :].rearrange("p c t -> p (c t)"), [j - 1])

        def ffn_pe(pe, name, adas=()):
            for j in range(FFN_OUTS + 1):
                if j < FFN_OUTS:
                    gemm(pe, name + "_up", j, from_lhs, 512)
                if 0 <= j - 1 < len(adas):
                    ada_sum(pe, adas[j - 1])
                if j >= 1:
                    o = plan.outputs[name + "_up", j - 1][0]
                    for tt in range(TT):
                        pe.wait_ge(bank_free["dve", tt], plan.free_count("dve", tt, o))
                    turn(pe, name + "_h", j - 1, [(up_h[:, (j - 1) % 2, tt, h * P:(h + 1) * P], P, P, h * T + tt * P)
                                                  for h in range(2) for tt in range(TT)])
            await_turns_read(pe, name + "_h", range(FFN_OUTS))
            for j in range(2):
                gemm(pe, name + "_down", j, lambda k, tt: upT[:, k, tt * P:(tt + 1) * P], 512, kc_total=FC)

        mix = Space(0)
        qkT = mix.take(2 * DN_HEADS, T)
        z_gain = mix.take(TT, D)
        sig = mix.take(TT, 2, D)
        y_aT = mix.take(CONV_A // P, T)
        beta = mix.take(TT, 2 * DN_HEADS)
        beta_k = mix.take(TT, 2 * DN_HEADS)
        g_log = mix.take(TT, 2 * DN_HEADS)
        sp_x, sp_abs, sp_e, sp_u, sp_l = [mix.take(TT, 2 * DN_HEADS) for _ in range(5)]
        head_row = mix.take(4 * DN_HEADS)
        a_rate = mix.take(2 * DN_HEADS)
        dn_gain = mix.take(P)
        g_in = mix.take(TT, 2 * DN_HEADS)
        g_cum = mix.take(TT, 2 * DN_HEADS)
        g_off = mix.take(2 * DN_HEADS)
        g_rows = mix.take(T)
        qk_sum = mix.take(2, TT, DN_HEADS)
        k_len = mix.take(TT, DN_HEADS)
        q_scale = mix.take(TT, DN_HEADS)
        y_ss, y_ms, y_r = [mix.take(DN_HEADS, TT) for _ in range(3)]
        early = Space(mix.at)
        tok = early.take(2, TT, 512)
        padded = early.take(2, 2, T + 4)
        conv_acc = early.take(2, 2, T)
        vT = early.take(DN_HEADS, T)
        sq = early.take(2, 2, T)
        ca_b, ca_c = early.take(TT, CONV_A), early.take(TT, CONV_A)
        pad_a = early.take(CONV_A // P, T + 2)
        acc_a = early.take(CONV_A // P, T)
        v_hat = xn.rearrange("p t (h d) -> p t h d", h=DN_HEADS)
        y_b = qkT[:, 0:DN_HEADS, :].rearrange("p h (t d) -> p t h d", t=TT)

        pads_ready = sem("pads_ready")
        rows_in = sem("rows_in")
        rate_ready, z_ready, z_gained = sem("rate_ready"), sem("z_ready"), sem("z_gained")
        conv_done, qkv_ready = sem("conv_done"), sem("qkv_ready")
        sq_ready, qk_summed_pair, qk_sum_read = sem("sq_ready"), sem("qk_summed_pair"), sem("qk_sum_read")
        k_len_ready = sem("k_len_ready")
        sp_ready, sp_exp, sp_sum, sp_ln = sem("sp_ready"), sem("sp_exp"), sem("sp_sum"), sem("sp_ln")
        g_ready, g_summed, g_cum_ready = sem("g_ready"), sem("g_summed"), sem("g_cum_ready")
        y_a_ready, v_ready = sem("y_a_ready"), sem("v_ready")
        a_merged, b_gated, merged_ready = sem("a_merged"), sem("b_gated"), sem("merged_ready")

        def padded_out(b):
            return padded[:, b % 2, :, 2:T + 2]

        def mix_conv(dve, b, link):
            p = padded[:, b % 2, :, :]
            await_turns_read(dve, "qkv", [b])
            if b >= 2:
                dve.wait_ge(qkv_ready, b - 1)
            for tap in range(5):
                for h in range(2):
                    c = 2 * b + h
                    w = cols[:, 1, tap * (QKV // P) + c:tap * (QKV // P) + c + 1]
                    a, src = conv_acc[:, b % 2, h, :], p[:, h, tap:tap + T]
                    if tap == 0:
                        ins = dve.tensor_scalar(a, src, w, None, ALU.mult)
                    else:
                        ins = dve.scalar_tensor_tensor(a, src, w, a, ALU.mult, ALU.add)
                if tap < 4:
                    link(ins)
            ins.then_inc(conv_done, 1)

        def qkv_silu(act, b):
            act.wait_ge(conv_done, b + 1)
            dst = qkT[:, 2 * b:2 * b + 2, :] if b < 8 else vT[:, 2 * b - 16:2 * b - 14, :]
            act.activation(dst, conv_acc[:, b % 2, :, :], ACT.Silu).then_inc(qkv_ready, 1)

        def copy_padded(who, b):
            if turn_reader("qkv", b) == who:
                eng = ENG[who]
                await_turn(eng, "qkv", b)
                if b >= 2:
                    eng.wait_ge(conv_done, b - 1)
                copy(eng, padded_out(b), turn_bank("qkv", b).rearrange("p (h t) -> p h t", h=2)).then_inc(turn_read[who], 1)

        def mix_dve(dve, link):
            dve.memset(padded, 0.0)
            dve.memset(pad_a, 0.0).then_inc(pads_ready, 1)
            dve.wait_ge(pads_ready, 1)
            dve.wait_ge(rate_ready, 1)
            for b in range(12):
                copy_padded("dve", b)
                mix_conv(dve, b, link)
                if b == 9:
                    for tt in range(TT):
                        await_output(dve, "ba", 0, tt)
                        dve.tensor_tensor(sp_x[:, tt, :], gemm_bank("ba", 0, tt)[:, 16:32], head_row[:, 16:32],
                                          ALU.add).then_inc(bank_free["dve", tt], 1)
                    for tt in range(TT):
                        dve.wait_ge(bank_free["dve", tt], plan.free_count("dve", tt, plan.outputs["ba", 0][0]))
                    dve.scalar_tensor_tensor(sp_abs, sp_x, -1.0, sp_x, ALU.mult, ALU.max).then_inc(sp_ready, 1)
            dve.wait_ge(sp_exp, 1)
            dve.tensor_scalar(sp_u, sp_e, 1.0, None, ALU.add).then_inc(sp_sum, 1)
            dve.wait_ge(sp_sum, 1)
            link(dve.tensor_scalar(sp_abs, sp_u, -1.0, None, ALU.add))
            link(dve.tensor_tensor(sp_e, sp_e, sp_abs, ALU.subtract))
            dve.wait_ge(sp_ln, 1)
            link(dve.reciprocal(sp_u, sp_u))
            link(dve.tensor_tensor(sp_e, sp_e, sp_u, ALU.mult))
            link(dve.tensor_tensor(sp_l, sp_l, sp_e, ALU.add))
            link(dve.scalar_tensor_tensor(sp_l, sp_x, 0.0, sp_l, ALU.max, ALU.add))
            for tt in range(TT):
                ins = dve.scalar_tensor_tensor(g_log[:, tt, :], sp_l[:, tt, :], -1.0, a_rate, ALU.mult, ALU.mult)
            ins.then_inc(g_ready, 1)
            for tt in range(TT):
                await_output(dve, "ca", 2, tt)
                dve.wait_ge(bank_free["act", tt], plan.free_count("act", tt, plan.outputs["ca", 1][0]))
                dve.tensor_tensor(ca_c[:, tt, :], ca_c[:, tt, :], gemm_bank("ca", 2, tt)[:, :],
                                  ALU.mult).then_inc(bank_free["dve", tt], 1)
            dve.wait_ge(qk_summed_pair, 8)
            dve.tensor_scalar(qk_sum.rearrange("p a t h -> p (a t h)"), bank[7][:, 0:32], EPS, None,
                              ALU.add).then_inc(qk_sum_read, 1)
            dve.wait_ge(g_summed, 1)
            dve.tensor_copy(g_cum.rearrange("p t c -> p (t c)"), bank[6][:, 0:32])
            dve.tensor_scalar(g_in.rearrange("p t c -> p (t c)"), bank[6][:, 0:32], -1.0, None, ALU.mult)
            dve.tensor_copy(g_off, bank[6][:, 32:48]).then_inc(g_cum_ready, 1)
            dve.wait_ge(qk_sum_read, 1)
            link(dve.reciprocal(beta_k[:, :, 0:8], qk_sum[:, 1, :, :]))
            o = plan.outputs["ba", 0][0]
            for tt in range(TT):
                dve.wait_ge(bank_free["act", tt], plan.free_count("act", tt, o))
            link(dve.tensor_tensor(beta_k[:, :, 8:16], beta_k[:, :, 0:8], beta[:, :, 8:16], ALU.mult))
            link(dve.tensor_tensor(beta_k[:, :, 0:8], beta_k[:, :, 0:8], beta[:, :, 0:8], ALU.mult))
            for b in range(2):
                if turn_reader("prod", b) == "dve":
                    await_turn(dve, "prod", b)
                    dve.tensor_copy(pad_a[:, 2 * b:2 * b + 2, 1:T + 1],
                                    turn_bank("prod", b).rearrange("p (h t) -> p h t", h=2)).then_inc(turn_read["dve"], 1)
            await_turns_read(dve, "prod", range(2))
            for tap in range(3):
                for c in range(4):
                    w = cols[:, 0, 88 + 4 * tap + c:89 + 4 * tap + c]
                    a, src = acc_a[:, c, :], pad_a[:, c, tap:tap + T]
                    if tap == 0:
                        ins = dve.tensor_scalar(a, src, w, None, ALU.mult)
                    else:
                        ins = dve.scalar_tensor_tensor(a, src, w, a, ALU.mult, ALU.add)
                link(ins)
            for b in range(2):
                await_turn(dve, "cab", b)
                if turn_reader("cab", b) == "act":
                    await_turns_read(dve, "cab", [b])
                    src = y_aT[:, 2 * b:2 * b + 2, :]
                else:
                    src = turn_bank("cab", b).rearrange("p (h t) -> p h t", h=2)
                ins = dve.tensor_tensor(y_aT[:, 2 * b:2 * b + 2, :], acc_a[:, 2 * b:2 * b + 2, :], src, ALU.mult)
                if turn_reader("cab", b) == "dve":
                    ins.then_inc(turn_read["dve"], 1)
                else:
                    ins.then_inc(y_a_ready, 1)
            ada_accumulate(dve, 24, link)
            dve.wait_ge(k_len_ready, 2)
            for b in range(4):
                tt, hh = b // 2, 4 * (b % 2)
                await_turn(dve, "v", b)
                if turn_reader("v", b) == "act":
                    await_turns_read(dve, "v", [b])
                    src = v_hat[:, tt, hh:hh + 4, :]
                else:
                    src = turn_bank("v", b).rearrange("p (h d) -> p h d", h=4)
                ins = dve.tensor_tensor(v_hat[:, tt, hh:hh + 4, :], src,
                                        k_len[:, tt, hh:hh + 4].rearrange("p (h o) -> p h o", o=1).broadcast_to([P, 4, DN_D]),
                                        ALU.mult)
                if turn_reader("v", b) == "dve":
                    ins.then_inc(turn_read["dve"], 1)
                else:
                    link.mark(ins)
            read_rows("dve")
            for n in range(24, 30):
                ada_collect(dve, n, link)
                if n < 29:
                    ada_accumulate(dve, n + 1, link)
            for j in range(2):
                for tt in range(TT):
                    await_output(dve, "a_out", j, tt)
                    s = sig[:, tt, 0, 512 * j:512 * (j + 1)]
                    dve.tensor_tensor(s, s, gemm_bank("a_out", j, tt)[:, :], ALU.mult).then_inc(bank_free["dve", tt], 1)
            delta_dve(dve, link)
            read_turns("dve", "y_b", lambda b: lhs[:, 2 * b:2 * b + 2, :].rearrange("p c t -> p (c t)"), range(4))
            for j in range(2):
                for tt in range(TT):
                    await_output(dve, "b_out", j, tt)
                    s = sig[:, tt, 1, 512 * j:512 * (j + 1)]
                    dve.tensor_tensor(s, s, gemm_bank("b_out", j, tt)[:, :], ALU.mult).then_inc(bank_free["dve", tt], 1)
            read_turns("dve", "merged", lambda b: lhs[:, 2 * b:2 * b + 2, :].rearrange("p c t -> p (c t)"), range(4))
            residual_dve(dve, 3, "mix_out", link)

        def read_rows(who):
            if turn_reader("grow") == who:
                await_turn(ENG[who], "grow")
                copy(ENG[who], g_rows[0:16, :], turn_bank("grow")[0:16, 0:T]).then_inc(turn_read[who], 1)

        def mix_act(act):
            act.wait_ge(rows_in, 16 * 5)
            act.activation(a_rate, head_row[:, 0:16], ACT.Exp).then_inc(rate_ready, 1)
            act.wait_ge(pads_ready, 1)
            for b in range(12):
                if b % 2 == 0:
                    for tt in range(TT):
                        await_output(act, "qkv", b // 2, tt)
                        if b >= 4:
                            await_turn(act, "qkv", b - 3)
                        act.copy(tok[:, (b // 2) % 2, tt, :], gemm_bank("qkv", b // 2, tt)[:, :]).then_inc(
                            bank_free["act", tt], 1)
                if b >= 2:
                    copy_or_silu_act(act, b - 2)
            copy_or_silu_act(act, 10)
            copy_or_silu_act(act, 11)
            o = plan.outputs["ba", 0][0]
            for tt in range(TT):
                act.wait_ge(bank_free["dve", tt], plan.free_count("dve", tt, o))
                act.activation(beta[:, tt, :], gemm_bank("ba", 0, tt)[:, 0:16], ACT.Sigmoid)
                act.activation(sig[:, tt, 0, 0:GATE_W - 32], gemm_bank("ba", 0, tt)[:, 32:GATE_W],
                               ACT.Sigmoid).then_inc(bank_free["act", tt], 1)
            for tt in range(TT):
                await_output(act, "ca", 0, tt)
                act.copy(ca_b[:, tt, :], gemm_bank("ca", 0, tt)[:, :]).then_inc(bank_free["act", tt], 1)
            act.wait_ge(sp_ready, 1)
            act.activation(sp_e, sp_abs, ACT.Exp, scale=-1.0).then_inc(sp_exp, 1)
            act.wait_ge(sp_sum, 1)
            act.activation(sp_l, sp_u, ACT.Ln).then_inc(sp_ln, 1)
            for tt in range(TT):
                await_output(act, "ca", 1, tt)
                act.copy(ca_c[:, tt, :], gemm_bank("ca", 1, tt)[:, :]).then_inc(bank_free["act", tt], 1)
            for p in range(8):
                act.wait_ge(qkv_ready, 8)
                if p >= 2:
                    act.wait_ge(qk_summed_pair, p - 1)
                act.activation(sq[:, p % 2, :, :], qkT[:, 2 * p:2 * p + 2, :], ACT.Square).then_inc(sq_ready, 1)
            for b in range(2):
                if turn_reader("prod", b) == "act":
                    await_turn(act, "prod", b)
                    act.copy(pad_a[:, 2 * b:2 * b + 2, 1:T + 1],
                             turn_bank("prod", b).rearrange("p (h t) -> p h t", h=2)).then_inc(turn_read["act"], 1)
            read_turns("act", "cab", lambda b: y_aT[:, 2 * b:2 * b + 2, :].rearrange("p h t -> p (h t)"), range(2))
            for tt in range(TT):
                await_output(act, "z", 0, tt)
                act.activation(z_gain[:, tt, 0:512], gemm_bank("z", 0, tt)[:, :], ACT.Silu).then_inc(bank_free["act", tt], 1)
            read_turns("act", "v", lambda b: v_hat[:, b // 2, 4 * (b % 2):4 * (b % 2) + 4, :].rearrange("p h d -> p (h d)"), range(4))
            read_rows("act")
            for tt in range(TT):
                await_output(act, "z", 1, tt)
                act.activation(z_gain[:, tt, 512:1024], gemm_bank("z", 1, tt)[:, :], ACT.Silu).then_inc(bank_free["act", tt], 1)
            sig_all = sig.rearrange("p t g d -> p t (g d)")
            for j in range(4):
                at = GATE_W * (j + 1) - 32
                for tt in range(TT):
                    await_output(act, "gate", j, tt)
                    act.activation(sig_all[:, tt, at:at + GATE_W], gemm_bank("gate", j, tt)[:, 0:GATE_W],
                                   ACT.Sigmoid).then_inc(bank_free["act", tt], 1)
            delta_act(act)
            read_turns("act", "y_b", lambda b: lhs[:, 2 * b:2 * b + 2, :].rearrange("p c t -> p (c t)"), range(4))
            read_turns("act", "merged", lambda b: lhs[:, 2 * b:2 * b + 2, :].rearrange("p c t -> p (c t)"), range(4))

        def copy_or_silu_act(act, b):
            copy_padded("act", b)
            qkv_silu(act, b)

        def mix_pool(pool):
            pool.wait_ge(qk_sum_read, 1)
            n = TT * DN_HEADS
            qs = q_scale.rearrange("p t h -> p (t h)")
            pool.tensor_scalar(qs, qk_sum[:, 0, :, :].rearrange("p t h -> p (t h)"), float(DN_D), None,
                               ALU.mult).then_inc(k_len_ready, 1)
            pool.tensor_tensor(k_len.rearrange("p t h -> p (t h)"), qk_sum[:, 1, :, :].rearrange("p t h -> p (t h)"),
                               C("half").broadcast_to([P, n]), ALU.pow).then_inc(k_len_ready, 1)
            pool.wait_ge(k_len_ready, 2)
            pool.tensor_tensor(qs, qs, C("minus_half").broadcast_to([P, n]), ALU.pow).then_inc(k_len_ready, 1)
            o = plan.outputs["z", 1][0]
            for tt in range(TT):
                pool.wait_ge(bank_free["act", tt], plan.free_count("act", tt, o))
                z = z_gain[:, tt, :].rearrange("p (h d) -> p h d", h=DN_HEADS)
                pool.tensor_tensor(z, z, dn_gain.rearrange("p (o d) -> p o d", o=1).broadcast_to([P, DN_HEADS, DN_D]),
                                   ALU.mult).then_inc(z_gained, 1)
            delta_pool(pool)
            for j in range(2):
                for tt in range(TT):
                    o = plan.outputs["b_out", j][0]
                    pool.wait_ge(bank_free["dve", tt], plan.free_count("dve", tt, o))
                    a = sig[:, tt, 0, 512 * j:512 * (j + 1)]
                    pool.tensor_tensor(a, a, sig[:, tt, 1, 512 * j:512 * (j + 1)], ALU.add).then_inc(merged_ready, 1)
            residual_pool(pool, 3)

        def mix_pe(pe):
            def qkv_turns(j):
                o = plan.outputs["qkv", j][0]
                for tt in range(TT):
                    pe.wait_ge(bank_free["act", tt], plan.free_count("act", tt, o))
                for b in (2 * j, 2 * j + 1):
                    turn(pe, "qkv", b, [(tok[:, j % 2, tt, (2 * (b % 2) + h) * P:(2 * (b % 2) + h + 1) * P], P, P,
                                         h * T + tt * P) for h in range(2) for tt in range(TT)])
            for j in range(6):
                gemm(pe, "qkv", j, from_lhs, 512)
                if j:
                    qkv_turns(j - 1)
            gemm(pe, "ba", 0, from_lhs, GATE_W)
            qkv_turns(5)
            for j in range(3):
                gemm(pe, "ca", j, from_lhs, 512)
            pe.wait_ge(g_ready, 1)
            pe.wait_ge(mod_ready, 24)
            for tt in range(TT):
                for d, m in ((0, "cum_fwd"), (1, "cum_bwd")):
                    pe.matmul(bank[6][:, tt * 16 + d * 8:tt * 16 + d * 8 + 8], C(m), g_log[:, tt, d * 8:d * 8 + 8],
                              start=True, stop=True)
            pe.matmul(bank[6][:, 32:40], C("after"), g_log[:, 0, 0:8], start=True, stop=True)
            pe.matmul(bank[6][:, 40:48], C("before"), g_log[:, 1, 8:16], start=True, stop=True).then_inc(g_summed, 1)
            for p in range(8):
                pe.wait_ge(sq_ready, p + 1)
                for h in range(2):
                    c = 2 * p + h
                    for tt in range(TT):
                        col = (c // 8) * 16 + tt * 8 + c % 8
                        mm = pe.matmul(bank[7][:, col:col + 1], sq[:, p % 2, h, tt * P:(tt + 1) * P], ones[:, 0:1],
                                       start=True, stop=True)
                mm.then_inc(qk_summed_pair, 1)
            o = plan.outputs["ca", 2][0]
            for tt in range(TT):
                pe.wait_ge(bank_free["dve", tt], plan.free_count("dve", tt, o))
            for b in range(2):
                turn(pe, "prod", b, [(ca_c[:, tt, (2 * b + h) * P:(2 * b + h + 1) * P], P, P, h * T + tt * P)
                                     for h in range(2) for tt in range(TT)])
            for b in range(2):
                turn(pe, "cab", b, [(ca_b[:, tt, (2 * b + h) * P:(2 * b + h + 1) * P], P, P, h * T + tt * P)
                                    for h in range(2) for tt in range(TT)])
            gemm(pe, "z", 0, from_lhs, 512)
            pe.wait_ge(qkv_ready, 12)
            for b in range(4):
                tt, hh = b // 2, 4 * (b % 2)
                turn(pe, "v", b, [(vT[:, hh + h, tt * P:(tt + 1) * P], P, P, h * P) for h in range(4)])
            pe.wait_ge(g_cum_ready, 1)
            turn(pe, "grow", 0, [(g_cum[:, tt, :], P, 16, tt * P) for tt in range(TT)])
            gemm(pe, "z", 1, from_lhs, 512)
            ada_sum(pe, 24)
            for j in range(4):
                gemm(pe, "gate", j, from_lhs, GATE_W)
                ada_sum(pe, 25 + j)
            ada_sum(pe, 29)
            await_turns_read(pe, "cab", range(2))
            pe.wait_ge(y_a_ready, 1)
            for j in range(2):
                gemm(pe, "a_out", j, lambda k, tt: y_aT[:, k, tt * P:(tt + 1) * P], 512, kc_total=CONV_A // P)
            delta_pe(pe)
            turn_tokens(pe, "y_b", lambda tt, c: y_b[:, tt, c, :], range(4))
            await_turns_read(pe, "y_b", range(4))
            for j in range(2):
                gemm(pe, "b_out", j, from_lhs, 512)
            for b in range(4):
                pe.wait_ge(merged_ready, 2 if b < 2 else 4)
                turn_tokens(pe, "merged", lambda tt, c: sig[:, tt, 0, c * P:(c + 1) * P], [b])
            await_turns_read(pe, "merged", range(4))
            for j in range(2):
                gemm(pe, "mix_out", j, from_lhs, 512)

        LV = N_LEVELS - 1
        FAR = (2, 2)

        class Lane:
            def __init__(self, n, space):
                self.bank = bank[4 * n:4 * n + 4]
                self.shifted = space.take(2, TT, P)
                self.decay = space.take(2, 3, P)
                self.mix = space.take(2, 3, P)
                self.far = space.take(2, P)
                self.coupling = space.take(2 * TT, P)
                self.level = space.take(2, 2 * TT, P)
                self.X = space.take(2 * TT, P)
                self.Y = space.take(2 * TT, P)
                self.LX = space.take(2 * TT, P)
                self.u = space.take(2 * TT, P)
                self.rhs = self.shifted
                self.o = space.take(TT, P)

        lane_space = Space(mix.at)
        lanes = [Lane(n, lane_space) for n in range(2)]
        PAIRS = DN_HEADS // 2
        d_names = ["products", "shifted", "decay", "system", "first", "first_turned", "first_x", "lx", "lx_copied",
                   "stepped", "updated", "z_near", "u_near", "w", "rhs", "z_far", "u_far", "o", "o_scaled", "squared",
                   "mean", "rms", "y", "level"]
        d = {n: sem("delta_" + n) for n in d_names}

        def at_level(h, s):
            return (h // 2) * 2 * LV + 2 * (s - 1) + h % 2 + 1

        def masked_level(h, s):
            return (h // 2) * 2 * (LV + 1) + 2 * s + h % 2 + 1

        def delta_pe(pe):
            for tt in range(TT):
                for e in ("dve", "act"):
                    pe.wait_ge(bank_free[e, tt], plan.free_count(e, tt, plan.outputs["a_out", 1][0]))
            await_turns_read(pe, "grow", [0])
            await_turns_read(pe, "v", range(4))
            pe.wait_ge(mod_ready, 30)
            for pair in range(PAIRS):
                heads = (2 * pair, 2 * pair + 1)
                for h in heads:
                    b = lanes[h % 2].bank
                    if pair:
                        pe.wait_ge(d["o_scaled"], h - 1)
                    for dr in range(2):
                        c = dr * DN_HEADS + h
                        pe.matmul(b[3][:, dr * T:(dr + 1) * T], ident[0:16, c:c + 1].broadcast_to([16, P]),
                                  g_rows[0:16, :], start=True, stop=True)
                    kT, qT = qkT[:, DN_HEADS + h, :], qkT[:, h, :]
                    for i, (jt, it) in enumerate(((0, 0), (1, 1), (0, 1), (1, 0))):
                        pe.matmul(b[0][:, i * P:(i + 1) * P], kT[:, jt * P:(jt + 1) * P], kT[:, it * P:(it + 1) * P],
                                  start=True, stop=True)
                        mm = pe.matmul(b[1][:, i * P:(i + 1) * P], kT[:, jt * P:(jt + 1) * P],
                                       qT[:, it * P:(it + 1) * P], start=True, stop=True)
                    mm.then_inc(d["products"], 1)
                for h in heads:
                    L = lanes[h % 2]
                    pe.wait_ge(d["first"], h + 1)
                    for m in range(4):
                        mm = pe.transpose(L.bank[0][:, m * P:(m + 1) * P], L.Y[:, m, :], ident)
                    mm.then_inc(d["first_turned"], 1)
                for s in range(1, LV + 1):
                    for h in heads:
                        L = lanes[h % 2]
                        pe.wait_ge(d["level"], masked_level(h, s))
                        if s == 1:
                            pe.wait_ge(d["first_x"], h + 1)
                        else:
                            pe.wait_ge(d["updated"], at_level(h, s - 1))
                        for m in range(4):
                            mm = pe.matmul(L.bank[0][:, m * P:(m + 1) * P], L.level[:, s % 2, m, :], L.X[:, m, :],
                                           start=True, stop=True)
                        mm.then_inc(d["lx"], 1)
                    for h in heads:
                        L = lanes[h % 2]
                        pe.wait_ge(d["lx_copied"], at_level(h, s))
                        for m in range(4):
                            if s < LV:
                                pe.matmul(L.bank[1][:, m * P:(m + 1) * P], L.Y[:, m, :], L.LX[:, m, :],
                                          start=True, stop=True)
                            mm = pe.matmul(L.bank[2][:, m * P:(m + 1) * P], L.LX[:, m, :], L.Y[:, m, :],
                                           start=True, stop=True)
                        mm.then_inc(d["stepped"], 1)
                for h in heads:
                    L = lanes[h % 2]
                    pe.wait_ge(d["updated"], at_level(h, LV))
                    pe.matmul(L.bank[3][:, 0:P], L.Y[:, 0, :], v_hat[:, 0, h, :], start=True, stop=True)
                    pe.matmul(L.bank[3][:, P:2 * P], L.Y[:, 3, :], v_hat[:, 1, h, :], start=True,
                              stop=True).then_inc(d["z_near"], 1)
                for h in heads:
                    L = lanes[h % 2]
                    pe.wait_ge(d["u_near"], h + 1)
                    pe.matmul(L.bank[0][:, 0:P], L.far[:, 0, :], L.u[:, 0, :], start=True, stop=True)
                    pe.matmul(L.bank[0][:, P:2 * P], L.far[:, 1, :], L.u[:, 3, :], start=True,
                              stop=True).then_inc(d["w"], 1)
                for h in heads:
                    L = lanes[h % 2]
                    pe.wait_ge(d["rhs"], h + 1)
                    pe.matmul(L.bank[3][:, 0:P], L.Y[:, 1, :], L.rhs[:, 0, 0, :], start=True, stop=True)
                    pe.matmul(L.bank[3][:, P:2 * P], L.Y[:, 2, :], L.rhs[:, 0, 1, :], start=True,
                              stop=True).then_inc(d["z_far"], 1)
                for h in heads:
                    L = lanes[h % 2]
                    pe.wait_ge(d["u_far"], h + 1)
                    for tt, terms in enumerate((((0, 0, 0), (1, 0, 2), (1, 2, 3)), ((0, 1, 1), (0, 2, 0), (1, 1, 3)))):
                        for i, (dr, blk, m) in enumerate(terms):
                            mm = pe.matmul(L.bank[1][:, tt * P:(tt + 1) * P], L.mix[:, dr, blk, :], L.u[:, m, :],
                                           start=(i == 0), stop=(i == 2))
                    mm.then_inc(d["o"], 1)
            pe.wait_ge(d["y"], 2 * DN_HEADS)

        def delta_dve(dve, link):
            link.wait()
            dve.wait_ge(z_gained, 2)
            dve.wait_ge(k_len_ready, 3)
            for pair in range(PAIRS):
                heads = (2 * pair, 2 * pair + 1)
                for h in heads:
                    L = lanes[h % 2]
                    dve.wait_ge(d["products"], h + 1)
                    for dr, name in enumerate(("incl_fwd", "incl_bwd")):
                        mask = C(name).rearrange("p (o i) -> p o i", o=1).broadcast_to([P, TT, P])
                        ins = dve.tensor_tensor(L.shifted[:, dr, :, :],
                                                L.bank[3][:, dr * T:(dr + 1) * T].rearrange("p (t i) -> p t i", t=TT),
                                                mask, ALU.add)
                    ins.then_inc(d["shifted"], 1)
                for h in heads:
                    L = lanes[h % 2]
                    kk, kq = L.bank[0], L.bank[1]
                    dve.wait_ge(d["decay"], h + 1)
                    for dr in range(2):
                        for tt in range(TT):
                            bk = beta_k[:, tt, dr * DN_HEADS + h:dr * DN_HEADS + h + 1]
                            dve.scalar_tensor_tensor(L.coupling[:, 2 * dr + tt, :], kk[:, tt * P:(tt + 1) * P], bk,
                                                     L.decay[:, dr, tt, :], ALU.mult, ALU.mult)
                        ins = dve.tensor_tensor(L.far[:, dr, :], kk[:, (2 + dr) * P:(3 + dr) * P], L.decay[:, dr, 2, :],
                                                ALU.mult)
                    ins.then_inc(d["system"], 1)
                    dve.tensor_tensor(L.mix[:, 0, :, :], kq[:, 0:3 * P].rearrange("p (b i) -> p b i", b=3),
                                      L.decay[:, 0, :, :], ALU.mult)
                    dve.tensor_tensor(L.mix[:, 1, 0:2, :], kq[:, 0:2 * P].rearrange("p (b i) -> p b i", b=2),
                                      L.decay[:, 1, 0:2, :], ALU.mult)
                    dve.tensor_tensor(L.mix[:, 1, 2, :], kq[:, 3 * P:4 * P], L.decay[:, 1, 2, :], ALU.mult)
                for h in heads:
                    L = lanes[h % 2]
                    dve.wait_ge(d["level"], masked_level(h, 0))
                    dve.tensor_tensor(L.Y, ident.rearrange("p (o i) -> p o i", o=1).broadcast_to([P, 4, P]),
                                      L.level[:, 0, :, :], ALU.subtract).then_inc(d["first"], 1)
                for s in range(1, LV + 1):
                    for h in heads:
                        L = lanes[h % 2]
                        dve.wait_ge(d["stepped"], at_level(h, s))
                        if s < LV:
                            dve.tensor_tensor(L.X.rearrange("p m i -> p (m i)"), L.X.rearrange("p m i -> p (m i)"),
                                              L.bank[1][:, :], ALU.subtract)
                        if s == 1:
                            dve.wait_ge(d["first"], h + 1)
                        else:
                            dve.wait_ge(d["updated"], at_level(h, s - 1))
                        dve.tensor_tensor(L.Y.rearrange("p m i -> p (m i)"), L.Y.rearrange("p m i -> p (m i)"),
                                          L.bank[2][:, :], ALU.subtract).then_inc(d["updated"], 1)
                for h in heads:
                    L = lanes[h % 2]
                    dve.wait_ge(d["z_near"], h + 1)
                    dve.tensor_scalar(L.u[:, 0, :], L.bank[3][:, 0:P], beta_k[:, 0, h:h + 1], None, ALU.mult)
                    dve.tensor_scalar(L.u[:, 3, :], L.bank[3][:, P:2 * P], beta_k[:, 1, DN_HEADS + h:DN_HEADS + h + 1],
                                      None, ALU.mult).then_inc(d["u_near"], 1)
                for h in heads:
                    L = lanes[h % 2]
                    dve.wait_ge(d["w"], h + 1)
                    dve.tensor_tensor(L.rhs[:, 0, 0, :], v_hat[:, 1, h, :], L.bank[0][:, 0:P], ALU.subtract)
                    dve.tensor_tensor(L.rhs[:, 0, 1, :], v_hat[:, 0, h, :], L.bank[0][:, P:2 * P],
                                      ALU.subtract).then_inc(d["rhs"], 1)
                for h in heads:
                    L = lanes[h % 2]
                    dve.wait_ge(d["z_far"], h + 1)
                    dve.tensor_scalar(L.u[:, 1, :], L.bank[3][:, 0:P], beta_k[:, 1, h:h + 1], None, ALU.mult)
                    dve.tensor_scalar(L.u[:, 2, :], L.bank[3][:, P:2 * P], beta_k[:, 0, DN_HEADS + h:DN_HEADS + h + 1],
                                      None, ALU.mult).then_inc(d["u_far"], 1)
                for h in heads:
                    L = lanes[h % 2]
                    dve.wait_ge(d["o"], h + 1)
                    if pair:
                        dve.wait_ge(d["y"], 2 * (h - 1))
                    dve.tensor_tensor(L.o, L.bank[1][:, 0:T].rearrange("p (t i) -> p t i", t=TT),
                                      q_scale[:, :, h:h + 1].broadcast_to([P, TT, P]), ALU.mult).then_inc(d["o_scaled"], 1)
                for h in heads:
                    L = lanes[h % 2]
                    dve.wait_ge(d["squared"], h + 1)
                    dve.tensor_scalar(y_ms[:, h, :], y_ss[:, h, :], 1.0 / DN_D, EPS, ALU.mult, ALU.add).then_inc(d["mean"], 1)
                for h in heads:
                    L = lanes[h % 2]
                    dve.wait_ge(d["rms"], h + 1)
                    for tt in range(TT):
                        dve.scalar_tensor_tensor(y_b[:, tt, h, :], L.o[:, tt, :], y_r[:, h, tt:tt + 1],
                                                 z_gain[:, tt, h * P:(h + 1) * P], ALU.mult, ALU.mult).then_inc(d["y"], 1)

        def delta_act(act):
            for pair in range(PAIRS):
                heads = (2 * pair, 2 * pair + 1)
                for h in heads:
                    L = lanes[h % 2]
                    act.wait_ge(d["shifted"], h + 1)
                    for dr in range(2):
                        c = dr * DN_HEADS + h
                        for tt in range(TT):
                            act.activation(L.decay[:, dr, tt, :], L.shifted[:, dr, tt, :], ACT.Exp,
                                           bias=g_in[:, tt, c:c + 1])
                        it = 1 - dr
                        ins = act.activation(L.decay[:, dr, 2, :], L.bank[3][:, dr * T + it * P:dr * T + (it + 1) * P],
                                             ACT.Exp, bias=g_off[:, c:c + 1])
                    ins.then_inc(d["decay"], 1)
                for h in heads:
                    L = lanes[h % 2]
                    act.wait_ge(d["first_turned"], h + 1)
                    act.copy(L.X.rearrange("p m i -> p (m i)"), L.bank[0][:, :]).then_inc(d["first_x"], 1)
                for s in range(1, LV + 1):
                    for h in heads:
                        L = lanes[h % 2]
                        act.wait_ge(d["lx"], at_level(h, s))
                        act.copy(L.LX.rearrange("p m i -> p (m i)"), L.bank[0][:, :]).then_inc(d["lx_copied"], 1)
                for h in heads:
                    L = lanes[h % 2]
                    act.wait_ge(d["o_scaled"], h + 1)
                    for tt in range(TT):
                        ins = act.activation(L.rhs[:, 1, tt, :], L.o[:, tt, :], ACT.Square, accum_out=y_ss[:, h, tt:tt + 1])
                    ins.then_inc(d["squared"], 1)

        def delta_pool(pool):
            for pair in range(PAIRS):
                heads = (2 * pair, 2 * pair + 1)
                for s in range(LV + 1):
                    for h in heads:
                        L = lanes[h % 2]
                        if s == 0:
                            pool.wait_ge(d["system"], h + 1)
                        if s == 2:
                            pool.wait_ge(d["first"], h + 1)
                        if s > 2:
                            pool.wait_ge(d["lx"], at_level(h, s - 2))
                        elif pair:
                            pool.wait_ge(d["lx"], at_level(h - 2, LV))
                        pool.tensor_tensor(L.level[:, s % 2, :, :], L.coupling,
                                           C(f"level_{s}").rearrange("p (o i) -> p o i", o=1).broadcast_to([P, 4, P]),
                                           ALU.mult).then_inc(d["level"], 1)
                for h in heads:
                    pool.wait_ge(d["mean"], h + 1)
                    pool.tensor_tensor(y_r[:, h, :], y_ms[:, h, :], C("minus_half").broadcast_to([P, TT]),
                                       ALU.pow).then_inc(d["rms"], 1)

        def second_dve(dve, link):
            norm_dve(dve, 2, link)
            norm_read("dve", 2)
            ffn_dve(dve, "ffn1", 2, link, range(18, 24))
            norm_dve(dve, 3, link)
            norm_read("dve", 3)
            mix_dve(dve, link)
            norm_dve(dve, 4, link)
            norm_read("dve", 4)
            ffn_dve(dve, "ffn2", 4, link)

        def second_act(act):
            norm_act(act, 2)
            norm_read("act", 2)
            ffn_act(act, "ffn1")
            norm_act(act, 3)
            norm_read("act", 3)
            for i, name in enumerate(("a_log_fwd_2", "a_log_bwd_2", "dt_bias_fwd_2", "dt_bias_bwd_2")):
                act.dma_start(head_row[:, 8 * i:8 * i + 8], A[name][0].partition_broadcast(P)).then_inc(rows_in, 16)
            act.dma_start(dn_gain, A["dn_norm_2"][0].partition_broadcast(P)).then_inc(rows_in, 16)
            mix_act(act)
            norm_act(act, 4)
            norm_read("act", 4)
            act.wait_ge(x_ready, 16)
            act.dma_start(last_gain, A["norm_final_2"].partition_broadcast(P)).then_inc(gain_in, 16)
            ffn_act(act, "ffn2")

        def second_pool(pool):
            rstd_pool(pool, 3)
            residual_pool(pool, 2)
            rstd_pool(pool, 4)
            mix_pool(pool)
            rstd_pool(pool, 5)
            residual_pool(pool, 4)

        def second_pe(pe):
            norm_pe(pe, 2)
            await_turns_read(pe, "norm2", range(4))
            ffn_pe(pe, "ffn1", range(18, 24))
            norm_pe(pe, 3)
            await_turns_read(pe, "norm3", range(4))
            mix_pe(pe)
            norm_pe(pe, 4)
            await_turns_read(pe, "norm4", range(4))
            ffn_pe(pe, "ffn2")
        first_gain = dil_z[:, 0, :]
        last_gain = gate_row[:, 1, :]

        def final_dve(dve, i, layer, gain, gains, dst, link):
            dve.wait_ge(x_ready, 4 * layer)
            mean_dve(dve, i, link)
            dve.wait_ge(gain_in, 16 * gains)
            for tt in range(TT):
                dve.scalar_tensor_tensor(dst[:, tt, :], x[:, tt, :], stat[:, i, 2, tt:tt + 1], gain,
                                         ALU.mult, ALU.mult).then_inc(x_scaled, 1)

        def final_act(act, i, layer):
            act.wait_ge(x_ready, 4 * layer)
            squares_act(act, i)

        block = ctx.enter_context(nc.Block())

        @block.sync
        def _(sp):
            view = "(t p) d -> p t d"
            for u, (dmas, consumer, _) in enumerate(plan.units):
                if u >= RING:
                    _, who, ordinal = plan.units[u - RING]
                    sp.wait_ge(pe_units if who == "pe" else ada_units, ordinal + 1)
                for src, kn, width, at, cn in dmas:
                    dst = ring[:, u % RING, 0:kn * width].rearrange("p (k n) -> p k n", k=kn)[:, :, at:at + cn]
                    sp.dma_start(dst, src).then_inc(landed[u % RING], 16)
            for tt in range(TT):
                sp.wait_ge(x_scaled, TT * (last_block - 1) + tt + 1)
                sp.dma_start(out[0, tt * P:(tt + 1) * P, :], xn[:, tt, :]).then_inc(stored, 16)
            sp.wait_ge(stored, 16 * TT)

        @block.scalar
        def _(act):
            at = 0
            for ap, n in param_rows(A):
                act.dma_start(rows[at:at + n, 0, :], ap).then_inc(params_in, 16)
                at += n
            act.dma_start(rows[0:120, 1, :], A["conv_dn_2"][0].rearrange("k (r c) -> (k r) c", c=P)).then_inc(params_in, 16)
            act.dma_start(rows[0:24, 2, :], A["ada_b"][0].rearrange("(r c) -> r c", c=P)).then_inc(params_in, 16)
            act.dma_start(rows[24:48, 2, :], A["ada_b"][1].rearrange("(r c) -> r c", c=P)).then_inc(params_in, 16)
            act.dma_start(rows[48:120, 2, :], A["b_ada_2"][0].rearrange("(r c) -> r c", c=P)).then_inc(params_in, 16)
            act.dma_start(const[:, :], const_ap).then_inc(params_in, 16)
            act.dma_start(x[:, :, :], A["x"][0].rearrange("(t p) d -> p t d", p=P)).then_inc(x_in, 16)
            for twice in range(2):
                act.dma_start(w2k[:, :, twice, :], A["nsa_ck_w2"][0].rearrange("(c p) d -> p c d", p=P)).then_inc(w2_in, 16)
            act.dma_start(w2v, A["nsa_cv_w2"][0].rearrange("(c p) d -> p c d", p=P)).then_inc(w2_in, 16)
            act.wait_ge(cols_ready, 1)
            act.activation(c_act[:, :], cols[:, 0, 0:2 * KC], ACT.Silu).then_inc(c_ready, 1)
            norm_act(act, 0)
            norm_read("act", 0)
            nsa_act(act)
            norm_act(act, 1)
            norm_read("act", 1)
            dil_act(act)
            act.wait_ge(o_ready, 4)
            act.dma_start(first_gain, A["final_g"].partition_broadcast(P)).then_inc(gain_in, 16)
            final_act(act, 2, 2)
            if last_block == 2:
                second_act(act)
                final_act(act, 6, 5)

        @block.gpsimd
        def _(pool):
            rstd_pool(pool, 0)
            nsa_pool(pool)
            rstd_pool(pool, 1)
            dil_pool(pool)
            rstd_pool(pool, 2)
            if last_block == 2:
                second_pool(pool)
                rstd_pool(pool, 6)

        @block.vector
        def _(dve):
            link = Chain(dve, dve_chain)
            dve.wait_ge(cols_done, 1)
            dve.tensor_copy(cols[:, 0, 0:100], bank[7][:, 0:100])
            dve.tensor_copy(cols[:, 1, 0:120], bank[7][:, P:P + 120])
            dve.tensor_copy(cols[:, 2, 0:120], bank[7][:, 2 * P:2 * P + 120]).then_inc(cols_ready, 1)
            dve.wait_ge(cols_ready, 1)
            dve.wait_ge(c_ready, 1)
            for n in range(4):
                ada_accumulate(dve, n, link)
                ada_collect(dve, n, link)
                if n == 0:
                    norm_dve(dve, 0, link)
            norm_read("dve", 0)
            nsa_dve(dve, link)
            ada_accumulate(dve, 10, link)
            ada_accumulate(dve, 11, link)
            residual_dve(dve, 0, "nsa_out", link, between=lambda j: ada_collect(dve, 10 + j, link))
            norm_dve(dve, 1, link)
            norm_read("dve", 1)
            dil_dve(dve, link)
            residual_dve(dve, 1, "dil_out", link)
            final_dve(dve, 2, 2, first_gain, 1, xn if last_block == 1 else x, link)
            if last_block == 2:
                second_dve(dve, link)
                final_dve(dve, 6, 5, last_gain, 2, xn, link)

        @block.tensor
        def _(pe):
            pe.wait_ge(params_in, 16 * (len(param_rows(A)) + 5))
            pe.transpose(bank[7][:, 0:100], rows[0:100, 0, :], ident[0:100, 0:100])
            pe.transpose(bank[7][:, P:P + 120], rows[0:120, 1, :], ident[0:120, 0:120])
            pe.transpose(bank[7][:, 2 * P:2 * P + 120], rows[0:120, 2, :], ident[0:120, 0:120]).then_inc(cols_done, 1)
            pe.wait_ge(cols_ready, 1)
            for n in range(4):
                ada_sum(pe, n)
            norm_pe(pe, 0)
            await_turns_read(pe, "norm0", range(4))
            nsa_pe(pe)
            norm_pe(pe, 1)
            await_turns_read(pe, "norm1", range(4))
            dil_pe(pe)
            if last_block == 2:
                second_pe(pe)


def param_rows(A):
    def r(ap):
        return ap.rearrange("(r c) -> r c", c=P)
    return [(r(A["c"][0]), 8), (r(A["c_2"][0]), 8), (r(A["norm_g"][0]), 8), (r(A["norm_g"][1]), 8),
            (r(A["norm_ffn1_2"][0]), 8), (r(A["norm_mix_2"][0]), 8), (r(A["norm_ffn2_2"][0]), 8),
            (A["nsa_pe_k"][0].rearrange("(r a) d -> r (a d)", a=2), 16),
            (A["nsa_pe_v"][0].rearrange("(r a) d -> r (a d)", a=2), 16),
            (A["conv_a_2"][0].rearrange("k (r c) -> (k r) c", c=P), 12)]


def turn_order(last_block):
    def four(name):
        return [(name, b) for b in range(4)]
    t = four("norm0") + [("kc", 0), ("vc", 0), ("ks", 0), ("kw", 0), ("hid", 0)] + four("qp") + four("qr")
    t += [("pc", 0)] + four("nsa_o") + four("norm1") + four("dil_q") + four("dil_k") + four("dil_o")
    if last_block == 2:
        t += second_turns()
    return t


_INS = ["x", "c", "norm_g", "ada_w", "ada_b", "nsa_w_in", "nsa_pe_k", "nsa_pe_v", "nsa_ck_w1", "nsa_ck_w2",
        "nsa_cv_w1", "nsa_cv_w2", "nsa_w_out", "dil_w_in", "dil_w_out", "final_g", "c_2", "w_ada_2", "b_ada_2",
        "norm_ffn1_2", "w_ffn1_up_2", "w_ffn1_down_2", "norm_mix_2", "w_in_2", "conv_a_2", "conv_dn_2",
        "a_log_fwd_2", "dt_bias_fwd_2", "a_log_bwd_2", "dt_bias_bwd_2", "dn_norm_2", "w_a_out_2", "w_b_out_2",
        "w_out_2", "norm_ffn2_2", "w_ffn2_up_2", "w_ffn2_down_2", "norm_final_2"]


def kernel(**inputs):
    import numpy as _np
    import concourse.bacc as _bacc
    from concourse import mybir as _mybir
    from concourse.bass_utils import run_bass_kernel_spmd as _run

    nc = _bacc.Bacc("TRN2", target_bir_lowering=False, num_devices=1)
    arrays, aps = {}, {}
    for name in _INS:
        a = _np.ascontiguousarray(inputs[name])
        arrays[f"in_{name}"] = a
        aps[name] = nc.dram_tensor(f"in_{name}", a.shape, _mybir.dt.float32, kind="ExternalInput").ap()
    arrays["const_table"] = CONST_TABLE
    const_ap = nc.dram_tensor("const_table", CONST_TABLE.shape, _mybir.dt.float32, kind="ExternalInput").ap()
    out = nc.dram_tensor("out", (1, T, D), _mybir.dt.float32, kind="ExternalOutput").ap()
    build(nc, aps, const_ap, out, LAST_BLOCK)
    r = _run(nc, [arrays], core_ids=[0])
    return r.results[0]["out"]
```

```python
from contextlib import ExitStack

import numpy as np
import concourse.bass as bass
from concourse import mybir

P = 128
T = 256
TT = T // P
D = 1024
KC = D // P
NH, DH = 16, 64
G, HG = 2, 8
SCALE = DH ** -0.5
CMP_LEN, CMP_STRIDE, CMP_HIDDEN = 32, 16, 256
NCMP = (T - CMP_LEN) // CMP_STRIDE + 1
D_FF = 2816
FFN_OUTS = D_FF // 256
FC = D_FF // P
DN_HEADS, DN_D = 8, 128
CONV_A = 512
EPS = 1e-6
NEG = -1e30
FLOOR = -1e25

F32 = mybir.dt.float32
F32R = mybir.dt.float32r
ALU = mybir.AluOpType
ACT = mybir.ActivationFunctionType
AX = mybir.AxisListType.X

CHUNKS = 2
UNIT = 512 * CHUNKS
RING = 6
SPLIT = 4
POOL_STAGES = ("dil", "ffn1_up", "qkv", "ba", "ca")
SUMS = 4
DIL_MASK = ((0, 6, "window"), (6, 11, 4), (11, 16, 16))
N_LEVELS = 7


def constants():
    p = np.arange(P)
    parts, where, at = [], {}, 0

    def add(name, a):
        nonlocal at
        a = np.asarray(a, np.float32).reshape(P, -1)
        parts.append(a)
        where[name] = (at, at + a.shape[1])
        at += a.shape[1]

    add("ident", np.eye(P))
    add("ones", np.ones((P, P)))
    q = P + p[:, None]
    k = np.arange(T)[None, :]
    causal = k <= q
    add("mask_causal", np.where(causal, 0.0, NEG))
    add("mask_window", np.where(causal & (q - k <= 128), 0.0, NEG))
    add("mask_4", np.where(causal & ((q - k) % 4 == 0), 0.0, NEG))
    add("mask_16", np.where(causal & ((q - k) % 16 == 0), 0.0, NEG))
    t = p[:, None] + P * np.arange(TT)[None, :]
    cmp_end = CMP_STRIDE * np.arange(NCMP) + CMP_LEN - 1
    add("mask_cmp", np.where(cmp_end[None, None, :] <= t[:, :, None], 0.0, NEG))
    half = DH // 2
    inv = (np.float32(10000.0) ** (-np.arange(half, dtype=np.float32) / np.float32(half))).astype(np.float32)
    ang = (t.astype(np.float32)[:, :, None] * inv[None, None, :]).astype(np.float32)
    cos, sin = np.cos(ang), np.sin(ang)
    add("rope_cos", np.concatenate([cos, cos], -1))
    add("rope_sin", np.concatenate([-sin, sin], -1))
    add("head_block", np.where(p[:, None] // NCMP == np.arange(HG)[None, :], 1.0, 0.0))
    for lv in range(N_LEVELS):
        s = 1 << lv
        add(f"level_{lv}", (p[:, None] // (2 * s) == p[None, :] // (2 * s)) & (p[:, None] // s != p[None, :] // s))
    j, i = p[:, None], p[None, :]
    add("incl_fwd", np.where(j <= i, 0.0, NEG))
    add("incl_bwd", np.where(j >= i, 0.0, NEG))
    add("cum_fwd", j <= i)
    add("cum_bwd", j >= i)
    add("minus_half", np.full((P, 1), -0.5))
    add("after", j > i)
    add("before", j < i)
    add("half", np.full((P, 1), 0.5))
    return np.ascontiguousarray(np.concatenate(parts, 1)), where


CONST_TABLE, CONST_AT = constants()


class Plan:

    def __init__(self, stages):
        self.units = []
        self.count = {"split": 0, "pe": 0, "ada": 0}
        self.outputs = {}
        self.freers = []
        self.ada_at = {}
        self.slot_total = [0] * RING
        self.arrive = []
        for kind, key, lots, freers in stages:
            first = len(self.units)
            consumer = {"ada": "ada", "pe": "pe", "gemm": "split"}[kind]
            for dmas in lots:
                slot = len(self.units) % RING
                self.slot_total[slot] += 16 * len(dmas)
                self.arrive.append(self.slot_total[slot])
                self.units.append((dmas, consumer, self.count[consumer]))
                self.count[consumer] += 1
            units = list(range(first, len(self.units)))
            if kind == "ada":
                for u in units:
                    self.ada_at[u] = key[1]
            if kind == "gemm":
                self.outputs[key] = (len(self.freers), units)
                self.freers.append(freers)
            else:
                self.outputs[key] = (None, units)
        self.rest_of = {}
        count = {"pool": 0, "dve": 0}
        for (stage, _), (_, units) in self.outputs.items():
            for i, u in enumerate(units):
                if self.units[u][1] == "split":
                    who = "pool" if stage in POOL_STAGES and i % 2 else "dve"
                    self.rest_of[u] = (who, count[who])
                    count[who] += 1
        self.split_units = [u for u, (_, who, _) in enumerate(self.units) if who == "split"]

    def free_count(self, eng, tt, o):
        return sum(eng in f[tt] for f in self.freers[:o + 1])


def column_units(w, width_cols, kc_total, kc=CHUNKS):
    lots = []
    for k0 in range(0, kc_total, kc):
        kn = min(kc, kc_total - k0)
        dmas, at = [], 0
        for ap, c0, cn in w:
            dmas.append((ap[k0 * P:(k0 + kn) * P, c0:c0 + cn].rearrange("(k p) n -> p k n", p=P), kn, width_cols, at, cn))
            at += cn
        lots.append(dmas)
    return lots

ARENA = 21392
UP_AT = 2048
LAST_BLOCK = 2


QKV = 3 * DN_HEADS * DN_D
Z_AT = 3 * CONV_A + QKV
BA_AT = Z_AT + DN_HEADS * DN_D
GATE_W = 416


def first_stages(A):
    both = {0: ("dve", "act"), 1: ("dve", "act")}
    dve, act = {0: ("dve",), 1: ("dve",)}, {0: ("act",), 1: ("act",)}
    gated = {0: ("gated",), 1: ("gated",)}
    ada0, ada1 = A["ada_w"][0], A["ada_w"][1]
    w, o, ck, cv = A["nsa_w_in"][0], A["nsa_w_out"][0], A["nsa_ck_w1"][0], A["nsa_cv_w1"][0]
    dw, do = A["dil_w_in"][0], A["dil_w_out"][0]
    a2 = A["w_ada_2"][0]

    def ada(n):
        src = (ada0, ada1, a2)[min(n // 6, 2)]
        c = 512 * (n - 6 * min(n // 6, 2))
        return ("ada", ("ada", n), column_units([(src, c, 512)], 512, KC), None)

    def gemm(stage, j, ap, c, n, freers, kc=KC):
        return ("gemm", (stage, j), column_units([(ap, c, n)], n, kc), freers)

    s = [ada(n) for n in range(4)]
    s += [gemm("nsa", 2, w, 1024, 512, both), ada(4), gemm("nsa", 3, w, 1536, 512, both), ada(5)]
    s += [gemm("nsa", 0, w, 0, 512, both), ada(6), gemm("nsa", 1, w, 512, 512, both), ada(7)]
    s += [("pe", ("cmp", 0), column_units([(ck, 0, 256)], 256, 16, 2 * CHUNKS), None),
          ("pe", ("cmp", 1), column_units([(cv, 0, 256)], 256, 16, 2 * CHUNKS), None)]
    s += [gemm("nsa", 4, w, 2048, 512, act), ada(8), gemm("nsa", 5, w, 2560, 304, act)]
    s += [gemm("nsa_out", 0, o, 0, 512, gated)] + [ada(n) for n in range(9, 13)]
    s += [gemm("nsa_out", 1, o, 512, 512, gated)]
    for j in range(8):
        s.append(gemm("dil", j, dw, 512 * j, 512, dve if j < 4 else act))
        if 1 <= j < 6:
            s.append(ada(12 + j))
    s += [gemm("dil_out", 0, do, 0, 512, gated)] + [ada(n) for n in range(18, 20)]
    s += [gemm("dil_out", 1, do, 512, 512, gated)]
    return s, ada, gemm


def second_stages(A, ada, gemm):
    dve, act = {0: ("dve",), 1: ("dve",)}, {0: ("act",), 1: ("act",)}
    gated = {0: ("gated",), 1: ("gated",)}
    s = []

    def ffn(name, up, down, adas):
        for j in range(FFN_OUTS):
            s.append(("gemm", (name + "_up", j),
                      column_units([(up, 256 * j, 256), (up, D_FF + 256 * j, 256)], 512, KC), dve))
            if j in adas:
                s.append(ada(adas[j]))
        for j in range(2):
            s.append(gemm(name + "_down", j, down, 512 * j, 512, gated, FC))

    ffn("ffn1", A["w_ffn1_up_2"][0], A["w_ffn1_down_2"][0], {j: 18 + j for j in range(2, 6)})
    w = A["w_in_2"][0]
    for j in range(6):
        s.append(gemm("qkv", j, w, 3 * CONV_A + 512 * j, 512, act))
    both = {0: ("dve", "act"), 1: ("dve", "act")}
    s.append(gemm("ba", 0, w, BA_AT, GATE_W, both))
    for j in range(3):
        s.append(gemm("ca", j, w, CONV_A * j, CONV_A, (act, act, dve)[j]))
    for j in range(2):
        s += [gemm("z", j, w, Z_AT + 512 * j, 512, act), ada(24 + j)]
    for j in range(4):
        s += [gemm("gate", j, w, BA_AT + GATE_W * (j + 1), GATE_W, act), ada(26 + j)]
    for j in range(2):
        s.append(gemm("a_out", j, A["w_a_out_2"][0], 512 * j, 512, dve, CONV_A // P))
    for j in range(2):
        s.append(gemm("b_out", j, A["w_b_out_2"][0], 512 * j, 512, dve))
    for j in range(2):
        s.append(gemm("mix_out", j, A["w_out_2"][0], 512 * j, 512, gated))
    ffn("ffn2", A["w_ffn2_up_2"][0], A["w_ffn2_down_2"][0], {})
    return s


def second_turns():
    t = turns("norm2", 4, "dve") + turns("ffn1_h", FFN_OUTS, "dve") + turns("norm3", 4, "dve")
    t += turns("qkv", 12) + turns("prod", 2) + turns("cab", 2, "dve") + turns("v", 4) + turns("grow", 1, "act")
    t += turns("y_b", 4, "dve") + turns("merged", 4, "dve")
    return t + turns("norm4", 4, "dve") + turns("ffn2_h", FFN_OUTS, "dve")


def turns(name, n, reader=None):
    return [(name, b, reader or ("act", "dve")[b % 2]) for b in range(n)]


def left_order(last_block):
    names = [("norm0", 4), ("nsa_o", 4), ("norm1", 4), ("dil_o", 4)]
    if last_block == 2:
        names += [("norm2", 4), ("ffn1_h", FFN_OUTS), ("norm3", 4), ("y_a", 2), ("y_b", 4), ("merged", 4),
                  ("norm4", 4), ("ffn2_h", FFN_OUTS)]
    return [(n, b) for n, k in names for b in range(k)]


class Chain:

    def __init__(self, eng, sem):
        self.eng, self.sem, self.n = eng, sem, 0

    def __call__(self, ins):
        self.mark(ins)
        self.wait()

    def mark(self, ins):
        self.n += 1
        ins.then_inc(self.sem, 1)

    def wait(self):
        self.eng.wait_ge(self.sem, self.n)


def build(nc, A, const_ap, out, last_block=2):
    ctx = ExitStack()
    with ctx:
        def sb(name, shape, dtype=F32):
            return ctx.enter_context(nc.sbuf_tensor(name, shape, dtype))

        def sem(name):
            return ctx.enter_context(nc.semaphore(name))

        const = sb("const", [P, CONST_TABLE.shape[1]])

        def C(name):
            a, b = CONST_AT[name]
            return const[:, a:b]

        ident, ones = C("ident"), C("ones")
        ring = sb("ring", [P, RING, UNIT])
        x = sb("x", [P, TT, D])
        xn = sb("xn", [P, TT, D])
        lhs_hi = sb("lhs_hi", [P, KC, T], F32R)
        lhs_lo = sb("lhs_lo", [P, KC, T], F32R)
        rows = sb("rows", [P, 3, P])
        cols = sb("cols", [P, 3, P])
        c_act = sb("c_act", [P, 2 * KC])
        ada_acc = sb("ada_acc", [P, SUMS, 512])
        mod_shift = sb("mod_shift", [P, 5, KC])
        mod_tmp = sb("mod_tmp", [P, 4])
        mod_scale = sb("mod_scale", [P, 5, KC])
        gate_row = sb("gate_row", [P, 2, D])
        y_gated = xn[:, 0, :].rearrange("p (t n) -> p t n", t=2)
        left_tmp = sb("left_tmp", [P, 2, 512])
        stat = sb("stat", [P, 7, 3, TT])
        arena_at = -(-nc.sbuf_base // 32) * 32
        arena = sb("arena", [P, ARENA])
        parts_at = -(-nc.sbuf_base // 32) * 32
        w_parts = sb("w_parts", [P, 2 * SPLIT * UNIT], F32R)
        w_hi = w_parts[:, 0:SPLIT * UNIT].rearrange("p (s n) -> p s n", s=SPLIT)
        w_lo = w_parts[:, SPLIT * UNIT:].rearrange("p (s n) -> p s n", s=SPLIT)
        lane_mem = nc.alloc_sbuf_tensor_at("lane_mem", [P, 2 * SPLIT * UNIT], F32, offset=parts_at)
        up_hi = nc.alloc_sbuf_tensor_at("up_hi", [P, FC, T], F32R, offset=arena_at + 4 * UP_AT)
        up_lo = nc.alloc_sbuf_tensor_at("up_lo", [P, FC, T], F32R, offset=arena_at + 4 * (UP_AT + FC * T))
        bank = [ctx.enter_context(nc.psum_tensor(f"bank{i}", [P, 512], F32))[:, :] for i in range(8)]

        class Space:

            def __init__(self, at=0, memory=None, end=ARENA):
                self.at, self.memory, self.end = at, arena if memory is None else memory, end

            def take(self, *shape):
                n = 1
                for s in shape:
                    n *= s
                assert self.at + n <= self.end, (self.at, n)
                view = self.memory[:, self.at:self.at + n]
                self.at += n
                names = "abcd"[:len(shape)]
                if len(shape) > 1:
                    view = view.rearrange(f"p ({' '.join(names)}) -> p {' '.join(names)}",
                                          **dict(zip(names, shape)))
                return view

        landed = [sem(f"landed{i}") for i in range(RING)]
        pe_units = sem("pe_units")
        hi_ready = sem("hi_ready")
        lo_ready = {e: sem("lo_ready_" + e) for e in ("dve", "pool")}
        hi_used = sem("hi_used")
        parts_used = sem("parts_used")
        left_hi, left_lo = sem("left_hi"), sem("left_lo")
        ada_units = sem("ada_units")
        gemm_tile0 = sem("gemm_tile0")
        y_ready = [sem(f"y_ready{t}") for t in range(TT)]
        bank_free = {(e, t): sem(f"bank_free_{e}{t}") for e in ("dve", "act") for t in range(TT)}
        bank_free.update({("gated", t): y_ready[t] for t in range(TT)})
        turned = sem("turned")
        turn_read = {"dve": sem("turn_read_dve"), "act": sem("turn_read_act")}
        params_in = sem("params_in")
        x_in = sem("x_in")
        const_in = sem("const_in")
        cols_done = sem("cols_done")
        cols_ready = sem("cols_ready")
        c_ready = sem("c_ready")
        ada_summed = sem("ada_summed")
        mod_ready = sem("mod_ready")
        dve_chain = sem("dve_chain")
        act_chain = sem("act_chain")
        x_ready = sem("x_ready")
        x_scaled = sem("x_scaled")
        gain_in = sem("gain_in")
        squares = sem("squares")
        mean_ready = sem("mean_ready")
        rstd_ready = sem("rstd_ready")
        xn_ready = {"dve": sem("xn_ready_dve"), "act": sem("xn_ready_act")}
        stored = sem("stored")

        stages, ada_stage, gemm_stage = first_stages(A)
        if last_block == 2:
            stages += second_stages(A, ada_stage, gemm_stage)
        plan = Plan(stages)

        TURNS = turn_order(last_block)
        TURN_AT = {(n, b): i for i, (n, b, _) in enumerate(TURNS)}
        LEFT_AT = {key: i for i, key in enumerate(left_order(last_block))}

        def turn_bank(name, b=0):
            return bank[4 + TURN_AT[name, b] % 2]

        def turn_reader(name, b=0):
            return TURNS[TURN_AT[name, b]][2]

        def turn_count(name, b):
            i = TURN_AT[name, b]
            return sum(e == TURNS[i][2] for n, _, e in TURNS[:i + 1] if n.startswith("norm") or (n, 0) not in LEFT_AT)

        ENG = {"dve": nc.vector, "act": nc.scalar, "pool": nc.gpsimd}
        streamed = {"dve": 0, "act": 0, "pool": 0}
        stream_end = {"dve": None, "act": None, "pool": None}
        chain = {}

        def await_unit(eng, u):
            eng.wait_ge(landed[u % RING], plan.arrive[u])

        def stream_to(who, last):
            eng = ENG[who]
            if stream_end[who] is not None:
                last = min(last, stream_end[who])
            while streamed[who] <= last:
                u = streamed[who]
                streamed[who] += 1
                dmas, consumer, v = plan.units[u]
                if consumer == "split":
                    n = dmas[0][1] * dmas[0][2]
                    raw, hi, lo = ring[:, u % RING, 0:n], w_hi[:, v % SPLIT, 0:n], w_lo[:, v % SPLIT, 0:n]
                    if who == "act":
                        await_unit(eng, u)
                        if v >= SPLIT:
                            eng.wait_ge(hi_used, v - SPLIT + 1)
                            e, ordinal = plan.rest_of[plan.split_units[v - SPLIT]]
                            eng.wait_ge(lo_ready[e], ordinal + 1)
                        eng.copy(hi, raw).then_inc(hi_ready, 1)
                    elif who == plan.rest_of[u][0]:
                        eng.wait_ge(hi_ready, v + 1)
                        if v >= SPLIT:
                            eng.wait_ge(parts_used, v - SPLIT + 1)
                        eng.tensor_tensor(lo, raw, hi.bitcast(F32), ALU.subtract).then_inc(lo_ready[who], 1)
                elif consumer == "ada" and who == "dve":
                    n = plan.ada_at[u]
                    part = plan.outputs["ada", n][1].index(u)
                    if part == 0:
                        ada_collect_up_to(n)
                    for kk in range(CHUNKS * part, CHUNKS * (part + 1)):
                        ada_step(n, kk)

        def stream_ahead(who, stage, j, more=1):
            v = plan.units[plan.outputs[stage, j][1][-1]][2] + more * (KC // 2 // CHUNKS)
            stream_to(who, plan.split_units[min(v, len(plan.split_units) - 1)])

        lefts_used = set()

        def gemm(pe, stage, j, left, ready, n, kc_total=KC):
            o, units = plan.outputs[stage, j]
            first_use = ready not in lefts_used
            lefts_used.add(ready)
            k0 = 0
            for u in units:
                v = plan.units[u][2]
                kn = min(CHUNKS, kc_total - k0)
                hi, lo = w_hi[:, v % SPLIT, :], w_lo[:, v % SPLIT, :]
                if first_use:
                    last = LEFT_AT[ready, (k0 + kn - 1) // 2]
                    pe.wait_ge(left_hi, last + 1)
                    pe.wait_ge(left_lo, last + 1)
                pe.wait_ge(hi_ready, v + 1)
                for tt in range(TT):
                    b = bank[2 * (o % 2) + tt][:, 0:n]
                    if k0 == 0 and o >= 2:
                        for e in plan.freers[o - 2][tt]:
                            pe.wait_ge(bank_free[e, tt], plan.free_count(e, tt, o - 2))
                    for k in range(kn):
                        x_hi, x_lo = left(k0 + k, tt)
                        w = hi[:, k * n:(k + 1) * n]
                        pe.matmul(b, x_hi, w, start=(k0 + k == 0), stop=False)
                        mm = pe.matmul(b, x_lo, w, start=False, stop=False)
                mm.then_inc(hi_used, 1)
                who, ordinal = plan.rest_of[u]
                pe.wait_ge(lo_ready[who], ordinal + 1)
                for tt in range(TT):
                    for k in range(kn):
                        x_hi, _ = left(k0 + k, tt)
                        mm = pe.matmul(bank[2 * (o % 2) + tt][:, 0:n], x_hi, lo[:, k * n:(k + 1) * n],
                                       start=False, stop=(k0 + k == kc_total - 1))
                    if tt == 0 and k0 + kn == kc_total:
                        mm.then_inc(gemm_tile0, 1)
                mm.then_inc(parts_used, 1)
                k0 += kn

        def gemm_bank(stage, j, tt):
            return bank[2 * (plan.outputs[stage, j][0] % 2) + tt]

        def await_output(eng, stage, j, tt):
            o, units = plan.outputs[stage, j]
            for who in ("dve", "act"):
                if eng is ENG[who]:
                    stream_ahead(who, stage, j)
            if tt == 0:
                eng.wait_ge(gemm_tile0, o + 1)
            else:
                eng.wait_ge(parts_used, plan.units[units[-1]][2] + 1)

        def turn(pe, name, b, blocks):
            i = TURN_AT[name, b]
            if i >= 2:
                await_turns_read(pe, TURNS[i - 2][0], [TURNS[i - 2][1]])
            for src, kin, mout, col in blocks:
                mm = pe.transpose(bank[4 + i % 2][0:mout, col:col + kin], src, ident[0:kin, 0:kin])
            mm.then_inc(turned, 1)

        def await_turn(eng, name, b=0):
            eng.wait_ge(turned, TURN_AT[name, b] + 1)

        def turn_tokens(pe, name, src, banks):
            for b in banks:
                turn(pe, name, b, [(src(tt, 2 * b + h), P, P, h * T + tt * P)
                                   for h in range(2) for tt in range(TT)])

        def copy(eng, dst, src):
            return eng.tensor_copy(dst, src) if eng is nc.vector else eng.copy(dst, src)

        def read_turns(who, name, dst, banks):
            for b in banks:
                if turn_reader(name, b) == who:
                    await_turn(ENG[who], name, b)
                    copy(ENG[who], dst(b), turn_bank(name, b)).then_inc(turn_read[who], 1)

        def await_turns_read(eng, name, banks):
            if (name, 0) in LEFT_AT and not name.startswith("norm"):
                eng.wait_ge(left_lo, LEFT_AT[name, banks[-1]] + 1)
                return
            for e in ("dve", "act"):
                last = [b for b in banks if turn_reader(name, b) == e]
                if last:
                    eng.wait_ge(turn_read[e], turn_count(name, last[-1]))

        def ada_step(n, kk):
            dve, link = nc.vector, chain["dve"]
            u = plan.outputs["ada", n][1][kk // CHUNKS]
            acc = ada_acc[:, n % SUMS, :]
            if n >= SUMS and kk == 0:
                dve.wait_ge(ada_summed, n - SUMS + 1)
            k = kk % CHUNKS
            if k == 0:
                await_unit(dve, u)
            w = ring[:, u % RING, k * 512:(k + 1) * 512]
            c = (0 if n < 12 else KC) + kk
            s = c_act[:, c:c + 1]
            if kk == 0:
                ins = dve.tensor_scalar(acc, w, s, None, ALU.mult)
            else:
                if k == 0:
                    dve.wait_ge(ada_units, plan.units[u][2])
                else:
                    link.wait()
                ins = dve.scalar_tensor_tensor(acc, w, s, acc, ALU.mult, ALU.add)
            if k < CHUNKS - 1:
                link.mark(ins)
            else:
                ins.then_inc(ada_units, 1)

        def ada_beside(n0, i):
            n, kk = n0 + i // 8, i % 8
            ada_step(n, kk)
            if kk % CHUNKS == CHUNKS - 1:
                streamed["dve"] += 1
                assert streamed["dve"] == plan.outputs["ada", n][1][kk // CHUNKS] + 1

        def ada_sum(pe, n):
            _, units = plan.outputs["ada", n]
            pe.wait_ge(ada_units, plan.units[units[-1]][2] + 1)
            if n >= 1:
                pe.wait_ge(mod_ready, n)
            acc = ada_acc[:, n % SUMS, :]
            if n % 6 < 4:
                for c in range(4):
                    mm = pe.matmul(bank[7][:, c:c + 1], acc[:, c * P:(c + 1) * P], ones[:, 0:1],
                                   start=True, stop=True)
            else:
                for c in range(4):
                    r = 4 * n + c
                    mm = pe.matmul(bank[6][:, c * P:(c + 1) * P], ones, acc[:, c * P:(c + 1) * P],
                                   start=True, stop=False)
                    mm = pe.matmul(bank[6][:, c * P:(c + 1) * P], bias_pick(r), rows[0:120, 2, :],
                                   start=False, stop=True)
            mm.then_inc(ada_summed, 1)

        def bias_pick(r):
            return ident[0:120, r:r + 1].broadcast_to([120, P])

        collected = [0]

        def ada_collect_up_to(n):
            while collected[0] < n:
                ada_collect(collected[0])

        def ada_collect(n):
            dve, link = nc.vector, chain["dve"]
            assert collected[0] == n, n
            collected[0] += 1
            layer, part = n // 6, n % 6
            dve.wait_ge(ada_summed, n + 1)
            half = slice(4 * (part % 2), 4 * (part % 2) + 4)
            bias = cols[:, 2, 4 * n:4 * n + 4]
            if part < 2:
                dve.tensor_tensor(mod_shift[:, layer, half], bank[7][:, 0:4], bias, ALU.add).then_inc(mod_ready, 1)
            elif part < 4:
                gain = cols[:, 0, 16 + 8 * layer + half.start:16 + 8 * layer + half.stop]
                link(dve.tensor_tensor(mod_tmp[:, :], bank[7][:, 0:4], bias, ALU.add))
                dve.scalar_tensor_tensor(mod_scale[:, layer, half], mod_tmp[:, :], 1.0, gain,
                                         ALU.add, ALU.mult).then_inc(mod_ready, 1)
            else:
                row = gate_row[:, layer % 2, 512 * (part % 2):512 * (part % 2) + 512]
                half_ffn = 0.5 if layer in (2, 4) else 1.0
                dve.tensor_scalar(row, bank[6][:, :], half_ffn, None, ALU.mult).then_inc(mod_ready, 1)

        def await_x(eng, n):
            if n == 0:
                eng.wait_ge(x_in, 16)
            elif n == 2:
                eng.wait_ge(x_scaled, TT)
            else:
                eng.wait_ge(x_ready, 4 * n)

        def statistic(n):
            return n if n < 2 else n + 1

        def mean_dve(dve, i, link):
            link(dve.tensor_tensor_reduce(xn[:, 1, :], x[:, 1, :], x[:, 1, :], 1.0, 0.0, ALU.mult, ALU.add,
                                          stat[:, i, 0, 1:2]))
            dve.wait_ge(squares, i + 1)
            dve.tensor_scalar(stat[:, i, 1, :], stat[:, i, 0, :], 1.0 / D, EPS, ALU.mult,
                              ALU.add).then_inc(mean_ready, 1)
            dve.wait_ge(rstd_ready, i + 1)

        def squares_act(act, i):
            act.activation(xn[:, 0, :], x[:, 0, :], ACT.Square, accum_out=stat[:, i, 0, 0:1]).then_inc(squares, 1)

        def rstd_pool(pool, i):
            pool.wait_ge(mean_ready, i + 1)
            pool.tensor_tensor(stat[:, i, 2, :], stat[:, i, 1, :], C("minus_half").broadcast_to([P, TT]),
                               ALU.pow).then_inc(rstd_ready, 1)

        NEXT = [("nsa", 2), ("dil", 0), ("ffn1_up", 0), ("qkv", 0), ("ffn2_up", 0)]

        def norm_pool(pool, n):
            if n:
                stream_ahead("pool", *NEXT[n], -1)
            rstd_pool(pool, statistic(n))
            stream_ahead("pool", *NEXT[n], 0)

        def norm_dve(dve, n, link):
            i = statistic(n)
            if n:
                stream_ahead("dve", *NEXT[n], -1)
            await_x(dve, n)
            mean_dve(dve, i, link)
            dve.tensor_scalar(xn[:, 0, :], x[:, 0, :], stat[:, i, 2, 0:1], None, ALU.mult).then_inc(xn_ready["dve"], 1)
            if n:
                stream_ahead("dve", *NEXT[n], 0)

        def norm_act(act, n):
            i = statistic(n)
            if n:
                stream_ahead("act", *NEXT[n], -1)
            await_x(act, n)
            squares_act(act, i)
            act.wait_ge(rstd_ready, i + 1)
            act.activation(xn[:, 1, :], x[:, 1, :], ACT.Copy, scale=stat[:, i, 2, 1:2]).then_inc(xn_ready["act"], 1)
            stream_ahead("act", *NEXT[n], 0)

        def norm_pe(pe, n):
            pe.wait_ge(xn_ready["dve"], n + 1)
            pe.wait_ge(xn_ready["act"], n + 1)
            turn_tokens(pe, f"norm{n}", lambda tt, c: xn[:, tt, c * P:(c + 1) * P], range(4))

        def norm_left_dve(dve, n):
            dve.wait_ge(mod_ready, 6 * n + 4)
            name = f"norm{n}"
            for b in range(6):
                if b < 4:
                    await_turn(dve, name, b)
                    if b >= 2:
                        dve.wait_ge(left_lo, LEFT_AT[name, b - 2] + 1)
                    for h in range(2):
                        c = 2 * b + h
                        ins = dve.tensor_scalar(left_tmp[:, b % 2, h * T:(h + 1) * T],
                                                turn_bank(name, b)[:, h * T:(h + 1) * T],
                                                mod_scale[:, n, c:c + 1], mod_shift[:, n, c:c + 1], ALU.mult, ALU.add)
                    ins.then_inc(turn_read["dve"], 1)
                if 1 <= b < 5:
                    left_rest(dve, name, b - 1, left_tmp[:, (b - 1) % 2, :], lhs_pair)

        def norm_left_act(act, n):
            for b in range(4):
                act.wait_ge(turn_read["dve"], turn_count(f"norm{n}", b))
                left_round(act, left_tmp[:, b % 2, :], lhs_pair(b)[0])

        def lhs_pair(b):
            return [p[:, 2 * b:2 * b + 2, :].rearrange("p c t -> p (c t)") for p in (lhs_hi, lhs_lo)]

        def left_round(act, src, hi):
            act.copy(hi, src).then_inc(left_hi, 1)

        def left_rest(dve, name, b, src, pair):
            hi, lo = pair(b)
            dve.wait_ge(left_hi, LEFT_AT[name, b] + 1)
            dve.tensor_tensor(lo, src, hi.bitcast(F32), ALU.subtract).then_inc(left_lo, 1)

        def turned_left_act(act, name, banks, pair=None):
            for b in banks:
                await_turn(act, name, b)
                left_round(act, turn_bank(name, b), (pair or lhs_pair)(b)[0])

        def turned_left_dve(dve, name, banks, pair=None):
            for b in banks:
                await_turn(dve, name, b)
                left_rest(dve, name, b, turn_bank(name, b), pair or lhs_pair)

        def from_lhs(k, tt):
            return lhs_hi[:, k, tt * P:(tt + 1) * P], lhs_lo[:, k, tt * P:(tt + 1) * P]

        def residual_dve(dve, layer, stage):
            for j in range(2):
                for tt in range(TT):
                    await_output(dve, stage, j, tt)
                    step = 2 * layer + j
                    if step >= 1:
                        dve.wait_ge(x_ready, 2 * step + tt - 1)
                    dve.wait_ge(mod_ready, 6 * layer + 5 + j)
                    dve.tensor_tensor(y_gated[:, tt, :], gemm_bank(stage, j, tt)[:, :],
                                      gate_row[:, layer % 2, 512 * j:512 * (j + 1)], ALU.mult).then_inc(y_ready[tt], 1)

        def residual_pool(pool, layer):
            for j in range(2):
                for tt in range(TT):
                    pool.wait_ge(y_ready[tt], 2 * layer + j + 1)
                    xs = x[:, tt, 512 * j:512 * (j + 1)]
                    pool.tensor_tensor(xs, xs, y_gated[:, tt, :], ALU.add).then_inc(x_ready, 1)

        nsa = Space()
        rope_a = nsa.take(2, TT, 512)
        rope_b = xn.rearrange("p t (r n) -> p r t n", r=2)
        nsa_rope_end = nsa.at
        q_plain = nsa.take(TT, NH, DH)
        q_rope = nsa.take(TT, NH, DH)
        z_act = nsa.take(TT, D)
        gates = nsa.take(TT, 3 * NH)
        late = Space(nsa.at)
        kc2, vc2, ks2, kw2 = [nsa.take(TT, G, 2, DH) for _ in range(4)]
        v_slc, v_win = nsa.take(TT, G, DH), nsa.take(TT, G, DH)
        ksT, kwT = nsa.take(G, T), nsa.take(G, T)
        kc_next, vc_next = nsa.take(G, T), nsa.take(G, T)
        qpT, qrT = nsa.take(KC, T), nsa.take(KC, T)
        nsa_o = q_plain
        on_xn = Space(0, xn.rearrange("p t d -> p (t d)"), TT * D)
        probsT_mem = on_xn.take(2, 3 * P)
        o_part = on_xn.take(2, HG, DH)
        blocks = nsa.take(2, CMP_LEN // 2, G, NCMP)
        w2k = nsa.take(2, 2, DH)
        w2v = nsa.take(2, DH)
        hidden = nsa.take(2, CMP_HIDDEN)
        hidT = nsa.take(2, 2, G * NCMP)
        hid_rep = nsa.take(2, G, HG, NCMP)
        k_cmpT = nsa.take(G * NCMP)
        v_blocks = nsa.take(G, HG, DH)
        s_cmp = late.take(TT, NH, NCMP)
        p_cmp = late.take(TT, NH, NCMP)
        m_cmp, d_cmp, w_cmp = [late.take(TT, NH) for _ in range(3)]
        p_cmpT = late.take(TT, G, P)

        class Attention:

            def __init__(self, name, space, items):
                self.name, self.items, n = name, items, len(items)
                self.masked = space.take(2, 3 * P)
                self.probs = space.take(2, 3 * P)
                self.probsT = probsT_mem
                self.top = space.take(n, TT)
                self.bias = space.take(n, TT)
                self.den = space.take(n, TT)
                self.rden = space.take(n // 8, TT, 8)
                self.weight = space.take(n // 8, TT, 8)
                assert space.at <= nsa_rope_end
                self.scored = sem(name + "_scored")
                self.masked_done = sem(name + "_masked")
                self.bias_ready = sem(name + "_bias_ready")
                self.exp_done = sem(name + "_exp_done")
                self.probs_turned = sem(name + "_probs_turned")
                self.probsT_ready = [sem(name + "_probsT_act"), sem(name + "_probsT_dve")]
                self.pv_done = sem(name + "_pv_done")
                self.pv_read = sem(name + "_pv_read")

            def pe(self, pe):
                n = len(self.items)
                for i in range(n + 3):
                    if i < n:
                        q, k, _, _ = self.items[i]
                        if i >= 2:
                            pe.wait_ge(self.masked_done, i - 1)
                        pe.matmul(bank[i % 2][:, 0:P], q(0), k()[:, 0:P], start=True, stop=True)
                        pe.matmul(bank[i % 2][:, P:3 * P], q(1), k(), start=True,
                                  stop=True).then_inc(self.scored, 1)
                    if 2 <= i < n + 2:
                        j = i - 2
                        pe.wait_ge(self.exp_done, j + 1)
                        if j >= 2:
                            pe.wait_ge(self.probsT_ready[j % 2], j // 2)
                        for b in range(3):
                            mm = pe.transpose(bank[2 + j % 2][:, b * P:(b + 1) * P],
                                              self.probs[:, j % 2, b * P:(b + 1) * P], ident)
                        mm.then_inc(self.probs_turned, 1)
                    if i >= 3:
                        j = i - 3
                        g, c = j // 8, (j % 8) * DH
                        pe.wait_ge(self.probsT_ready[j % 2], j // 2 + 1)
                        if j % 8 == 0 and g >= 2:
                            pe.wait_ge(self.pv_read, g - 1)
                        v = self.items[j][3]
                        pT = self.probsT[:, j % 2, :]
                        o0, o1 = bank[4 + 2 * (g % 2)], bank[5 + 2 * (g % 2)]
                        pe.matmul(o0[:, c:c + DH], pT[:, 0:P], v(0), start=True, stop=True)
                        pe.matmul(o1[:, c:c + DH], pT[:, P:2 * P], v(0), start=True, stop=False)
                        pe.matmul(o1[:, c:c + DH], pT[:, 2 * P:3 * P], v(1), start=False,
                                  stop=True).then_inc(self.pv_done, 1)

            def dve(self, dve, link, weigh, beside):
                n = len(self.items)
                for i in range(n + 4):
                    if i < n:
                        mask = self.items[i][2]
                        dve.wait_ge(self.scored, i + 1)
                        if i >= 2:
                            dve.wait_ge(self.exp_done, i - 1)
                        m, s = self.masked[:, i % 2, :], bank[i % 2]
                        dve.tensor_tensor_reduce(m[:, 0:P], s[:, 0:P], mask[:, P:T], 1.0, NEG, ALU.add, ALU.max,
                                                 self.top[:, i, 0:1])
                        dve.tensor_tensor_reduce(m[:, P:3 * P], s[:, P:3 * P], mask, 1.0, NEG, ALU.add, ALU.max,
                                                 self.top[:, i, 1:2]).then_inc(self.masked_done, 1)
                        dve.wait_ge(self.masked_done, i + 1)
                        dve.tensor_scalar(self.bias[:, i, :], self.top[:, i, :], -SCALE, None,
                                          ALU.mult).then_inc(self.bias_ready, 1)
                        beside(i)
                    if 2 <= i < n + 2 and i % 2 == 1:
                        self.copy_turned(dve, i - 2)
                    if i >= 4 and (i - 4) % 8 == 7:
                        weigh((i - 4) // 8)

            def copy_turned(self, eng, j):
                eng.wait_ge(self.probs_turned, j + 1)
                if j >= 2:
                    eng.wait_ge(self.pv_done, j - 1)
                copy(eng, self.probsT[:, j % 2, :], bank[2 + j % 2][:, 0:3 * P]).then_inc(self.probsT_ready[j % 2], 1)

            def act(self, act):
                n = len(self.items)
                for i in range(n + 2):
                    if i < n:
                        act.wait_ge(self.bias_ready, i + 1)
                        if i >= 2:
                            act.wait_ge(self.probs_turned, i - 1)
                        m, p = self.masked[:, i % 2, :], self.probs[:, i % 2, :]
                        act.activation(p[:, 0:P], m[:, 0:P], ACT.Exp, bias=self.bias[:, i, 0:1], scale=SCALE,
                                       accum_out=self.den[:, i, 0:1])
                        act.activation(p[:, P:3 * P], m[:, P:3 * P], ACT.Exp, bias=self.bias[:, i, 1:2],
                                       scale=SCALE, accum_out=self.den[:, i, 1:2]).then_inc(self.exp_done, 1)
                    if i >= 2 and i % 2 == 0:
                        self.copy_turned(act, i - 2)

            def reciprocal(self, dve, g, link):
                dve.wait_ge(self.exp_done, 8 * g + 8)
                link(dve.reciprocal(self.rden[:, g, :, :],
                                    self.den[:, 8 * g:8 * g + 8, :].rearrange("p h t -> p t h")))

        def head_rows(h):
            return slice(DH * (h % 2), DH * (h % 2) + DH)

        def nsa_item(kT, v, g, h):
            hh = HG * g + h
            return (lambda tt: qrT[head_rows(hh), hh // 2, tt * P:(tt + 1) * P],
                    lambda: kT[head_rows(hh), g, :], C("mask_causal"),
                    lambda kt: v[:, kt, g, :])

        nsa_att = Attention("nsa_att", Space(0), [nsa_item(kT, v, g, h) for g in range(G)
                                             for kT, v in ((ksT, v_slc), (kwT, v_win)) for h in range(HG)])

        rope_done = sem("rope_done")
        blocks_ready = sem("blocks_ready")
        w2_in = sem("w2_in")
        hidden_act = sem("hidden_act")
        cmp_kv_done, cmp_kv_read = sem("cmp_kv_done"), sem("cmp_kv_read")
        cmp_scored, cmp_shifted, cmp_exp = sem("cmp_scored"), sem("cmp_shifted"), sem("cmp_exp")
        cmp_pv_done, cmp_pv_read = sem("cmp_pv_done"), sem("cmp_pv_read")
        o_added = sem("o_added")
        o_ready = sem("o_ready")

        ROPES = [("nsa", 2), ("nsa", 3), ("nsa", 0), ("nsa", 1), ("dil", 0), ("dil", 1), ("dil", 2), ("dil", 3)]

        def rope_parts(dve, key, src, heads):
            r = ROPES.index(key)
            cos = C("rope_cos").rearrange("p (t d) -> p t d", t=TT)
            sin = C("rope_sin").rearrange("p (t d) -> p t d", t=TT)
            for tt in range(TT):
                await_output(dve, *key, tt)
                if r >= 2:
                    dve.wait_ge(rope_done, 2 * (r - 2) + tt + 1)
                n = heads * DH
                s = src(tt).rearrange("p (h d) -> p h d", d=DH)
                a = rope_a[:, r % 2, tt, 0:n].rearrange("p (h d) -> p h d", d=DH)
                b = rope_b[:, r % 2, tt, 0:n].rearrange("p (h d) -> p h d", d=DH)
                half = DH // 2
                dve.tensor_tensor(a, s, cos[:, tt:tt + 1, :].broadcast_to([P, heads, DH]), ALU.mult)
                dve.tensor_tensor(b[:, :, 0:half], s[:, :, half:DH],
                                  sin[:, tt:tt + 1, 0:half].broadcast_to([P, heads, half]), ALU.mult)
                dve.tensor_tensor(b[:, :, half:DH], s[:, :, 0:half],
                                  sin[:, tt:tt + 1, half:DH].broadcast_to([P, heads, half]),
                                  ALU.mult).then_inc(bank_free["dve", tt], 1)

        def rope_add(pool, key, dst, heads):
            r = ROPES.index(key)
            o = plan.outputs[key][0]
            stream_ahead("pool", *key)
            for tt in range(TT):
                pool.wait_ge(bank_free["dve", tt], plan.free_count("dve", tt, o))
                n = heads * DH
                a = rope_a[:, r % 2, tt, 0:n].rearrange("p (h d) -> p h d", d=DH)
                b = rope_b[:, r % 2, tt, 0:n].rearrange("p (h d) -> p h d", d=DH)
                for d in dst(tt)[:-1]:
                    pool.tensor_tensor(d, a, b, ALU.add)
                pool.tensor_tensor(dst(tt)[-1], a, b, ALU.add).then_inc(rope_done, 1)

        def nsa_dve(dve, link):
            dve.wait_ge(const_in, 16)
            for tt in range(TT):
                await_output(dve, "nsa", 2, tt)
                src = gemm_bank("nsa", 2, tt)
                for d, c in ((kc2, 0), (vc2, P)):
                    for twice in range(2):
                        ins = dve.tensor_copy(d[:, tt, :, twice, :],
                                              src[:, c:c + P].rearrange("p (g d) -> p g d", g=G))
            rope_parts(dve, ("nsa", 2), lambda tt: gemm_bank("nsa", 2, tt)[:, 2 * P:3 * P], G)
            rope_parts(dve, ("nsa", 3), lambda tt: gemm_bank("nsa", 3, tt)[:, 0:P], G)
            stream_ahead("dve", "nsa", 0, 0)
            for kv, (name, d) in enumerate((("kc", kc_next), ("vc", vc_next))):
                if kv == 0:
                    assert turn_reader("kc") == "dve" and turn_reader("ks") == "dve"
                    await_turn(dve, "kc")
                    dve.tensor_copy(d[0:DH, :, :], turn_bank("kc")[0:DH, :].rearrange("p (g t) -> p g t", g=G))
                    dve.tensor_copy(d[DH:P, :, 0:T - 1],
                                    turn_bank("kc")[DH:P, :].rearrange("p (g t) -> p g t", g=G)[:, :, 1:T]).then_inc(
                                        turn_read["dve"], 1)
                    read_turns("dve", "ks", lambda b: ksT.rearrange("p g t -> p (g t)"), [0])
                else:
                    await_turns_read(dve, "vc", [0])
            await_turns_read(dve, "kc", [0])
            for kv, (d, pe0) in enumerate(((kc_next, 56), (vc_next, 72))):
                for g in range(G):
                    src = d[:, g, 0:CMP_STRIDE * (NCMP + 1)].rearrange("p (n s) -> p s n", s=CMP_STRIDE)
                    for h in range(2):
                        o = blocks[:, kv, 8 * h:8 * h + 8, g, :]
                        pos = cols[:, 0, pe0 + 8 * h:pe0 + 8 * h + 8].rearrange("p (j o) -> p j o", o=1)
                        ins = dve.tensor_tensor(o, src[:, 0:CMP_STRIDE:2, h:h + NCMP],
                                                pos.broadcast_to([P, 8, NCMP]), ALU.add)
                ins.then_inc(blocks_ready, 1)
            rope_parts(dve, ("nsa", 0), lambda tt: gemm_bank("nsa", 0, tt)[:, :], 8)
            stream_end["dve"] = plan.outputs["ada", 7][1][-1]
            rope_parts(dve, ("nsa", 1), lambda tt: gemm_bank("nsa", 1, tt)[:, :], 8)
            stream_end["dve"] = None
            ada_collect_up_to(8)
            stream_ahead("dve", "nsa", 4, 0)
            await_turn(dve, "hid")
            hb = turn_bank("hid")[:, 0:4 * G * NCMP].rearrange("p (v c m) -> p v c m", v=2, c=2)
            dve.tensor_copy(hidT, hb)
            for c in range(2):
                src = hb[:, 1, c, :].rearrange("p (g n) -> p g n", g=G)
                for g in range(G):
                    ins = dve.tensor_copy(hid_rep[:, c, g, :, :], src[:, g:g + 1, :].broadcast_to([P, HG, NCMP]))
            ins.then_inc(turn_read["dve"], 1)
            dve.wait_ge(cmp_kv_done, 1)
            dve.tensor_copy(k_cmpT, bank[6][:, 256:256 + G * NCMP])
            for g in range(G):
                n = HG * NCMP
                ins = dve.tensor_tensor(v_blocks[0:n, g, :, :],
                                        bank[7][0:n, 256 + g * DH:256 + (g + 1) * DH].rearrange(
                                            "p (o d) -> p o d", o=1).broadcast_to([n, HG, DH]),
                                        C("head_block")[0:n, :].rearrange("p (h o) -> p h o", o=1).broadcast_to([n, HG, DH]),
                                        ALU.mult)
            ins.then_inc(cmp_kv_read, 1)
            stream_ahead("dve", "nsa", 5, 0)
            read_turns("dve", "qp", lambda b: qpT[:, 2 * b:2 * b + 2, :].rearrange("p c t -> p (c t)"), range(4))
            read_turns("dve", "qr", lambda b: qrT[:, 2 * b:2 * b + 2, :].rearrange("p c t -> p (c t)"), range(4))
            ada_collect_up_to(9)
            dve.wait_ge(cmp_scored, 1)
            for tt in range(TT):
                mask = C("mask_cmp").rearrange("p (t n) -> p t n", t=TT)[:, tt:tt + 1, :]
                for odd in range(2):
                    half = bank[6 + odd][:, tt * HG * NCMP:(tt + 1) * HG * NCMP]
                    ins = dve.tensor_tensor(s_cmp[:, tt, odd:NH:2, :], half.rearrange("p (h n) -> p h n", n=NCMP),
                                            mask.broadcast_to([P, HG, NCMP]), ALU.add)
            link(ins)
            link(dve.tensor_reduce(m_cmp, s_cmp, AX, ALU.max))
            link(dve.tensor_scalar(m_cmp, m_cmp, FLOOR, None, ALU.max))
            for tt in range(TT):
                ins = dve.tensor_tensor(s_cmp[:, tt, :, :], s_cmp[:, tt, :, :],
                                        m_cmp[:, tt, :].rearrange("p (h o) -> p h o", o=1).broadcast_to([P, NH, NCMP]),
                                        ALU.subtract)
            ins.then_inc(cmp_shifted, 1)
            dve.wait_ge(cmp_exp, 1)
            link(dve.tensor_reduce(d_cmp, p_cmp, AX, ALU.add))
            link(dve.tensor_scalar(d_cmp, d_cmp, 1e-30, None, ALU.max))
            link(dve.reciprocal(d_cmp, d_cmp))
            dve.wait_ge(bank_free["act", 1], plan.free_count("act", 1, plan.outputs["nsa", 5][0]))
            link(dve.tensor_tensor(w_cmp, d_cmp, gates.rearrange("p t (h b) -> p t h b", b=3)[:, :, :, 0], ALU.mult))
            if turn_reader("pc") == "dve":
                n = HG * NCMP
                await_turn(dve, "pc")
                dve.tensor_copy(p_cmpT.rearrange("p t g q -> p (t g q)")[0:n, :],
                                turn_bank("pc")[0:n, :]).then_inc(turn_read["dve"], 1)
            stream_ahead("dve", "nsa_out", 0, -1)
            for i in range(4):
                tt, g = i // 2, i % 2
                dve.wait_ge(cmp_pv_done, i + 1)
                dve.tensor_tensor(nsa_o[:, tt, HG * g:HG * g + HG, :],
                                  bank[6 + i % 2].rearrange("p (h d) -> p h d", d=DH),
                                  w_cmp[:, tt, HG * g:HG * g + HG].rearrange("p (h o) -> p h o", o=1).broadcast_to([P, HG, DH]),
                                  ALU.mult).then_inc(cmp_pv_read, 1)

            def weigh(grp):
                g, branch = grp // 2, 1 + grp % 2
                nsa_att.reciprocal(dve, grp, link)
                gt = gates.rearrange("p t (h b) -> p t h b", b=3)[:, :, HG * g:HG * g + HG, branch]
                link(dve.tensor_tensor(nsa_att.weight[:, grp, :, :], nsa_att.rden[:, grp, :, :], gt, ALU.mult))
                dve.wait_ge(nsa_att.pv_done, 8 * grp + 8)
                for tt in range(TT):
                    if grp:
                        dve.wait_ge(o_added, 2 * (grp - 1) + tt + 1)
                    ins = dve.tensor_tensor(o_part[:, tt, :, :],
                                            bank[4 + 2 * (grp % 2) + tt].rearrange("p (h d) -> p h d", d=DH),
                                            nsa_att.weight[:, grp, tt, :].rearrange("p (h o) -> p h o", o=1).broadcast_to(
                                                [P, HG, DH]), ALU.mult)
                ins.then_inc(nsa_att.pv_read, 1)

            stream_ahead("dve", "nsa_out", 0, 0)
            nsa_att.dve(dve, link, weigh, lambda i: ada_beside(9, i))
            for tt in range(TT):
                dve.wait_ge(o_added, 2 * 3 + tt + 1)
                o = nsa_o[:, tt, :, :].rearrange("p h d -> p (h d)")
                dve.tensor_tensor(o, o, z_act[:, tt, :], ALU.mult).then_inc(o_ready, 1)
            turned_left_dve(dve, "nsa_o", range(4))
            stream_ahead("dve", "nsa_out", 0)
            ada_collect_up_to(12)

        def await_rotation(act, j, tt):
            act.wait_ge(bank_free["dve", tt], plan.free_count("dve", tt, plan.outputs["nsa", j][0]))

        def nsa_act(act):
            for tt in range(TT):
                await_output(act, "nsa", 2, tt)
                await_rotation(act, 2, tt)
                act.copy(v_slc[:, tt, :, :], gemm_bank("nsa", 2, tt)[:, 3 * P:4 * P].rearrange(
                    "p (g d) -> p g d", g=G)).then_inc(bank_free["act", tt], 1)
            for tt in range(TT):
                await_output(act, "nsa", 3, tt)
                await_rotation(act, 3, tt)
                act.copy(v_win[:, tt, :, :], gemm_bank("nsa", 3, tt)[:, P:2 * P].rearrange("p (g d) -> p g d", g=G))
                act.activation(z_act[:, tt, 0:256], gemm_bank("nsa", 3, tt)[:, 256:512],
                               ACT.Silu).then_inc(bank_free["act", tt], 1)
            stream_ahead("act", "nsa", 0, 0)
            await_turn(act, "vc")
            b = turn_bank("vc")
            act.copy(vc_next[0:DH, :, :], b[0:DH, :].rearrange("p (g t) -> p g t", g=G))
            act.copy(vc_next[DH:P, :, 0:T - 1],
                     b[DH:P, :].rearrange("p (g t) -> p g t", g=G)[:, :, 1:T]).then_inc(turn_read["act"], 1)
            read_turns("act", "kw", lambda b: kwT.rearrange("p g t -> p (g t)"), [0])
            for j in range(2):
                stream_end["act"] = plan.outputs["ada", 7][1][-1]
                for tt in range(TT):
                    await_output(act, "nsa", j, tt)
                    await_rotation(act, j, tt)
                    act.copy(q_plain[:, tt, 8 * j:8 * j + 8, :], gemm_bank("nsa", j, tt).rearrange(
                        "p (h d) -> p h d", d=DH)).then_inc(bank_free["act", tt], 1)
            stream_end["act"] = None
            stream_ahead("act", "nsa", 4, 0)
            act.wait_ge(pe_units, plan.units[plan.outputs["cmp", 0][1][-1]][2] + 1)
            act.activation(hidden[0:G * NCMP, 0, :], bank[6][0:G * NCMP, 0:CMP_HIDDEN], ACT.Silu)
            act.wait_ge(pe_units, plan.units[plan.outputs["cmp", 1][1][-1]][2] + 1)
            act.activation(hidden[0:G * NCMP, 1, :], bank[7][0:G * NCMP, 0:CMP_HIDDEN],
                           ACT.Silu).then_inc(hidden_act, 1)
            for tt in range(TT):
                await_output(act, "nsa", 4, tt)
                act.activation(z_act[:, tt, 256:768], gemm_bank("nsa", 4, tt)[:, :],
                               ACT.Silu).then_inc(bank_free["act", tt], 1)
            stream_ahead("act", "nsa", 5, 0)
            read_turns("act", "qp", lambda b: qpT[:, 2 * b:2 * b + 2, :].rearrange("p c t -> p (c t)"), range(4))
            read_turns("act", "qr", lambda b: qrT[:, 2 * b:2 * b + 2, :].rearrange("p c t -> p (c t)"), range(4))
            for tt in range(TT):
                await_output(act, "nsa", 5, tt)
                act.activation(z_act[:, tt, 768:1024], gemm_bank("nsa", 5, tt)[:, 0:256], ACT.Silu)
            for tt in range(TT):
                act.activation(gates[:, tt, :], gemm_bank("nsa", 5, tt)[:, 256:304],
                               ACT.Sigmoid).then_inc(bank_free["act", tt], 1)
            act.wait_ge(cmp_shifted, 1)
            act.activation(p_cmp, s_cmp, ACT.Exp, scale=SCALE).then_inc(cmp_exp, 1)
            stream_ahead("act", "nsa_out", 0, -1)
            if turn_reader("pc") == "act":
                n = HG * NCMP
                await_turn(act, "pc")
                act.copy(p_cmpT.rearrange("p t g q -> p (t g q)")[0:n, :],
                         turn_bank("pc")[0:n, :]).then_inc(turn_read["act"], 1)
            stream_ahead("act", "nsa_out", 0, 0)
            nsa_att.act(act)
            turned_left_act(act, "nsa_o", range(4))

        def nsa_pool(pool):
            rope_add(pool, ("nsa", 2), lambda tt: [ks2[:, tt, :, 0, :], ks2[:, tt, :, 1, :]], G)
            rope_add(pool, ("nsa", 3), lambda tt: [kw2[:, tt, :, 0, :], kw2[:, tt, :, 1, :]], G)
            rope_add(pool, ("nsa", 0), lambda tt: [q_rope[:, tt, 0:8, :]], 8)
            stream_end["pool"] = plan.outputs["ada", 7][1][-1]
            rope_add(pool, ("nsa", 1), lambda tt: [q_rope[:, tt, 8:16, :]], 8)
            stream_end["pool"] = None
            stream_ahead("pool", "nsa", 5, 0)
            pool.wait_ge(cmp_pv_read, 4)
            for grp in range(4):
                pool.wait_ge(nsa_att.pv_read, grp + 1)
                for tt in range(TT):
                    o = nsa_o[:, tt, HG * (grp // 2):HG * (grp // 2) + HG, :]
                    if grp % 2:
                        pool.wait_ge(o_added, 2 * (grp - 1) + tt + 1)
                    pool.tensor_tensor(o, o, o_part[:, tt, :, :], ALU.add).then_inc(o_added, 1)
            residual_pool(pool, 0)

        def nsa_pe(pe):
            def project(j, n=512):
                gemm(pe, "nsa", j, from_lhs, "norm0", n)

            project(2)
            ada_sum(pe, 4)
            project(3)
            ada_sum(pe, 5)
            o2 = plan.outputs["nsa", 2][0]
            for tt in range(TT):
                pe.wait_ge(bank_free["dve", tt], plan.free_count("dve", tt, o2))
            for name, src in (("kc", kc2), ("vc", vc2), ("ks", ks2), ("kw", kw2)):
                if name == "ks":
                    pe.wait_ge(rope_done, 2)
                if name == "kw":
                    pe.wait_ge(rope_done, 4)
                turn(pe, name, 0, [(src[:, tt, g, :, :].rearrange("p a d -> p (a d)"), P, P, g * T + tt * P)
                                   for g in range(G) for tt in range(TT)])
            project(0)
            ada_sum(pe, 6)
            project(1)
            ada_sum(pe, 7)
            for kv in range(2):
                pe.wait_ge(blocks_ready, kv + 1)
                if kv == 0:
                    pe.wait_ge(mod_ready, 8)
                for u, unit in enumerate(plan.outputs["cmp", kv][1]):
                    await_unit(pe, unit)
                    for k in range(2 * CHUNKS):
                        j = 2 * CHUNKS * u + k
                        mm = pe.matmul(bank[6 + kv][0:G * NCMP, 0:CMP_HIDDEN],
                                       blocks[:, kv, j, :, :].rearrange("p g n -> p (g n)"),
                                       ring[:, unit % RING, k * 256:(k + 1) * 256], start=(j == 0), stop=(j == 15))
                    mm.then_inc(pe_units, 1)
            project(4)
            n = G * NCMP
            pe.wait_ge(hidden_act, 1)
            turn(pe, "hid", 0, [(hidden[0:n, kv, c * P:(c + 1) * P], n, P, (2 * kv + c) * n)
                                for kv in range(2) for c in range(2)])
            pe.wait_ge(w2_in, 48)
            await_turns_read(pe, "hid", [0])
            for c in range(2):
                pe.matmul(bank[6][:, 256:256 + n], w2k[:, c, :, :].rearrange("p a d -> p (a d)"), hidT[:, 0, c, :],
                          start=(c == 0), stop=(c == 1))
            for g in range(G):
                for c in range(2):
                    mm = pe.matmul(bank[7][0:HG * NCMP, 256 + g * DH:256 + (g + 1) * DH],
                                   hid_rep[:, c, g, :, :].rearrange("p h n -> p (h n)"), w2v[:, c, :],
                                   start=(c == 0), stop=(c == 1))
            mm.then_inc(cmp_kv_done, 1)
            pe.wait_ge(cmp_kv_read, 1)
            ada_sum(pe, 8)
            o1 = plan.outputs["nsa", 1][0]
            for tt in range(TT):
                pe.wait_ge(bank_free["act", tt], plan.free_count("act", tt, o1))
            turn_tokens(pe, "qp", lambda tt, c: q_plain[:, tt, 2 * c:2 * c + 2, :].rearrange("p h d -> p (h d)"), range(4))
            pe.wait_ge(rope_done, 8)
            turn_tokens(pe, "qr", lambda tt, c: q_rope[:, tt, 2 * c:2 * c + 2, :].rearrange("p h d -> p (h d)"), range(4))
            project(5, 304)
            await_turns_read(pe, "qp", range(4))
            pe.wait_ge(mod_ready, 9)
            for tt in range(TT):
                for h in range(NH):
                    g = h // HG
                    at = (tt * HG + h // 2) * NCMP
                    mm = pe.matmul(bank[6 + h % 2][:, at:at + NCMP],
                                   qpT[head_rows(h), h // 2, tt * P:(tt + 1) * P],
                                   k_cmpT[head_rows(h), g * NCMP:(g + 1) * NCMP], start=True, stop=True)
            mm.then_inc(cmp_scored, 1)
            pe.wait_ge(cmp_exp, 1)
            turn(pe, "pc", 0, [(p_cmp[:, tt, HG * g:HG * g + HG, :].rearrange("p h n -> p (h n)"), P, HG * NCMP,
                                (2 * tt + g) * P) for tt in range(TT) for g in range(G)])
            await_turns_read(pe, "pc", [0])
            for i in range(4):
                tt, g = i // 2, i % 2
                if i >= 2:
                    pe.wait_ge(cmp_pv_read, i - 1)
                pe.matmul(bank[6 + i % 2][:, :], p_cmpT[0:HG * NCMP, tt, g, :],
                          v_blocks[0:HG * NCMP, g, :, :].rearrange("p h d -> p (h d)"),
                          start=True, stop=True).then_inc(cmp_pv_done, 1)
            await_turns_read(pe, "qr", range(4))
            o5 = plan.outputs["nsa", 5][0]
            for o in (o5 - 1, o5):
                for tt in range(TT):
                    pe.wait_ge(bank_free["act", tt], plan.free_count("act", tt, o))
            pe.wait_ge(cmp_pv_read, 4)
            nsa_att.pe(pe)
            pe.wait_ge(o_ready, 2)
            turn_tokens(pe, "nsa_o", lambda tt, c: nsa_o[:, tt, 2 * c:2 * c + 2, :].rearrange("p h d -> p (h d)"), range(4))
            gemm(pe, "nsa_out", 0, from_lhs, "nsa_o", 512)
            for n in range(9, 12):
                ada_sum(pe, n)
            gemm(pe, "nsa_out", 1, from_lhs, "nsa_o", 512)

        dil = Space(nsa_rope_end)
        dil_q, dil_k, dil_v = [dil.take(TT, NH, DH) for _ in range(3)]
        dil_z = dil.take(TT, D)
        dil_qT, dil_kT = dil.take(KC, T), dil.take(KC, T)
        dil_o = dil.take(TT, NH, DH)
        lse, lse_e = dil.take(TT, NH), dil.take(TT, NH)
        lse_top, lse_sum, alpha_den = [dil.take(TT) for _ in range(3)]
        alpha = dil.take(TT, 3)

        def dil_mask(h):
            kind = [m for a, b, m in DIL_MASK if a <= h < b][0]
            return C(f"mask_{kind}")

        def dil_item(h):
            return (lambda tt: dil_qT[head_rows(h), h // 2, tt * P:(tt + 1) * P],
                    lambda: dil_kT[head_rows(h), h // 2, :], dil_mask(h), lambda kt: dil_v[:, kt, h, :])

        dil_att = Attention("dil_att", Space(0), [dil_item(h) for h in range(NH)])
        lse_ln, lse_shifted, lse_exp = sem("lse_ln"), sem("lse_shifted"), sem("lse_exp")
        log_den = dil.take(NH, TT)

        def dil_dve(dve, link):
            for j in range(4):
                rope_parts(dve, ("dil", j), lambda tt: gemm_bank("dil", j, tt)[:, :], 8)
                if j:
                    ada_collect_up_to(12 + j)
            stream_ahead("dve", "dil", 4)
            read_turns("dve", "dil_q", lambda b: dil_qT[:, 2 * b:2 * b + 2, :].rearrange("p c t -> p (c t)"), range(4))
            stream_ahead("dve", "dil", 5)
            read_turns("dve", "dil_k", lambda b: dil_kT[:, 2 * b:2 * b + 2, :].rearrange("p c t -> p (c t)"), range(4))
            stream_ahead("dve", "dil_out", 0, 0)
            ada_collect_up_to(18)

            def weigh(grp):
                dil_att.reciprocal(dve, grp, link)
                dve.wait_ge(dil_att.pv_done, 8 * grp + 8)
                for tt in range(TT):
                    ins = dve.tensor_tensor(dil_o[:, tt, 8 * grp:8 * grp + 8, :],
                                            bank[4 + 2 * (grp % 2) + tt].rearrange("p (h d) -> p h d", d=DH),
                                            dil_att.rden[:, grp, tt, :].rearrange("p (h o) -> p h o", o=1).broadcast_to(
                                                [P, HG, DH]), ALU.mult)
                ins.then_inc(dil_att.pv_read, 1)

            dil_att.dve(dve, link, weigh, lambda i: ada_beside(18, i))
            dve.wait_ge(lse_ln, 1)
            link(dve.tensor_tensor(lse, log_den.rearrange("p h t -> p t h"),
                                   dil_att.bias.rearrange("p h t -> p t h"), ALU.subtract))
            link(dve.tensor_reduce(lse_top, lse, AX, ALU.max))
            dve.tensor_tensor(lse, lse, lse_top.rearrange("p (t o) -> p t o", o=1).broadcast_to([P, TT, NH]),
                              ALU.subtract).then_inc(lse_shifted, 1)
            dve.wait_ge(lse_exp, 1)
            for i, (a, b, _) in enumerate(DIL_MASK):
                ins = dve.tensor_reduce(alpha[:, :, i:i + 1], lse_e[:, :, a:b], AX, ALU.add)
            link(ins)
            for i, (a, b, _) in enumerate(DIL_MASK):
                ins = dve.tensor_scalar(alpha[:, :, i:i + 1], alpha[:, :, i:i + 1], 1.0 / (b - a), None, ALU.mult)
            link(ins)
            link(dve.tensor_reduce(lse_sum, alpha, AX, ALU.add))
            link(dve.reciprocal(alpha_den, lse_sum))
            link(dve.tensor_scalar(alpha_den, alpha_den, float(len(DIL_MASK)), None, ALU.mult))
            link(dve.tensor_tensor(alpha, alpha, alpha_den.rearrange("p (t o) -> p t o", o=1).broadcast_to([P, TT, 3]),
                                   ALU.mult))
            for tt in range(TT):
                dve.wait_ge(dil_att.pv_read, 2)
                for i, (a, b, _) in enumerate(DIL_MASK):
                    o = dil_o[:, tt, a:b, :].rearrange("p h d -> p (h d)")
                    ins = dve.scalar_tensor_tensor(o, o, alpha[:, tt, i:i + 1], dil_z[:, tt, a * DH:b * DH],
                                                   ALU.mult, ALU.mult)
                ins.then_inc(o_ready, 1)
            turned_left_dve(dve, "dil_o", range(4))

        def dil_act(act):
            for j in (4, 5, 6, 7):
                for tt in range(TT):
                    await_output(act, "dil", j, tt)
                    if j < 6:
                        act.copy(dil_v[:, tt, 8 * (j - 4):8 * (j - 4) + 8, :], gemm_bank("dil", j, tt).rearrange(
                            "p (h d) -> p h d", d=DH)).then_inc(bank_free["act", tt], 1)
                    else:
                        act.activation(dil_z[:, tt, 512 * (j - 6):512 * (j - 6) + 512], gemm_bank("dil", j, tt)[:, :],
                                       ACT.Silu).then_inc(bank_free["act", tt], 1)
                if j == 4:
                    read_turns("act", "dil_q", lambda b: dil_qT[:, 2 * b:2 * b + 2, :].rearrange("p c t -> p (c t)"), range(4))
                if j == 5:
                    read_turns("act", "dil_k", lambda b: dil_kT[:, 2 * b:2 * b + 2, :].rearrange("p c t -> p (c t)"), range(4))
            stream_ahead("act", "dil_out", 0, 0)
            dil_att.act(act)
            act.wait_ge(dil_att.exp_done, NH)
            act.activation(log_den, dil_att.den, ACT.Ln).then_inc(lse_ln, 1)
            act.wait_ge(lse_shifted, 1)
            act.activation(lse_e, lse, ACT.Exp).then_inc(lse_exp, 1)
            turned_left_act(act, "dil_o", range(4))

        def dil_pool(pool):
            for j, d in enumerate((dil_q, dil_q, dil_k, dil_k)):
                rope_add(pool, ("dil", j), lambda tt: [d[:, tt, 8 * (j % 2):8 * (j % 2) + 8, :]], 8)
            stream_ahead("pool", "dil", 7, 0)
            residual_pool(pool, 1)

        def dil_pe(pe):
            for j in range(8):
                gemm(pe, "dil", j, from_lhs, "norm1", 512)
                if j < 6:
                    ada_sum(pe, 12 + j)
                if j == 4:
                    pe.wait_ge(rope_done, 12)
                    turn_tokens(pe, "dil_q", lambda tt, c: dil_q[:, tt, 2 * c:2 * c + 2, :].rearrange("p h d -> p (h d)"), range(4))
                if j == 5:
                    pe.wait_ge(rope_done, 16)
                    turn_tokens(pe, "dil_k", lambda tt, c: dil_k[:, tt, 2 * c:2 * c + 2, :].rearrange("p h d -> p (h d)"), range(4))
            await_turns_read(pe, "dil_k", range(4))
            pe.wait_ge(mod_ready, 18)
            o7 = plan.outputs["dil", 7][0]
            for tt in range(TT):
                pe.wait_ge(bank_free["act", tt], plan.free_count("act", tt, o7))
            dil_att.pe(pe)
            pe.wait_ge(o_ready, 4)
            turn_tokens(pe, "dil_o", lambda tt, c: dil_o[:, tt, 2 * c:2 * c + 2, :].rearrange("p h d -> p (h d)"), range(4))
            for j in range(2):
                gemm(pe, "dil_out", j, from_lhs, "dil_o", 512)


        silu_done, h_ready = sem("silu_done"), sem("h_ready")
        ffn = Space(0)
        up_a, up_h = ffn.take(2, TT, 256), ffn.take(2, TT, 256)
        assert ffn.at <= UP_AT and UP_AT + 2 * FC * T <= ARENA

        def up_pair(b):
            return [u[:, 2 * b:2 * b + 2, :].rearrange("p c t -> p (c t)") for u in (up_hi, up_lo)]
        FFN_AT = {"ffn1": 0, "ffn2": 1}

        def ffn_dve(dve, name, layer, adas=()):
            base = 2 * FFN_OUTS * FFN_AT[name]
            for j in range(FFN_OUTS + 1):
                if j < FFN_OUTS:
                    stream_ahead("dve", name + "_up", j)
                    for tt in range(TT):
                        dve.wait_ge(silu_done, base + 2 * j + tt + 1)
                        if j >= 2:
                            await_turn(dve, name + "_h", j - 2)
                        dve.tensor_tensor(up_h[:, j % 2, tt, :], up_a[:, j % 2, tt, :],
                                          gemm_bank(name + "_up", j, tt)[:, 256:512],
                                          ALU.mult).then_inc(bank_free["dve", tt], 1)
                if 0 <= j - 1 < len(adas):
                    ada_collect_up_to(adas[j - 1] + 1)
                if j >= 1:
                    turned_left_dve(dve, name + "_h", [j - 1], up_pair)
            if adas:
                ada_collect_up_to(adas[-1] + 1)
            residual_dve(dve, layer, name + "_down")

        def ffn_act(act, name):
            for j in range(FFN_OUTS + 1):
                if j < FFN_OUTS:
                    for tt in range(TT):
                        await_output(act, name + "_up", j, tt)
                        act.activation(up_a[:, j % 2, tt, :], gemm_bank(name + "_up", j, tt)[:, 0:256],
                                       ACT.Silu).then_inc(silu_done, 1)
                if j >= 1:
                    turned_left_act(act, name + "_h", [j - 1], up_pair)

        def ffn_pe(pe, name, norm, adas=()):
            for j in range(FFN_OUTS + 1):
                if j < FFN_OUTS:
                    gemm(pe, name + "_up", j, from_lhs, norm, 512)
                if j < len(adas):
                    ada_sum(pe, adas[j])
                if j >= 1:
                    o = plan.outputs[name + "_up", j - 1][0]
                    for tt in range(TT):
                        pe.wait_ge(bank_free["dve", tt], plan.free_count("dve", tt, o))
                    turn(pe, name + "_h", j - 1, [(up_h[:, (j - 1) % 2, tt, h * P:(h + 1) * P], P, P, h * T + tt * P)
                                                  for h in range(2) for tt in range(TT)])
            for j in range(2):
                gemm(pe, name + "_down", j, lambda k, tt: [u[:, k, tt * P:(tt + 1) * P] for u in (up_hi, up_lo)],
                     name + "_h", 512, kc_total=FC)

        mix = Space(0)
        qkT = mix.take(2 * DN_HEADS, T)
        under_z = Space(mix.at)
        z_gain = mix.take(TT, D)
        sig = mix.take(TT, 2, D)
        beta = mix.take(TT, 2 * DN_HEADS)
        beta_k = mix.take(TT, 2 * DN_HEADS)
        g_log = mix.take(TT, 2 * DN_HEADS)
        sp_x, sp_abs, sp_e, sp_u, sp_l = [mix.take(TT, 2 * DN_HEADS) for _ in range(5)]
        head_row = mix.take(4 * DN_HEADS)
        a_rate = mix.take(2 * DN_HEADS)
        dn_gain = mix.take(P)
        g_in = mix.take(TT, 2 * DN_HEADS)
        g_cum = mix.take(TT, 2 * DN_HEADS)
        g_off = mix.take(2 * DN_HEADS)
        g_rows = mix.take(T)
        qk_sum = mix.take(2, TT, DN_HEADS)
        k_len = mix.take(TT, DN_HEADS)
        q_scale = mix.take(TT, DN_HEADS)
        y_ss, y_ms, y_r = [mix.take(DN_HEADS, TT) for _ in range(3)]
        early = Space(mix.at)
        early_at = early.at = -(-early.at // 8) * 8
        tok = early.take(2, TT, 512)
        padded = early.take(2, 2, T + 4)
        conv_acc = early.take(2, 2, T)
        vT = early.take(DN_HEADS, T)
        sq = early.take(2, 2, T)
        ca_b, ca_c = under_z.take(TT, CONV_A), under_z.take(TT, CONV_A)
        pad_a = early.take(CONV_A // P, T + 2)
        acc_a = early.take(CONV_A // P, T)
        y_a_hi, y_a_lo = [nc.alloc_sbuf_tensor_at(name, [P, CONV_A // P, T], F32R,
                                                  offset=arena_at + 4 * (early_at + i * CONV_A // P * T))
                          for i, name in enumerate(("y_a_hi", "y_a_lo"))]

        def y_a_pair(b):
            return [y[:, 2 * b:2 * b + 2, :].rearrange("p c t -> p (c t)") for y in (y_a_hi, y_a_lo)]

        def y_a_chunks(b):
            return acc_a[:, 2 * b:2 * b + 2, :].rearrange("p c t -> p (c t)")
        v_hat = xn.rearrange("p t (h d) -> p t h d", h=DN_HEADS)
        y_b = qkT[:, 0:DN_HEADS, :].rearrange("p h (t d) -> p t h d", t=TT)

        pads_ready = sem("pads_ready")
        rows_in = sem("rows_in")
        rate_ready, z_ready, z_gained = sem("rate_ready"), sem("z_ready"), sem("z_gained")
        conv_done, qkv_ready = sem("conv_done"), sem("qkv_ready")
        sq_ready, qk_summed_pair, qk_sum_read = sem("sq_ready"), sem("qk_summed_pair"), sem("qk_sum_read")
        k_len_ready = sem("k_len_ready")
        sp_ready, sp_exp, sp_sum, sp_ln = sem("sp_ready"), sem("sp_exp"), sem("sp_sum"), sem("sp_ln")
        g_ready, g_summed, g_cum_ready = sem("g_ready"), sem("g_summed"), sem("g_cum_ready")
        a_merged, b_gated, merged_ready = sem("a_merged"), sem("b_gated"), sem("merged_ready")

        def padded_out(b):
            return padded[:, b % 2, :, 2:T + 2]

        def mix_conv(dve, b, link):
            p = padded[:, b % 2, :, :]
            await_turns_read(dve, "qkv", [b])
            if b >= 2:
                dve.wait_ge(qkv_ready, b - 1)
            for tap in range(5):
                for h in range(2):
                    c = 2 * b + h
                    w = cols[:, 1, tap * (QKV // P) + c:tap * (QKV // P) + c + 1]
                    a, src = conv_acc[:, b % 2, h, :], p[:, h, tap:tap + T]
                    if tap == 0:
                        ins = dve.tensor_scalar(a, src, w, None, ALU.mult)
                    else:
                        ins = dve.scalar_tensor_tensor(a, src, w, a, ALU.mult, ALU.add)
                if tap < 4:
                    link(ins)
            ins.then_inc(conv_done, 1)

        def qkv_silu(act, b):
            act.wait_ge(conv_done, b + 1)
            dst = qkT[:, 2 * b:2 * b + 2, :] if b < 8 else vT[:, 2 * b - 16:2 * b - 14, :]
            act.activation(dst, conv_acc[:, b % 2, :, :], ACT.Silu).then_inc(qkv_ready, 1)

        def copy_padded(who, b):
            if turn_reader("qkv", b) == who:
                eng = ENG[who]
                await_turn(eng, "qkv", b)
                if b >= 2:
                    eng.wait_ge(conv_done, b - 1)
                copy(eng, padded_out(b), turn_bank("qkv", b).rearrange("p (h t) -> p h t", h=2)).then_inc(turn_read[who], 1)

        def mix_dve(dve, link):
            dve.memset(padded, 0.0)
            dve.memset(pad_a, 0.0).then_inc(pads_ready, 1)
            dve.wait_ge(pads_ready, 1)
            dve.wait_ge(rate_ready, 1)
            stream_end["dve"] = plan.outputs["a_out", 1][1][-1]
            for b in range(12):
                after = ("qkv", b // 2 + 1) if b < 10 else ("ba", 0)
                stream_ahead("dve", *after)
                copy_padded("dve", b)
                await_turn(dve, "qkv", b)
                stream_ahead("dve", *after, 2)
                mix_conv(dve, b, link)
                if b == 9:
                    for tt in range(TT):
                        await_output(dve, "ba", 0, tt)
                        dve.tensor_tensor(sp_x[:, tt, :], gemm_bank("ba", 0, tt)[:, 16:32], head_row[:, 16:32],
                                          ALU.add).then_inc(bank_free["dve", tt], 1)
                    for tt in range(TT):
                        dve.wait_ge(bank_free["dve", tt], plan.free_count("dve", tt, plan.outputs["ba", 0][0]))
                    dve.scalar_tensor_tensor(sp_abs, sp_x, -1.0, sp_x, ALU.mult, ALU.max).then_inc(sp_ready, 1)
            stream_ahead("dve", "ca", 0)
            dve.wait_ge(sp_exp, 1)
            dve.tensor_scalar(sp_u, sp_e, 1.0, None, ALU.add).then_inc(sp_sum, 1)
            dve.wait_ge(sp_sum, 1)
            link(dve.tensor_scalar(sp_abs, sp_u, -1.0, None, ALU.add))
            link(dve.tensor_tensor(sp_e, sp_e, sp_abs, ALU.subtract))
            dve.wait_ge(sp_ln, 1)
            link(dve.reciprocal(sp_u, sp_u))
            link(dve.tensor_tensor(sp_e, sp_e, sp_u, ALU.mult))
            link(dve.tensor_tensor(sp_l, sp_l, sp_e, ALU.add))
            link(dve.scalar_tensor_tensor(sp_l, sp_x, 0.0, sp_l, ALU.max, ALU.add))
            for tt in range(TT):
                ins = dve.scalar_tensor_tensor(g_log[:, tt, :], sp_l[:, tt, :], -1.0, a_rate, ALU.mult, ALU.mult)
            ins.then_inc(g_ready, 1)
            for tt in range(TT):
                await_output(dve, "ca", 2, tt)
                dve.wait_ge(bank_free["act", tt], plan.free_count("act", tt, plan.outputs["ca", 1][0]))
                dve.tensor_tensor(ca_c[:, tt, :], ca_c[:, tt, :], gemm_bank("ca", 2, tt)[:, :],
                                  ALU.mult).then_inc(bank_free["dve", tt], 1)
            dve.wait_ge(qk_summed_pair, 8)
            dve.tensor_scalar(qk_sum.rearrange("p a t h -> p (a t h)"), bank[7][:, 0:32], EPS, None,
                              ALU.add).then_inc(qk_sum_read, 1)
            dve.wait_ge(g_summed, 1)
            dve.tensor_copy(g_cum.rearrange("p t c -> p (t c)"), bank[6][:, 0:32])
            dve.tensor_scalar(g_in.rearrange("p t c -> p (t c)"), bank[6][:, 0:32], -1.0, None, ALU.mult)
            dve.tensor_copy(g_off, bank[6][:, 32:48]).then_inc(g_cum_ready, 1)
            dve.wait_ge(qk_sum_read, 1)
            link(dve.reciprocal(beta_k[:, :, 0:8], qk_sum[:, 1, :, :]))
            o = plan.outputs["ba", 0][0]
            for tt in range(TT):
                dve.wait_ge(bank_free["act", tt], plan.free_count("act", tt, o))
            link(dve.tensor_tensor(beta_k[:, :, 8:16], beta_k[:, :, 0:8], beta[:, :, 8:16], ALU.mult))
            link(dve.tensor_tensor(beta_k[:, :, 0:8], beta_k[:, :, 0:8], beta[:, :, 0:8], ALU.mult))
            for b in range(2):
                if turn_reader("prod", b) == "dve":
                    await_turn(dve, "prod", b)
                    dve.tensor_copy(pad_a[:, 2 * b:2 * b + 2, 1:T + 1],
                                    turn_bank("prod", b).rearrange("p (h t) -> p h t", h=2)).then_inc(turn_read["dve"], 1)
            await_turns_read(dve, "prod", range(2))
            for tap in range(3):
                for c in range(4):
                    w = cols[:, 0, 88 + 4 * tap + c:89 + 4 * tap + c]
                    a, src = acc_a[:, c, :], pad_a[:, c, tap:tap + T]
                    if tap == 0:
                        ins = dve.tensor_scalar(a, src, w, None, ALU.mult)
                    else:
                        ins = dve.scalar_tensor_tensor(a, src, w, a, ALU.mult, ALU.add)
                link(ins)
            for b in range(2):
                await_turn(dve, "cab", b)
                dve.tensor_tensor(y_a_chunks(b), y_a_chunks(b), turn_bank("cab", b),
                                  ALU.mult).then_inc(turn_read["dve"], 1)
            stream_ahead("dve", "z", 0)
            for b in range(2):
                left_rest(dve, "y_a", b, y_a_chunks(b), y_a_pair)
            dve.wait_ge(k_len_ready, 2)
            for b in range(4):
                tt, hh = b // 2, 4 * (b % 2)
                await_turn(dve, "v", b)
                if turn_reader("v", b) == "act":
                    await_turns_read(dve, "v", [b])
                    src = v_hat[:, tt, hh:hh + 4, :]
                else:
                    src = turn_bank("v", b).rearrange("p (h d) -> p h d", h=4)
                ins = dve.tensor_tensor(v_hat[:, tt, hh:hh + 4, :], src,
                                        k_len[:, tt, hh:hh + 4].rearrange("p (h o) -> p h o", o=1).broadcast_to([P, 4, DN_D]),
                                        ALU.mult)
                if turn_reader("v", b) == "dve":
                    ins.then_inc(turn_read["dve"], 1)
                else:
                    link.mark(ins)
            stream_ahead("dve", "a_out", 0, 0)
            ada_collect_up_to(30)
            for j in range(2):
                for tt in range(TT):
                    await_output(dve, "a_out", j, tt)
                    s = sig[:, tt, 0, 512 * j:512 * (j + 1)]
                    dve.tensor_tensor(s, s, gemm_bank("a_out", j, tt)[:, :], ALU.mult).then_inc(bank_free["dve", tt], 1)
            delta_dve(dve, link)
            stream_end["dve"] = None
            for half in range(2):
                stream_ahead("dve", "b_out", 0, half - 1)
                turned_left_dve(dve, "y_b", (2 * half, 2 * half + 1))
            for j in range(2):
                for tt in range(TT):
                    await_output(dve, "b_out", j, tt)
                    s = sig[:, tt, 1, 512 * j:512 * (j + 1)]
                    dve.tensor_tensor(s, s, gemm_bank("b_out", j, tt)[:, :], ALU.mult).then_inc(bank_free["dve", tt], 1)
            for half in range(2):
                stream_ahead("dve", "mix_out", 0, half - 1)
                turned_left_dve(dve, "merged", (2 * half, 2 * half + 1))
            residual_dve(dve, 3, "mix_out")

        def read_rows(who):
            if turn_reader("grow") == who:
                await_turn(ENG[who], "grow")
                copy(ENG[who], g_rows[0:16, :], turn_bank("grow")[0:16, 0:T]).then_inc(turn_read[who], 1)

        def mix_act(act):
            act.wait_ge(rows_in, 16 * 5)
            act.activation(a_rate, head_row[:, 0:16], ACT.Exp).then_inc(rate_ready, 1)
            act.wait_ge(pads_ready, 1)
            stream_end["act"] = plan.outputs["a_out", 1][1][-1]
            for b in range(12):
                if b % 2 == 0:
                    for tt in range(TT):
                        await_output(act, "qkv", b // 2, tt)
                        if b >= 4:
                            await_turn(act, "qkv", b - 3)
                        act.copy(tok[:, (b // 2) % 2, tt, :], gemm_bank("qkv", b // 2, tt)[:, :]).then_inc(
                            bank_free["act", tt], 1)
                    stream_ahead("act", "qkv", b // 2, 2)
                if b >= 2:
                    copy_or_silu_act(act, b - 2)
            stream_ahead("act", "ba", 0, 2)
            copy_or_silu_act(act, 10)
            copy_or_silu_act(act, 11)
            o = plan.outputs["ba", 0][0]
            for tt in range(TT):
                act.wait_ge(bank_free["dve", tt], plan.free_count("dve", tt, o))
                act.activation(beta[:, tt, :], gemm_bank("ba", 0, tt)[:, 0:16], ACT.Sigmoid)
                act.activation(sig[:, tt, 0, 0:GATE_W - 32], gemm_bank("ba", 0, tt)[:, 32:GATE_W],
                               ACT.Sigmoid).then_inc(bank_free["act", tt], 1)
            for tt in range(TT):
                await_output(act, "ca", 0, tt)
                act.copy(ca_b[:, tt, :], gemm_bank("ca", 0, tt)[:, :]).then_inc(bank_free["act", tt], 1)
            act.wait_ge(sp_ready, 1)
            act.activation(sp_e, sp_abs, ACT.Exp, scale=-1.0).then_inc(sp_exp, 1)
            act.wait_ge(sp_sum, 1)
            act.activation(sp_l, sp_u, ACT.Ln).then_inc(sp_ln, 1)
            for tt in range(TT):
                await_output(act, "ca", 1, tt)
                act.copy(ca_c[:, tt, :], gemm_bank("ca", 1, tt)[:, :]).then_inc(bank_free["act", tt], 1)
            stream_ahead("act", "ca", 2)
            for p in range(8):
                act.wait_ge(qkv_ready, 8)
                if p >= 2:
                    act.wait_ge(qk_summed_pair, p - 1)
                act.activation(sq[:, p % 2, :, :], qkT[:, 2 * p:2 * p + 2, :], ACT.Square).then_inc(sq_ready, 1)
            for b in range(2):
                if turn_reader("prod", b) == "act":
                    await_turn(act, "prod", b)
                    act.copy(pad_a[:, 2 * b:2 * b + 2, 1:T + 1],
                             turn_bank("prod", b).rearrange("p (h t) -> p h t", h=2)).then_inc(turn_read["act"], 1)
            for tt in range(TT):
                await_output(act, "z", 0, tt)
                act.activation(z_gain[:, tt, 0:512], gemm_bank("z", 0, tt)[:, :], ACT.Silu).then_inc(bank_free["act", tt], 1)
            for b in range(2):
                await_turns_read(act, "cab", [b])
                left_round(act, y_a_chunks(b), y_a_pair(b)[0])
            read_turns("act", "v", lambda b: v_hat[:, b // 2, 4 * (b % 2):4 * (b % 2) + 4, :].rearrange("p h d -> p (h d)"), range(4))
            read_rows("act")
            for tt in range(TT):
                await_output(act, "z", 1, tt)
                act.activation(z_gain[:, tt, 512:1024], gemm_bank("z", 1, tt)[:, :], ACT.Silu).then_inc(bank_free["act", tt], 1)
            sig_all = sig.rearrange("p t g d -> p t (g d)")
            for j in range(4):
                at = GATE_W * (j + 1) - 32
                for tt in range(TT):
                    await_output(act, "gate", j, tt)
                    act.activation(sig_all[:, tt, at:at + GATE_W], gemm_bank("gate", j, tt)[:, 0:GATE_W],
                                   ACT.Sigmoid).then_inc(bank_free["act", tt], 1)
            stream_ahead("act", "a_out", 1)
            delta_act(act)
            act.wait_ge(d["y"], 2 * DN_HEADS)
            stream_end["act"] = None
            for half in range(2):
                stream_ahead("act", "b_out", 0, half - 1)
                turned_left_act(act, "y_b", (2 * half, 2 * half + 1))
            for half in range(2):
                stream_ahead("act", "mix_out", 0, half - 1)
                turned_left_act(act, "merged", (2 * half, 2 * half + 1))

        def copy_or_silu_act(act, b):
            copy_padded("act", b)
            qkv_silu(act, b)

        def mix_pool(pool):
            pool.wait_ge(qk_sum_read, 1)
            n = TT * DN_HEADS
            qs = q_scale.rearrange("p t h -> p (t h)")
            pool.tensor_scalar(qs, qk_sum[:, 0, :, :].rearrange("p t h -> p (t h)"), float(DN_D), None,
                               ALU.mult).then_inc(k_len_ready, 1)
            pool.tensor_tensor(k_len.rearrange("p t h -> p (t h)"), qk_sum[:, 1, :, :].rearrange("p t h -> p (t h)"),
                               C("half").broadcast_to([P, n]), ALU.pow).then_inc(k_len_ready, 1)
            pool.wait_ge(k_len_ready, 2)
            pool.tensor_tensor(qs, qs, C("minus_half").broadcast_to([P, n]), ALU.pow).then_inc(k_len_ready, 1)
            o = plan.outputs["z", 1][0]
            for tt in range(TT):
                pool.wait_ge(bank_free["act", tt], plan.free_count("act", tt, o))
                z = z_gain[:, tt, :].rearrange("p (h d) -> p h d", h=DN_HEADS)
                pool.tensor_tensor(z, z, dn_gain.rearrange("p (o d) -> p o d", o=1).broadcast_to([P, DN_HEADS, DN_D]),
                                   ALU.mult).then_inc(z_gained, 1)
            delta_pool(pool)
            for j in range(2):
                for tt in range(TT):
                    o = plan.outputs["b_out", j][0]
                    pool.wait_ge(bank_free["dve", tt], plan.free_count("dve", tt, o))
                    a = sig[:, tt, 0, 512 * j:512 * (j + 1)]
                    pool.tensor_tensor(a, a, sig[:, tt, 1, 512 * j:512 * (j + 1)], ALU.add).then_inc(merged_ready, 1)
            residual_pool(pool, 3)

        def mix_pe(pe):
            def qkv_turns(j):
                o = plan.outputs["qkv", j][0]
                for tt in range(TT):
                    pe.wait_ge(bank_free["act", tt], plan.free_count("act", tt, o))
                for b in (2 * j, 2 * j + 1):
                    turn(pe, "qkv", b, [(tok[:, j % 2, tt, (2 * (b % 2) + h) * P:(2 * (b % 2) + h + 1) * P], P, P,
                                         h * T + tt * P) for h in range(2) for tt in range(TT)])
            for j in range(6):
                gemm(pe, "qkv", j, from_lhs, "norm3", 512)
                if j:
                    qkv_turns(j - 1)
            gemm(pe, "ba", 0, from_lhs, "norm3", GATE_W)
            qkv_turns(5)
            for j in range(3):
                gemm(pe, "ca", j, from_lhs, "norm3", 512)
            pe.wait_ge(g_ready, 1)
            pe.wait_ge(mod_ready, 24)
            for tt in range(TT):
                for d, m in ((0, "cum_fwd"), (1, "cum_bwd")):
                    pe.matmul(bank[6][:, tt * 16 + d * 8:tt * 16 + d * 8 + 8], C(m), g_log[:, tt, d * 8:d * 8 + 8],
                              start=True, stop=True)
            pe.matmul(bank[6][:, 32:40], C("after"), g_log[:, 0, 0:8], start=True, stop=True)
            pe.matmul(bank[6][:, 40:48], C("before"), g_log[:, 1, 8:16], start=True, stop=True).then_inc(g_summed, 1)
            for p in range(8):
                pe.wait_ge(sq_ready, p + 1)
                for h in range(2):
                    c = 2 * p + h
                    for tt in range(TT):
                        col = (c // 8) * 16 + tt * 8 + c % 8
                        mm = pe.matmul(bank[7][:, col:col + 1], sq[:, p % 2, h, tt * P:(tt + 1) * P], ones[:, 0:1],
                                       start=True, stop=True)
                mm.then_inc(qk_summed_pair, 1)
            o = plan.outputs["ca", 2][0]
            for tt in range(TT):
                pe.wait_ge(bank_free["dve", tt], plan.free_count("dve", tt, o))
            for b in range(2):
                turn(pe, "prod", b, [(ca_c[:, tt, (2 * b + h) * P:(2 * b + h + 1) * P], P, P, h * T + tt * P)
                                     for h in range(2) for tt in range(TT)])
            for b in range(2):
                turn(pe, "cab", b, [(ca_b[:, tt, (2 * b + h) * P:(2 * b + h + 1) * P], P, P, h * T + tt * P)
                                    for h in range(2) for tt in range(TT)])
            gemm(pe, "z", 0, from_lhs, "norm3", 512)
            pe.wait_ge(g_cum_ready, 1)
            ada_sum(pe, 24)
            pe.wait_ge(qkv_ready, 12)
            for b in range(4):
                tt, hh = b // 2, 4 * (b % 2)
                turn(pe, "v", b, [(vT[:, hh + h, tt * P:(tt + 1) * P], P, P, h * P) for h in range(4)])
            turn(pe, "grow", 0, [(g_cum[:, tt, :], P, 16, tt * P) for tt in range(TT)])
            gemm(pe, "z", 1, from_lhs, "norm3", 512)
            ada_sum(pe, 25)
            for j in range(4):
                gemm(pe, "gate", j, from_lhs, "norm3", GATE_W)
                ada_sum(pe, 26 + j)
            for j in range(2):
                gemm(pe, "a_out", j, lambda k, tt: [y[:, k, tt * P:(tt + 1) * P] for y in (y_a_hi, y_a_lo)], "y_a", 512,
                     kc_total=CONV_A // P)
            delta_pe(pe)
            turn_tokens(pe, "y_b", lambda tt, c: y_b[:, tt, c, :], range(4))
            for j in range(2):
                gemm(pe, "b_out", j, from_lhs, "y_b", 512)
            for b in range(4):
                pe.wait_ge(merged_ready, 2 if b < 2 else 4)
                turn_tokens(pe, "merged", lambda tt, c: sig[:, tt, 0, c * P:(c + 1) * P], [b])
            for j in range(2):
                gemm(pe, "mix_out", j, from_lhs, "merged", 512)

        LV = N_LEVELS - 1
        FAR = (2, 2)

        class Lane:
            def __init__(self, n, space):
                self.bank = bank[4 * n:4 * n + 4]
                self.shifted = space.take(2, TT, P)
                self.decay = space.take(2, 3, P)
                self.mix = space.take(2, 3, P)
                self.far = space.take(2, P)
                self.coupling = space.take(2 * TT, P)
                self.level = space.take(2, 2 * TT, P)
                self.X = space.take(2 * TT, P)
                self.Y = space.take(2 * TT, P)
                self.LX = space.take(2 * TT, P)
                self.u = space.take(2 * TT, P)
                self.rhs = self.shifted
                self.o = space.take(TT, P)

        lanes = [Lane(0, Space(0, lane_mem[:, :], 2 * SPLIT * UNIT)), Lane(1, Space(mix.at))]
        PAIRS = DN_HEADS // 2
        d_names = ["products", "shifted", "decay", "system", "first", "first_turned", "first_x", "lx", "lx_copied",
                   "stepped", "updated", "z_near", "u_near", "w", "rhs", "z_far", "u_far", "o", "o_scaled", "squared",
                   "mean", "rms", "y", "level"]
        d = {n: sem("delta_" + n) for n in d_names}

        def at_level(h, s):
            return (h // 2) * 2 * LV + 2 * (s - 1) + h % 2 + 1

        def masked_level(h, s):
            return (h // 2) * 2 * (LV + 1) + 2 * s + h % 2 + 1

        def delta_pe(pe):
            for tt in range(TT):
                for e in ("dve", "act"):
                    pe.wait_ge(bank_free[e, tt], plan.free_count(e, tt, plan.outputs["a_out", 1][0]))
            await_turns_read(pe, "grow", [0])
            await_turns_read(pe, "v", range(4))
            pe.wait_ge(mod_ready, 30)
            for pair in range(PAIRS):
                heads = (2 * pair, 2 * pair + 1)
                for h in heads:
                    b = lanes[h % 2].bank
                    if pair:
                        pe.wait_ge(d["o_scaled"], h - 1)
                    for dr in range(2):
                        c = dr * DN_HEADS + h
                        pe.matmul(b[3][:, dr * T:(dr + 1) * T], ident[0:16, c:c + 1].broadcast_to([16, P]),
                                  g_rows[0:16, :], start=True, stop=True)
                    kT, qT = qkT[:, DN_HEADS + h, :], qkT[:, h, :]
                    for i, (jt, it) in enumerate(((0, 0), (1, 1), (0, 1), (1, 0))):
                        pe.matmul(b[0][:, i * P:(i + 1) * P], kT[:, jt * P:(jt + 1) * P], kT[:, it * P:(it + 1) * P],
                                  start=True, stop=True)
                        mm = pe.matmul(b[1][:, i * P:(i + 1) * P], kT[:, jt * P:(jt + 1) * P],
                                       qT[:, it * P:(it + 1) * P], start=True, stop=True)
                    mm.then_inc(d["products"], 1)
                for h in heads:
                    L = lanes[h % 2]
                    pe.wait_ge(d["first"], h + 1)
                    for m in range(4):
                        mm = pe.transpose(L.bank[0][:, m * P:(m + 1) * P], L.Y[:, m, :], ident)
                    mm.then_inc(d["first_turned"], 1)
                for s in range(1, LV + 1):
                    for h in heads:
                        L = lanes[h % 2]
                        pe.wait_ge(d["level"], masked_level(h, s))
                        if s == 1:
                            pe.wait_ge(d["first_x"], h + 1)
                        else:
                            pe.wait_ge(d["updated"], at_level(h, s - 1))
                        for m in range(4):
                            mm = pe.matmul(L.bank[0][:, m * P:(m + 1) * P], L.level[:, s % 2, m, :], L.X[:, m, :],
                                           start=True, stop=True)
                        mm.then_inc(d["lx"], 1)
                    for h in heads:
                        L = lanes[h % 2]
                        pe.wait_ge(d["lx_copied"], at_level(h, s))
                        for m in range(4):
                            if s < LV:
                                pe.matmul(L.bank[1][:, m * P:(m + 1) * P], L.Y[:, m, :], L.LX[:, m, :],
                                          start=True, stop=True)
                            mm = pe.matmul(L.bank[2][:, m * P:(m + 1) * P], L.LX[:, m, :], L.Y[:, m, :],
                                           start=True, stop=True)
                        mm.then_inc(d["stepped"], 1)
                for h in heads:
                    L = lanes[h % 2]
                    pe.wait_ge(d["updated"], at_level(h, LV))
                    pe.matmul(L.bank[3][:, 0:P], L.Y[:, 0, :], v_hat[:, 0, h, :], start=True, stop=True)
                    pe.matmul(L.bank[3][:, P:2 * P], L.Y[:, 3, :], v_hat[:, 1, h, :], start=True,
                              stop=True).then_inc(d["z_near"], 1)
                for h in heads:
                    L = lanes[h % 2]
                    pe.wait_ge(d["u_near"], h + 1)
                    pe.matmul(L.bank[0][:, 0:P], L.far[:, 0, :], L.u[:, 0, :], start=True, stop=True)
                    pe.matmul(L.bank[0][:, P:2 * P], L.far[:, 1, :], L.u[:, 3, :], start=True,
                              stop=True).then_inc(d["w"], 1)
                for h in heads:
                    L = lanes[h % 2]
                    pe.wait_ge(d["rhs"], h + 1)
                    pe.matmul(L.bank[3][:, 0:P], L.Y[:, 1, :], L.rhs[:, 0, 0, :], start=True, stop=True)
                    pe.matmul(L.bank[3][:, P:2 * P], L.Y[:, 2, :], L.rhs[:, 0, 1, :], start=True,
                              stop=True).then_inc(d["z_far"], 1)
                for h in heads:
                    L = lanes[h % 2]
                    pe.wait_ge(d["u_far"], h + 1)
                    for tt, terms in enumerate((((0, 0, 0), (1, 0, 2), (1, 2, 3)), ((0, 1, 1), (0, 2, 0), (1, 1, 3)))):
                        for i, (dr, blk, m) in enumerate(terms):
                            mm = pe.matmul(L.bank[1][:, tt * P:(tt + 1) * P], L.mix[:, dr, blk, :], L.u[:, m, :],
                                           start=(i == 0), stop=(i == 2))
                    mm.then_inc(d["o"], 1)
            pe.wait_ge(d["y"], 2 * DN_HEADS)

        def delta_dve(dve, link):
            link.wait()
            dve.wait_ge(z_gained, 2)
            dve.wait_ge(k_len_ready, 3)
            for pair in range(PAIRS):
                heads = (2 * pair, 2 * pair + 1)
                for h in heads:
                    L = lanes[h % 2]
                    dve.wait_ge(d["products"], h + 1)
                    for dr, name in enumerate(("incl_fwd", "incl_bwd")):
                        mask = C(name).rearrange("p (o i) -> p o i", o=1).broadcast_to([P, TT, P])
                        ins = dve.tensor_tensor(L.shifted[:, dr, :, :],
                                                L.bank[3][:, dr * T:(dr + 1) * T].rearrange("p (t i) -> p t i", t=TT),
                                                mask, ALU.add)
                    ins.then_inc(d["shifted"], 1)
                for h in heads:
                    L = lanes[h % 2]
                    kk, kq = L.bank[0], L.bank[1]
                    dve.wait_ge(d["decay"], h + 1)
                    for dr in range(2):
                        for tt in range(TT):
                            bk = beta_k[:, tt, dr * DN_HEADS + h:dr * DN_HEADS + h + 1]
                            dve.scalar_tensor_tensor(L.coupling[:, 2 * dr + tt, :], kk[:, tt * P:(tt + 1) * P], bk,
                                                     L.decay[:, dr, tt, :], ALU.mult, ALU.mult)
                        ins = dve.tensor_tensor(L.far[:, dr, :], kk[:, (2 + dr) * P:(3 + dr) * P], L.decay[:, dr, 2, :],
                                                ALU.mult)
                    ins.then_inc(d["system"], 1)
                    dve.tensor_tensor(L.mix[:, 0, :, :], kq[:, 0:3 * P].rearrange("p (b i) -> p b i", b=3),
                                      L.decay[:, 0, :, :], ALU.mult)
                    dve.tensor_tensor(L.mix[:, 1, 0:2, :], kq[:, 0:2 * P].rearrange("p (b i) -> p b i", b=2),
                                      L.decay[:, 1, 0:2, :], ALU.mult)
                    dve.tensor_tensor(L.mix[:, 1, 2, :], kq[:, 3 * P:4 * P], L.decay[:, 1, 2, :], ALU.mult)
                for h in heads:
                    L = lanes[h % 2]
                    dve.wait_ge(d["level"], masked_level(h, 0))
                    dve.tensor_tensor(L.Y, ident.rearrange("p (o i) -> p o i", o=1).broadcast_to([P, 4, P]),
                                      L.level[:, 0, :, :], ALU.subtract).then_inc(d["first"], 1)
                for s in range(1, LV + 1):
                    for h in heads:
                        L = lanes[h % 2]
                        dve.wait_ge(d["stepped"], at_level(h, s))
                        if s < LV:
                            dve.tensor_tensor(L.X.rearrange("p m i -> p (m i)"), L.X.rearrange("p m i -> p (m i)"),
                                              L.bank[1][:, :], ALU.subtract)
                        if s == 1:
                            dve.wait_ge(d["first"], h + 1)
                        else:
                            dve.wait_ge(d["updated"], at_level(h, s - 1))
                        dve.tensor_tensor(L.Y.rearrange("p m i -> p (m i)"), L.Y.rearrange("p m i -> p (m i)"),
                                          L.bank[2][:, :], ALU.subtract).then_inc(d["updated"], 1)
                for h in heads:
                    L = lanes[h % 2]
                    dve.wait_ge(d["z_near"], h + 1)
                    dve.tensor_scalar(L.u[:, 0, :], L.bank[3][:, 0:P], beta_k[:, 0, h:h + 1], None, ALU.mult)
                    dve.tensor_scalar(L.u[:, 3, :], L.bank[3][:, P:2 * P], beta_k[:, 1, DN_HEADS + h:DN_HEADS + h + 1],
                                      None, ALU.mult).then_inc(d["u_near"], 1)
                for h in heads:
                    L = lanes[h % 2]
                    dve.wait_ge(d["w"], h + 1)
                    dve.tensor_tensor(L.rhs[:, 0, 0, :], v_hat[:, 1, h, :], L.bank[0][:, 0:P], ALU.subtract)
                    dve.tensor_tensor(L.rhs[:, 0, 1, :], v_hat[:, 0, h, :], L.bank[0][:, P:2 * P],
                                      ALU.subtract).then_inc(d["rhs"], 1)
                for h in heads:
                    L = lanes[h % 2]
                    dve.wait_ge(d["z_far"], h + 1)
                    dve.tensor_scalar(L.u[:, 1, :], L.bank[3][:, 0:P], beta_k[:, 1, h:h + 1], None, ALU.mult)
                    dve.tensor_scalar(L.u[:, 2, :], L.bank[3][:, P:2 * P], beta_k[:, 0, DN_HEADS + h:DN_HEADS + h + 1],
                                      None, ALU.mult).then_inc(d["u_far"], 1)
                for h in heads:
                    L = lanes[h % 2]
                    dve.wait_ge(d["o"], h + 1)
                    if pair:
                        dve.wait_ge(d["y"], 2 * (h - 1))
                    dve.tensor_tensor(L.o, L.bank[1][:, 0:T].rearrange("p (t i) -> p t i", t=TT),
                                      q_scale[:, :, h:h + 1].broadcast_to([P, TT, P]), ALU.mult).then_inc(d["o_scaled"], 1)
                for h in heads:
                    L = lanes[h % 2]
                    dve.wait_ge(d["squared"], h + 1)
                    dve.tensor_scalar(y_ms[:, h, :], y_ss[:, h, :], 1.0 / DN_D, EPS, ALU.mult, ALU.add).then_inc(d["mean"], 1)
                for h in heads:
                    L = lanes[h % 2]
                    dve.wait_ge(d["rms"], h + 1)
                    for tt in range(TT):
                        dve.scalar_tensor_tensor(y_b[:, tt, h, :], L.o[:, tt, :], y_r[:, h, tt:tt + 1],
                                                 z_gain[:, tt, h * P:(h + 1) * P], ALU.mult, ALU.mult).then_inc(d["y"], 1)

        def delta_act(act):
            for pair in range(PAIRS):
                heads = (2 * pair, 2 * pair + 1)
                for h in heads:
                    L = lanes[h % 2]
                    act.wait_ge(d["shifted"], h + 1)
                    for dr in range(2):
                        c = dr * DN_HEADS + h
                        for tt in range(TT):
                            act.activation(L.decay[:, dr, tt, :], L.shifted[:, dr, tt, :], ACT.Exp,
                                           bias=g_in[:, tt, c:c + 1])
                        it = 1 - dr
                        ins = act.activation(L.decay[:, dr, 2, :], L.bank[3][:, dr * T + it * P:dr * T + (it + 1) * P],
                                             ACT.Exp, bias=g_off[:, c:c + 1])
                    ins.then_inc(d["decay"], 1)
                for h in heads:
                    L = lanes[h % 2]
                    act.wait_ge(d["first_turned"], h + 1)
                    act.copy(L.X.rearrange("p m i -> p (m i)"), L.bank[0][:, :]).then_inc(d["first_x"], 1)
                for s in range(1, LV + 1):
                    for h in heads:
                        L = lanes[h % 2]
                        act.wait_ge(d["lx"], at_level(h, s))
                        act.copy(L.LX.rearrange("p m i -> p (m i)"), L.bank[0][:, :]).then_inc(d["lx_copied"], 1)
                for h in heads:
                    L = lanes[h % 2]
                    act.wait_ge(d["o_scaled"], h + 1)
                    for tt in range(TT):
                        ins = act.activation(L.rhs[:, 1, tt, :], L.o[:, tt, :], ACT.Square, accum_out=y_ss[:, h, tt:tt + 1])
                    ins.then_inc(d["squared"], 1)

        def delta_pool(pool):
            for pair in range(PAIRS):
                heads = (2 * pair, 2 * pair + 1)
                for s in range(LV + 1):
                    for h in heads:
                        L = lanes[h % 2]
                        if s == 0:
                            pool.wait_ge(d["system"], h + 1)
                        if s == 2:
                            pool.wait_ge(d["first"], h + 1)
                        if s > 2:
                            pool.wait_ge(d["lx"], at_level(h, s - 2))
                        elif pair:
                            pool.wait_ge(d["lx"], at_level(h - 2, LV))
                        pool.tensor_tensor(L.level[:, s % 2, :, :], L.coupling,
                                           C(f"level_{s}").rearrange("p (o i) -> p o i", o=1).broadcast_to([P, 4, P]),
                                           ALU.mult).then_inc(d["level"], 1)
                for h in heads:
                    pool.wait_ge(d["mean"], h + 1)
                    pool.tensor_tensor(y_r[:, h, :], y_ms[:, h, :], C("minus_half").broadcast_to([P, TT]),
                                       ALU.pow).then_inc(d["rms"], 1)

        def second_dve(dve, link):
            norm_dve(dve, 2, link)
            norm_left_dve(dve, 2)
            ffn_dve(dve, "ffn1", 2, range(18, 24))
            norm_dve(dve, 3, link)
            norm_left_dve(dve, 3)
            mix_dve(dve, link)
            norm_dve(dve, 4, link)
            norm_left_dve(dve, 4)
            ffn_dve(dve, "ffn2", 4)

        def second_act(act):
            norm_act(act, 2)
            norm_left_act(act, 2)
            ffn_act(act, "ffn1")
            norm_act(act, 3)
            norm_left_act(act, 3)
            for i, name in enumerate(("a_log_fwd_2", "a_log_bwd_2", "dt_bias_fwd_2", "dt_bias_bwd_2")):
                act.dma_start(head_row[:, 8 * i:8 * i + 8], A[name][0].partition_broadcast(P)).then_inc(rows_in, 16)
            act.dma_start(dn_gain, A["dn_norm_2"][0].partition_broadcast(P)).then_inc(rows_in, 16)
            mix_act(act)
            norm_act(act, 4)
            norm_left_act(act, 4)
            act.wait_ge(x_ready, 16)
            act.dma_start(last_gain, A["norm_final_2"].partition_broadcast(P)).then_inc(gain_in, 16)
            ffn_act(act, "ffn2")
            stream_ahead("act", "ffn2_down", 1)

        def second_pool(pool):
            norm_pool(pool, 2)
            stream_ahead("pool", "ffn1_up", FFN_OUTS - 1, 0)
            residual_pool(pool, 2)
            norm_pool(pool, 3)
            stream_ahead("pool", "ca", 2, 0)
            mix_pool(pool)
            norm_pool(pool, 4)
            stream_ahead("pool", "ffn2_up", FFN_OUTS - 1, 0)
            residual_pool(pool, 4)

        def second_pe(pe):
            norm_pe(pe, 2)
            ffn_pe(pe, "ffn1", "norm2", range(18, 24))
            norm_pe(pe, 3)
            mix_pe(pe)
            norm_pe(pe, 4)
            ffn_pe(pe, "ffn2", "norm4")
        first_gain = dil_z[:, 0, :]
        last_gain = gate_row[:, 1, :]

        def final_dve(dve, i, layer, gain, gains, dst, link):
            dve.wait_ge(x_ready, 4 * layer)
            mean_dve(dve, i, link)
            dve.wait_ge(gain_in, 16 * gains)
            for tt in range(TT):
                dve.scalar_tensor_tensor(dst[:, tt, :], x[:, tt, :], stat[:, i, 2, tt:tt + 1], gain,
                                         ALU.mult, ALU.mult).then_inc(x_scaled, 1)

        def final_act(act, i, layer):
            act.wait_ge(x_ready, 4 * layer)
            squares_act(act, i)

        block = ctx.enter_context(nc.Block())

        @block.sync
        def _(sp):

            for u, (dmas, consumer, _) in enumerate(plan.units):
                if u >= RING:
                    _, who, ordinal = plan.units[u - RING]
                    if who == "split":
                        engine, ordinal = plan.rest_of[u - RING]
                        sp.wait_ge(lo_ready[engine], ordinal + 1)
                    else:
                        sp.wait_ge({"pe": pe_units, "ada": ada_units}[who], ordinal + 1)
                for src, kn, width, at, cn in dmas:
                    dst = ring[:, u % RING, 0:kn * width].rearrange("p (k n) -> p k n", k=kn)[:, :, at:at + cn]
                    sp.dma_start(dst, src).then_inc(landed[u % RING], 16)
            for tt in range(TT):
                sp.wait_ge(x_scaled, TT * (last_block - 1) + tt + 1)
                sp.dma_start(out[0, tt * P:(tt + 1) * P, :], xn[:, tt, :]).then_inc(stored, 16)
            sp.wait_ge(stored, 16 * TT)

        @block.scalar
        def _(act):
            at = 0
            for ap, n in param_rows(A):
                act.dma_start(rows[at:at + n, 0, :], ap).then_inc(params_in, 16)
                at += n
            act.dma_start(rows[0:120, 1, :], A["conv_dn_2"][0].rearrange("k (r c) -> (k r) c", c=P)).then_inc(params_in, 16)
            act.dma_start(rows[0:24, 2, :], A["ada_b"][0].rearrange("(r c) -> r c", c=P)).then_inc(params_in, 16)
            act.dma_start(rows[24:48, 2, :], A["ada_b"][1].rearrange("(r c) -> r c", c=P)).then_inc(params_in, 16)
            act.dma_start(rows[48:120, 2, :], A["b_ada_2"][0].rearrange("(r c) -> r c", c=P)).then_inc(params_in, 16)
            act.dma_start(const[:, 0:2 * P], const_ap[:, 0:2 * P]).then_inc(params_in, 16)
            act.dma_start(x[:, :, :], A["x"][0].rearrange("(t p) d -> p t d", p=P)).then_inc(x_in, 16)
            act.dma_start(const[:, 2 * P:], const_ap[:, 2 * P:]).then_inc(const_in, 16)
            for twice in range(2):
                act.dma_start(w2k[:, :, twice, :], A["nsa_ck_w2"][0].rearrange("(c p) d -> p c d", p=P)).then_inc(w2_in, 16)
            act.dma_start(w2v, A["nsa_cv_w2"][0].rearrange("(c p) d -> p c d", p=P)).then_inc(w2_in, 16)
            act.wait_ge(cols_ready, 1)
            act.activation(c_act[:, :], cols[:, 0, 0:2 * KC], ACT.Silu).then_inc(c_ready, 1)
            norm_act(act, 0)
            norm_left_act(act, 0)
            nsa_act(act)
            norm_act(act, 1)
            norm_left_act(act, 1)
            dil_act(act)
            act.wait_ge(o_ready, 4)
            act.dma_start(first_gain, A["final_g"].partition_broadcast(P)).then_inc(gain_in, 16)
            stream_ahead("act", "dil_out", 1)
            final_act(act, 2, 2)
            if last_block == 2:
                second_act(act)
                final_act(act, 6, 5)

        @block.gpsimd
        def _(pool):
            pool.wait_ge(const_in, 16)
            norm_pool(pool, 0)
            nsa_pool(pool)
            norm_pool(pool, 1)
            dil_pool(pool)
            rstd_pool(pool, 2)
            if last_block == 2:
                second_pool(pool)
                rstd_pool(pool, 6)

        @block.vector
        def _(dve):
            link = chain["dve"] = Chain(dve, dve_chain)
            dve.wait_ge(cols_done, 1)
            dve.tensor_copy(cols[:, 0, 0:100], bank[7][:, 0:100])
            dve.tensor_copy(cols[:, 1, 0:120], bank[7][:, P:P + 120])
            dve.tensor_copy(cols[:, 2, 0:120], bank[7][:, 2 * P:2 * P + 120]).then_inc(cols_ready, 1)
            dve.wait_ge(cols_ready, 1)
            dve.wait_ge(c_ready, 1)
            stream_to("dve", plan.outputs["ada", 0][1][-1])
            norm_dve(dve, 0, link)
            stream_to("dve", plan.outputs["ada", 3][1][-1])
            ada_collect_up_to(4)
            norm_left_dve(dve, 0)
            nsa_dve(dve, link)
            residual_dve(dve, 0, "nsa_out")
            norm_dve(dve, 1, link)
            norm_left_dve(dve, 1)
            dil_dve(dve, link)
            residual_dve(dve, 1, "dil_out")
            final_dve(dve, 2, 2, first_gain, 1, xn if last_block == 1 else x, link)
            if last_block == 2:
                second_dve(dve, link)
                final_dve(dve, 6, 5, last_gain, 2, xn, link)

        @block.tensor
        def _(pe):
            pe.wait_ge(params_in, 16 * (len(param_rows(A)) + 5))
            pe.transpose(bank[7][:, 0:100], rows[0:100, 0, :], ident[0:100, 0:100])
            pe.transpose(bank[7][:, P:P + 120], rows[0:120, 1, :], ident[0:120, 0:120])
            pe.transpose(bank[7][:, 2 * P:2 * P + 120], rows[0:120, 2, :], ident[0:120, 0:120]).then_inc(cols_done, 1)
            pe.wait_ge(cols_ready, 1)
            for n in range(4):
                ada_sum(pe, n)
            norm_pe(pe, 0)
            nsa_pe(pe)
            norm_pe(pe, 1)
            dil_pe(pe)
            if last_block == 2:
                second_pe(pe)


def param_rows(A):
    def r(ap):
        return ap.rearrange("(r c) -> r c", c=P)
    return [(r(A["c"][0]), 8), (r(A["c_2"][0]), 8), (r(A["norm_g"][0]), 8), (r(A["norm_g"][1]), 8),
            (r(A["norm_ffn1_2"][0]), 8), (r(A["norm_mix_2"][0]), 8), (r(A["norm_ffn2_2"][0]), 8),
            (A["nsa_pe_k"][0].rearrange("(r a) d -> r (a d)", a=2), 16),
            (A["nsa_pe_v"][0].rearrange("(r a) d -> r (a d)", a=2), 16),
            (A["conv_a_2"][0].rearrange("k (r c) -> (k r) c", c=P), 12)]


def turn_order(last_block):
    t = turns("norm0", 4, "dve") + turns("kc", 1, "dve") + turns("vc", 1, "act") + turns("ks", 1, "dve")
    t += turns("kw", 1, "act") + turns("hid", 1, "dve") + turns("qp", 4) + turns("qr", 4) + turns("pc", 1, "act")
    t += turns("nsa_o", 4, "dve") + turns("norm1", 4, "dve") + turns("dil_q", 4) + turns("dil_k", 4)
    t += turns("dil_o", 4, "dve")
    return t + second_turns() if last_block == 2 else t


_INS = ["x", "c", "norm_g", "ada_w", "ada_b", "nsa_w_in", "nsa_pe_k", "nsa_pe_v", "nsa_ck_w1", "nsa_ck_w2",
        "nsa_cv_w1", "nsa_cv_w2", "nsa_w_out", "dil_w_in", "dil_w_out", "final_g", "c_2", "w_ada_2", "b_ada_2",
        "norm_ffn1_2", "w_ffn1_up_2", "w_ffn1_down_2", "norm_mix_2", "w_in_2", "conv_a_2", "conv_dn_2",
        "a_log_fwd_2", "dt_bias_fwd_2", "a_log_bwd_2", "dt_bias_bwd_2", "dn_norm_2", "w_a_out_2", "w_b_out_2",
        "w_out_2", "norm_ffn2_2", "w_ffn2_up_2", "w_ffn2_down_2", "norm_final_2"]


def kernel(**inputs):
    import numpy as _np
    import concourse.bacc as _bacc
    from concourse import mybir as _mybir
    from concourse.bass_utils import run_bass_kernel_spmd as _run

    nc = _bacc.Bacc("TRN2", target_bir_lowering=False, num_devices=1)
    arrays, aps = {}, {}
    for name in _INS:
        a = _np.ascontiguousarray(inputs[name])
        arrays[f"in_{name}"] = a
        aps[name] = nc.dram_tensor(f"in_{name}", a.shape, _mybir.dt.float32, kind="ExternalInput").ap()
    arrays["const_table"] = CONST_TABLE
    const_ap = nc.dram_tensor("const_table", CONST_TABLE.shape, _mybir.dt.float32, kind="ExternalInput").ap()
    out = nc.dram_tensor("out", (1, T, D), _mybir.dt.float32, kind="ExternalOutput").ap()
    build(nc, aps, const_ap, out, LAST_BLOCK)
    r = _run(nc, [arrays], core_ids=[0])
    return r.results[0]["out"]
```
